# Optimizing a Trainium2 kernel written in Bass

```python
import jax, jax.numpy as jnp
from jax import lax
import numpy as np
import math

D_MODEL = 1024
BATCH = 1
SEQ = 256
DEPTH = 2

N_MIXERS = 2
N_CONV_LAYERS = (DEPTH + 1) // 2
N_MLA_LAYERS = DEPTH // 2
N_DENSE_LAYERS = (DEPTH + 1) // 2
N_MOE_LAYERS = DEPTH // 2
CONV_WIDTH = 3
N_HEADS = 8
QK_NOPE_DIM = 128
QK_ROPE_DIM = 64
QK_HEAD_DIM = QK_NOPE_DIM + QK_ROPE_DIM
V_HEAD_DIM = 128
Q_LORA_RANK = 384
KV_LORA_RANK = 256
ROPE_THETA = 10000.0
Q_BLOCK = 128
D_FF_DENSE = 2816
N_EXPERTS = 8
TOP_K = 2
D_FF_EXPERT = 2048
EPS = 1e-6


def rmsnorm(x, g):
    xf = x.astype(jnp.float32)
    y = xf * lax.rsqrt(jnp.mean(xf * xf, axis=-1, keepdims=True) + EPS)
    return (y * g.astype(jnp.float32)).astype(x.dtype)

def rope_tables(positions):
    inv_freq = ROPE_THETA ** (-jnp.arange(0, QK_ROPE_DIM, 2, dtype=jnp.float32) / QK_ROPE_DIM)
    ang = positions.astype(jnp.float32)[..., None] * inv_freq
    return jnp.cos(ang)[:, :, None, :], jnp.sin(ang)[:, :, None, :]

def apply_rope(x, cos, sin):
    x1, x2 = jnp.split(x, 2, axis=-1)
    cos = cos.astype(x.dtype)
    sin = sin.astype(x.dtype)
    return jnp.concatenate([x1 * cos - x2 * sin, x2 * cos + x1 * sin], axis=-1)

def short_conv_mixer(h, w_in, w_conv, w_out):
    seq = h.shape[1]
    b_gate, c_gate, u = jnp.split(h @ w_in, 3, axis=-1)
    v = c_gate * u
    vp = jnp.pad(v, ((0, 0), (CONV_WIDTH - 1, 0), (0, 0)))
    conv = vp[:, 0:seq] * w_conv[0]
    for k in range(1, CONV_WIDTH):
        conv = conv + vp[:, k:k + seq] * w_conv[k]
    return (b_gate * conv) @ w_out

def mla_mixer(h, cos, sin, w_down, q_a_norm, kv_a_norm, w_uq, w_ukv, q_norm, k_norm, w_o):
    bsz, seq, _ = h.shape
    down = h @ w_down
    c_q = rmsnorm(down[..., :Q_LORA_RANK], q_a_norm)
    c_kv = rmsnorm(down[..., Q_LORA_RANK:Q_LORA_RANK + KV_LORA_RANK], kv_a_norm)
    k_rope = down[..., Q_LORA_RANK + KV_LORA_RANK:]
    q = (c_q @ w_uq).reshape(bsz, seq, N_HEADS, QK_HEAD_DIM)
    kv = (c_kv @ w_ukv).reshape(bsz, seq, N_HEADS, QK_NOPE_DIM + V_HEAD_DIM)
    k_nope, v = kv[..., :QK_NOPE_DIM], kv[..., QK_NOPE_DIM:]
    k_rope_h = jnp.broadcast_to(k_rope[:, :, None, :], (bsz, seq, N_HEADS, QK_ROPE_DIM))
    k = jnp.concatenate([k_nope, k_rope_h], axis=-1)
    q = rmsnorm(q, q_norm)
    k = rmsnorm(k, k_norm)
    q = jnp.concatenate([q[..., :QK_NOPE_DIM], apply_rope(q[..., QK_NOPE_DIM:], cos, sin)], axis=-1)
    k = jnp.concatenate([k[..., :QK_NOPE_DIM], apply_rope(k[..., QK_NOPE_DIM:], cos, sin)], axis=-1)
    scale = QK_HEAD_DIM ** -0.5
    neg = jnp.finfo(jnp.float32).min
    outs = []
    for blk in range(seq // Q_BLOCK):
        s0 = blk * Q_BLOCK
        end = s0 + Q_BLOCK
        scores = jnp.einsum('bqhd,bkhd->bhqk', q[:, s0:end], k[:, :end]).astype(jnp.float32) * scale
        mask = jnp.arange(end)[None, :] <= (s0 + jnp.arange(Q_BLOCK))[:, None]
        p = jax.nn.softmax(jnp.where(mask, scores, neg), axis=-1).astype(v.dtype)
        outs.append(jnp.einsum('bhqk,bkhd->bqhd', p, v[:, :end]))
    o = jnp.concatenate(outs, axis=1).reshape(bsz, seq, N_HEADS * V_HEAD_DIM)
    return o @ w_o

def swiglu(h, w_gate, w_up, w_down):
    return (jax.nn.silu(h @ w_gate) * (h @ w_up)) @ w_down

def moe_swiglu(h, router, w_gate, w_up, w_down):
    bsz, seq, d = h.shape
    ht = h.reshape(bsz * seq, d)
    probs = jax.nn.softmax((ht @ router).astype(jnp.float32), axis=-1)
    vals, idx = lax.top_k(probs, TOP_K)
    wts = vals / jnp.sum(vals, axis=-1, keepdims=True)
    gates = jnp.einsum('tk,tke->te', wts, jax.nn.one_hot(idx, N_EXPERTS, dtype=jnp.float32)).astype(h.dtype)
    out = jnp.zeros_like(ht)
    for e in range(N_EXPERTS):
        out = out + gates[:, e:e + 1] * swiglu(ht, w_gate[e], w_up[e], w_down[e])
    return out.reshape(bsz, seq, d)

def first_inputs(seed: int = 0) -> dict:
    key = jax.random.key(seed)
    ks = jax.random.split(key, 24)
    f32 = jnp.float32
    res_scale = (2 * DEPTH) ** -0.5

    def w(k, shape, fan_in, extra=1.0):
        return jax.random.normal(k, shape, f32) * (fan_in ** -0.5) * extra

    def gain(k, shape):
        return 1.0 + 0.02 * jax.random.normal(k, shape, f32)

    x = jax.random.normal(ks[0], (BATCH, SEQ, D_MODEL), f32)
    start = jax.random.randint(ks[1], (BATCH, 1), 0, 4096, dtype=jnp.int32)
    positions = (start + jnp.arange(SEQ, dtype=jnp.int32)[None, :]).astype(jnp.int32)
    return {
        "x": x,
        "positions": positions,
        "norm_mix": gain(ks[2], (DEPTH, D_MODEL)),
        "norm_ffn": gain(ks[3], (DEPTH, D_MODEL)),
        "conv_w_in": w(ks[4], (N_CONV_LAYERS, D_MODEL, 3 * D_MODEL), D_MODEL),
        "conv_w": w(ks[5], (N_CONV_LAYERS, CONV_WIDTH, D_MODEL), CONV_WIDTH),
        "conv_w_out": w(ks[6], (N_CONV_LAYERS, D_MODEL, D_MODEL), D_MODEL, res_scale),
        "mla_w_down": w(ks[7], (N_MLA_LAYERS, D_MODEL, Q_LORA_RANK + KV_LORA_RANK + QK_ROPE_DIM), D_MODEL),
        "mla_q_a_norm": gain(ks[8], (N_MLA_LAYERS, Q_LORA_RANK)),
        "mla_kv_a_norm": gain(ks[9], (N_MLA_LAYERS, KV_LORA_RANK)),
        "mla_w_uq": w(ks[10], (N_MLA_LAYERS, Q_LORA_RANK, N_HEADS * QK_HEAD_DIM), Q_LORA_RANK),
        "mla_w_ukv": w(ks[11], (N_MLA_LAYERS, KV_LORA_RANK, N_HEADS * (QK_NOPE_DIM + V_HEAD_DIM)), KV_LORA_RANK),
        "mla_q_norm": gain(ks[12], (N_MLA_LAYERS, QK_HEAD_DIM)),
        "mla_k_norm": gain(ks[13], (N_MLA_LAYERS, QK_HEAD_DIM)),
        "mla_w_o": w(ks[14], (N_MLA_LAYERS, N_HEADS * V_HEAD_DIM, D_MODEL), N_HEADS * V_HEAD_DIM, res_scale),
        "ffn_w_gate": w(ks[15], (N_DENSE_LAYERS, D_MODEL, D_FF_DENSE), D_MODEL),
        "ffn_w_up": w(ks[16], (N_DENSE_LAYERS, D_MODEL, D_FF_DENSE), D_MODEL),
        "ffn_w_down": w(ks[17], (N_DENSE_LAYERS, D_FF_DENSE, D_MODEL), D_FF_DENSE, res_scale),
        "moe_router": w(ks[18], (N_MOE_LAYERS, D_MODEL, N_EXPERTS), D_MODEL),
        "moe_w_gate": w(ks[19], (N_MOE_LAYERS, N_EXPERTS, D_MODEL, D_FF_EXPERT), D_MODEL),
        "moe_w_up": w(ks[20], (N_MOE_LAYERS, N_EXPERTS, D_MODEL, D_FF_EXPERT), D_MODEL),
        "moe_w_down": w(ks[21], (N_MOE_LAYERS, N_EXPERTS, D_FF_EXPERT, D_MODEL), D_FF_EXPERT, res_scale),
    }

def first_block(x, positions, norm_mix, norm_ffn, conv_w_in, conv_w, conv_w_out,
              mla_w_down, mla_q_a_norm, mla_kv_a_norm, mla_w_uq, mla_w_ukv,
              mla_q_norm, mla_k_norm, mla_w_o, ffn_w_gate, ffn_w_up, ffn_w_down,
              moe_router, moe_w_gate, moe_w_up, moe_w_down):
    cos, sin = rope_tables(positions)
    for i in range(DEPTH):
        j = i // 2
        h = rmsnorm(x, norm_mix[i])
        if i % N_MIXERS == 0:
            x = x + short_conv_mixer(h, conv_w_in[j], conv_w[j], conv_w_out[j])
        else:
            x = x + mla_mixer(h, cos, sin, mla_w_down[j], mla_q_a_norm[j], mla_kv_a_norm[j],
                              mla_w_uq[j], mla_w_ukv[j], mla_q_norm[j], mla_k_norm[j], mla_w_o[j])
        h = rmsnorm(x, norm_ffn[i])
        if i % 2 == 0:
            x = x + swiglu(h, ffn_w_gate[j], ffn_w_up[j], ffn_w_down[j])
        else:
            x = x + moe_swiglu(h, moe_router[j], moe_w_gate[j], moe_w_up[j], moe_w_down[j])
    return x


DEPTH_2 = 1

HEAD_DIM = 64
A_Q_HEADS = 8
A_KV_HEADS = 2
A_GROUP = A_Q_HEADS // A_KV_HEADS
B_HEADS = 4
B_V_DIM = 2 * HEAD_DIM
A_Q = A_Q_HEADS * HEAD_DIM
A_KV = A_KV_HEADS * HEAD_DIM
B_QK = B_HEADS * 2 * HEAD_DIM
B_V = B_HEADS * B_V_DIM
MIX_WIDTH = A_Q + B_V
IN_WIDTH = A_Q + 2 * A_KV + 2 * B_QK + B_V
D_FF = 4 * D_MODEL
GRID_W = 64
REL_BUCKETS = 32
REL_MAX_DIST = 128


def rmsnorm_2(x, g):
    xf = x.astype(jnp.float32)
    y = xf * lax.rsqrt(jnp.mean(xf * xf, axis=-1, keepdims=True) + EPS)
    return (y * g.astype(jnp.float32)).astype(x.dtype)

def axial_rope_tables(seq_len, dtype):
    rows = seq_len // GRID_W
    row = jnp.broadcast_to(jnp.arange(rows)[:, None], (rows, GRID_W)).reshape(-1).astype(jnp.float32)
    col = jnp.broadcast_to(jnp.arange(GRID_W)[None, :], (rows, GRID_W)).reshape(-1).astype(jnp.float32)
    half = HEAD_DIM // 2
    inv_freq = 1.0 / (ROPE_THETA ** (jnp.arange(0, half, 2, dtype=jnp.float32) / half))
    ang_r = row[:, None] * inv_freq[None, :]
    ang_c = col[:, None] * inv_freq[None, :]
    return tuple(t.astype(dtype) for t in (jnp.cos(ang_r), jnp.sin(ang_r), jnp.cos(ang_c), jnp.sin(ang_c)))

def rope_rotate(x, cos, sin):
    x1, x2 = jnp.split(x, 2, axis=-1)
    c = cos[None, :, None, :]
    s = sin[None, :, None, :]
    return jnp.concatenate([x1 * c - x2 * s, x2 * c + x1 * s], axis=-1)

def apply_axial_rope(x, tables):
    cr, sr, cc, sc = tables
    xr, xc = jnp.split(x, 2, axis=-1)
    return jnp.concatenate([rope_rotate(xr, cr, sr), rope_rotate(xc, cc, sc)], axis=-1)

def t5_bucket(rel):
    nb = REL_BUCKETS // 2
    max_exact = nb // 2
    ret = (rel > 0).astype(jnp.int32) * nb
    n = jnp.abs(rel)
    nf = jnp.maximum(n, 1).astype(jnp.float32)
    large = max_exact + (jnp.log(nf / max_exact) / math.log(REL_MAX_DIST / max_exact) * (nb - max_exact)).astype(jnp.int32)
    large = jnp.minimum(large, nb - 1)
    return ret + jnp.where(n < max_exact, n, large)

def gqa_axial_attention(q, k, v):
    B, S = q.shape[0], q.shape[1]
    nblk = S // Q_BLOCK
    scale = HEAD_DIM ** -0.5
    qb = q.reshape(B, nblk, Q_BLOCK, A_KV_HEADS, A_GROUP, HEAD_DIM).transpose(1, 0, 3, 4, 2, 5)
    kt = k.transpose(0, 2, 1, 3)
    vt = v.transpose(0, 2, 1, 3)

    def block(qblk):
        s = jnp.einsum('bkgqd,bksd->bkgqs', qblk, kt).astype(jnp.float32) * scale
        p = jax.nn.softmax(s, axis=-1)
        return jnp.einsum('bkgqs,bksd->bkgqd', p.astype(vt.dtype), vt)

    o = lax.map(block, qb)
    return o.transpose(1, 0, 4, 2, 3, 5).reshape(B, S, A_Q)

def differential_attention(q, k, v, lam, rel_bias):
    B, S = q.shape[0], q.shape[1]
    nblk = S // Q_BLOCK
    scale = HEAD_DIM ** -0.5
    qb = q.reshape(B, nblk, Q_BLOCK, B_HEADS, 2, HEAD_DIM).transpose(1, 0, 3, 4, 2, 5)
    kt = k.transpose(0, 2, 3, 1, 4)
    vt = v.transpose(0, 2, 1, 3)
    starts = jnp.arange(nblk, dtype=jnp.int32) * Q_BLOCK
    k_pos = jnp.arange(S, dtype=jnp.int32)
    lam32 = lam.astype(jnp.float32)

    def block(args):
        qblk, start = args
        q_pos = start + jnp.arange(Q_BLOCK, dtype=jnp.int32)
        bucket = t5_bucket(k_pos[None, :] - q_pos[:, None])
        bias = rel_bias[bucket].astype(jnp.float32).transpose(2, 0, 1)
        s = jnp.einsum('bhcqd,bhcsd->bhcqs', qblk, kt).astype(jnp.float32) * scale + bias[None, :, None]
        p = jax.nn.softmax(s, axis=-1)
        attn = p[:, :, 0] - lam32 * p[:, :, 1]
        return jnp.einsum('bhqs,bhse->bhqe', attn.astype(vt.dtype), vt)

    o = lax.map(block, (qb, starts))
    return o.transpose(1, 0, 3, 2, 4).reshape(B, S, B_HEADS, B_V_DIM)

def second_inputs(seed: int = 0) -> dict:
    key = jax.random.key(seed)
    ks = jax.random.split(key, 20)
    f32 = jnp.float32
    nrm = lambda k, shape, s: jax.random.normal(k, shape, f32) * s
    return {
        "x": nrm(ks[0], (BATCH, SEQ, D_MODEL), 1.0),
        "attn_norm_g": 1.0 + nrm(ks[1], (DEPTH_2, D_MODEL), 0.05),
        "w_in": nrm(ks[2], (DEPTH_2, D_MODEL, IN_WIDTH), D_MODEL ** -0.5),
        "a_q_norm_g": 1.0 + nrm(ks[3], (DEPTH_2, HEAD_DIM), 0.05),
        "a_k_norm_g": 1.0 + nrm(ks[4], (DEPTH_2, HEAD_DIM), 0.05),
        "b_q_norm_g": 1.0 + nrm(ks[5], (DEPTH_2, HEAD_DIM), 0.05),
        "b_k_norm_g": 1.0 + nrm(ks[6], (DEPTH_2, HEAD_DIM), 0.05),
        "lambda_q1": nrm(ks[7], (DEPTH_2, HEAD_DIM), 0.1),
        "lambda_k1": nrm(ks[8], (DEPTH_2, HEAD_DIM), 0.1),
        "lambda_q2": nrm(ks[9], (DEPTH_2, HEAD_DIM), 0.1),
        "lambda_k2": nrm(ks[10], (DEPTH_2, HEAD_DIM), 0.1),
        "b_subln_g": 1.0 + nrm(ks[11], (DEPTH_2, B_V_DIM), 0.05),
        "rel_bias": nrm(ks[12], (REL_BUCKETS, B_HEADS), 0.5),
        "w_out": nrm(ks[13], (DEPTH_2, MIX_WIDTH, D_MODEL), MIX_WIDTH ** -0.5),
        "mlp_norm_g": 1.0 + nrm(ks[14], (DEPTH_2, D_MODEL), 0.05),
        "w_up": nrm(ks[15], (DEPTH_2, D_MODEL, D_FF), D_MODEL ** -0.5),
        "w_down": nrm(ks[16], (DEPTH_2, D_FF, D_MODEL), D_FF ** -0.5),
    }

def second_block(x, attn_norm_g, w_in, a_q_norm_g, a_k_norm_g, b_q_norm_g, b_k_norm_g,
              lambda_q1, lambda_k1, lambda_q2, lambda_k2, b_subln_g, rel_bias,
              w_out, mlp_norm_g, w_up, w_down):
    B, S, _ = x.shape
    rope_tables = axial_rope_tables(S, x.dtype)
    split_pts = np.cumsum([A_Q, A_KV, A_KV, B_QK, B_QK])[:].tolist()
    for l in range(DEPTH_2):
        h = rmsnorm_2(x, attn_norm_g[l])
        proj = jnp.einsum('bsd,de->bse', h, w_in[l])
        qa, ka, va, qb, kb, vb = jnp.split(proj, split_pts, axis=-1)

        qa = rmsnorm_2(qa.reshape(B, S, A_Q_HEADS, HEAD_DIM), a_q_norm_g[l])
        ka = rmsnorm_2(ka.reshape(B, S, A_KV_HEADS, HEAD_DIM), a_k_norm_g[l])
        qa = apply_axial_rope(qa, rope_tables).reshape(B, S, A_KV_HEADS, A_GROUP, HEAD_DIM)
        ka = apply_axial_rope(ka, rope_tables)
        va = va.reshape(B, S, A_KV_HEADS, HEAD_DIM)
        out_a = gqa_axial_attention(qa, ka, va)

        lambda_init = 0.8 - 0.6 * math.exp(-0.3 * l)
        lam = (jnp.exp(jnp.sum(lambda_q1[l].astype(jnp.float32) * lambda_k1[l].astype(jnp.float32)))
               - jnp.exp(jnp.sum(lambda_q2[l].astype(jnp.float32) * lambda_k2[l].astype(jnp.float32)))
               + lambda_init)
        qb = rmsnorm_2(qb.reshape(B, S, B_HEADS, 2, HEAD_DIM), b_q_norm_g[l])
        kb = rmsnorm_2(kb.reshape(B, S, B_HEADS, 2, HEAD_DIM), b_k_norm_g[l])
        vb = vb.reshape(B, S, B_HEADS, B_V_DIM)
        ob = differential_attention(qb, kb, vb, lam, rel_bias)
        out_b = (rmsnorm_2(ob, b_subln_g[l]) * (1.0 - lambda_init)).reshape(B, S, B_V)

        mixed = jnp.concatenate([out_a, out_b], axis=-1)
        x = x + jnp.einsum('bse,ed->bsd', mixed, w_out[l])

        h = rmsnorm_2(x, mlp_norm_g[l])
        u = jnp.einsum('bsd,df->bsf', h, w_up[l])
        u = jnp.square(jax.nn.relu(u))
        x = x + jnp.einsum('bsf,fd->bsd', u, w_down[l])
    return x


def setup_inputs(seed=0):
    out = dict(first_inputs(seed))
    for name, value in second_inputs(seed + 1).items():
        if name != "x":
            out[name + "_2"] = value
    return out


def reference(
    x, positions, norm_mix, norm_ffn, conv_w_in, conv_w, conv_w_out, mla_w_down, mla_q_a_norm,
    mla_kv_a_norm, mla_w_uq, mla_w_ukv, mla_q_norm, mla_k_norm, mla_w_o, ffn_w_gate, ffn_w_up,
    ffn_w_down, moe_router, moe_w_gate, moe_w_up, moe_w_down, attn_norm_g_2, w_in_2,
    a_q_norm_g_2, a_k_norm_g_2, b_q_norm_g_2, b_k_norm_g_2, lambda_q1_2, lambda_k1_2,
    lambda_q2_2, lambda_k2_2, b_subln_g_2, rel_bias_2, w_out_2, mlp_norm_g_2, w_up_2, w_down_2,
):
    x = first_block(
        x, positions, norm_mix, norm_ffn, conv_w_in, conv_w, conv_w_out, mla_w_down,
        mla_q_a_norm, mla_kv_a_norm, mla_w_uq, mla_w_ukv, mla_q_norm, mla_k_norm, mla_w_o,
        ffn_w_gate, ffn_w_up, ffn_w_down, moe_router, moe_w_gate, moe_w_up, moe_w_down,
    )
    return second_block(
        x, attn_norm_g_2, w_in_2, a_q_norm_g_2, a_k_norm_g_2, b_q_norm_g_2, b_k_norm_g_2,
        lambda_q1_2, lambda_k1_2, lambda_q2_2, lambda_k2_2, b_subln_g_2, rel_bias_2, w_out_2,
        mlp_norm_g_2, w_up_2, w_down_2,
    )


_drawn_inputs = setup_inputs


def setup_inputs(seed=0):
    import zlib

    import numpy as np

    out = dict(_drawn_inputs(seed))
    spreads = {}
    factors = {'mla_q_a_norm': 8.0,
     'mla_kv_a_norm': 5.695,
     'mla_q_norm': 8.0,
     'mla_k_norm': 7.214,
     'a_q_norm_g_2': 8.0,
     'a_k_norm_g_2': 8.0,
     'b_k_norm_g_2': 10.461,
     'lambda_q1_2': 8.717,
     'lambda_k2_2': 24.414,
     'b_q_norm_g_2': 2.696,
     'b_subln_g_2': 5.709,
     'mlp_norm_g_2': 2.717}
    for name, (base, spread) in spreads.items():
        noise = np.random.default_rng([zlib.crc32(name.encode()), seed]).standard_normal(out[name].shape)
        drawn = base * np.exp(spread * noise) if base else spread * noise
        out[name] = __import__('jax').numpy.asarray(drawn.astype(out[name].dtype))
    for name, factor in factors.items():
        out[name] = (out[name] * factor).astype(out[name].dtype)
    return out
```

```python
from contextlib import ExitStack

import numpy as np
import concourse.bass as bass
from concourse import mybir

F32 = mybir.dt.float32
F32R = mybir.dt.float32r
I32 = mybir.dt.int32
U32 = mybir.dt.uint32
ALU = mybir.AluOpType
ACT = mybir.ActivationFunctionType
AX = mybir.AxisListType

P = 128
D = 1024
TOK = 256
NT = TOK // P
KD = D // P
EPS = 1e-6
UNIT = 1024
WIDE = 512
RAW = 6
SPLIT = 6
ROUND = 2 * RAW

NH = 8
NOPE, ROPE, VD = 128, 64, 128
QH = NOPE + ROPE
QR, KVR = 384, 256
HD = 64
AQ, AKV, BQK, BV = 512, 128, 512, 512
IN2 = AQ + 2 * AKV + 2 * BQK + BV
NB2 = 4
BUCKETS = 32
LAMBDA0 = 0.8 - 0.6 * 1.0
FF1, FFE, FF2, NE = 2816, 2048, 4096, 8
FG = 256
FM = 512

U_IN = 0
U_OUT = U_IN + 24
U_FF1 = U_OUT + 8
U_DOWN = U_FF1 + 6 * (FF1 // FG)
U_UQ = U_DOWN + 6
U_UKV = U_UQ + 6
U_WO = U_UKV + 4
U_MOE = U_WO + 8
U_IN2 = U_MOE + NE * 6 * (FFE // FG)
U_OUT2 = U_IN2 + 18
U_FF2 = U_OUT2 + 8
U_END = U_FF2 + 8 * (FF2 // FM)
TOTAL = U_END + 2

COLS = {}
_at = 0
for _name, _n in (("mix0", 8), ("ffn0", 8), ("mix1", 8), ("ffn1", 8), ("attn2", 8), ("mlp2", 8), ("qa", 3), ("kva", 2),
                  ("qn", 1), ("kn", 1), ("conv", 24), ("bq", 1), ("bk", 1), ("sub", 1), ("router", 64)):
    COLS[_name] = _at
    _at += _n
NCOLS = _at
ROWS = {}
_at = 0
for _name, _n in (("qr", 64), ("kr", 64), ("aq", 64), ("ak", 64), ("lq1", 64), ("lk1", 64), ("lq2", 64), ("lk2", 64)):
    ROWS[_name] = _at
    _at += _n
NROWS = _at
FIXED = {}
_at = 0
for _name, _n in (("ident", 128), ("mask", 384), ("ctab", 128), ("stab", 128), ("freq", 32), ("iota", 8)):
    FIXED[_name] = _at
    _at += _n
NFIXED = _at

TWO_PI = 2.0 * np.pi
PI_A = 6.28125
PI_B = float(np.float32(np.round((TWO_PI - PI_A) * 2.0 ** 21) / 2.0 ** 21))
PI_C = float(TWO_PI - PI_A - PI_B)
ROUNDER = 1.5 * 2.0 ** 23
PI_IN = 3.1415925


def build(nc, x_in, pos_in, weights, cols_in, rows_in, fixed_in, onehot_in, relb_in, out):
    ctx = ExitStack()
    with ctx:
        def sb(name, shape, dt=F32):
            return ctx.enter_context(nc.sbuf_tensor(name, shape, dt))

        sems = {}

        def sem(name):
            if name not in sems:
                sems[name] = ctx.enter_context(nc.semaphore(name))
            return sems[name]

        raw = sb("raw", [P, RAW, 2 * UNIT])
        wh = sb("wh", [P, SPLIT, UNIT], F32R)
        wl = sb("wl", [P, SPLIT, UNIT], F32R)
        x = sb("x", [P, NT, D])
        xn = sb("xn", [P, NT, D])
        xth = sb("xth", [P, KD, TOK], F32R)
        xtl = sb("xtl", [P, KD, TOK], F32R)
        act = sb("act", [P, NT, 3584])
        wide = sb("wide", [P, 6144])
        hth = sb("hth", [P, 4, TOK], F32R)
        htl = sb("htl", [P, 4, TOK], F32R)
        ebuf = sb("ebuf", [P, NT, WIDE])
        hbuf = sb("hbuf", [P, NT, WIDE])
        cols = sb("cols", [P, NCOLS])
        rows = sb("rows", [P, NROWS])
        fixed = sb("fixed", [P, NFIXED])
        posi = sb("posi", [P, NT], I32)
        posf = sb("posf", [P, NT])
        relb = sb("relb", [BUCKETS, NB2])
        relw = sb("relw", [BUCKETS, NB2, P])
        ss = sb("ss", [P, 64])
        rs = sb("rs", [P, 64])
        sst = sb("sst", [P, 64])
        trig = sb("trig", [P, 2, NT, 32])
        gates = sb("gates", [P, NT, NE])
        rth = sb("rth", [P, KD * NE], F32R)
        rtl = sb("rtl", [P, KD * NE], F32R)
        small = sb("small", [P, 128])
        topi = sb("topi", [P, NT, 8], U32)
        lam = sb("lam", [P, 8])
        half = sb("half", [P, 64])
        bank = [ctx.enter_context(nc.psum_tensor(f"bank{i}", [P, WIDE], F32)) for i in range(8)]
        scratch = nc.dram_tensor("bias_scratch", (NB2 * P + 1, WIDE), F32).ap()

        ident = fixed[:, FIXED["ident"]:FIXED["ident"] + P]
        maskt = fixed[:, FIXED["mask"]:FIXED["mask"] + 384]
        onehot = ebuf[0:BUCKETS, 0, :]

        NORMS = ("mix0", "ffn0", "mix1", "ffn1", "attn2", "mlp2")

        def nth(tag):
            return NORMS.index(tag)

        raw_full = [sem(f"raw_full{i}") for i in range(RAW)]
        hi_done, lo_done, unit_used = sem("hi_done"), sem("lo_done"), sem("unit_used")

        def col(name, k=0):
            return cols[:, COLS[name] + k:COLS[name] + k + 1]

        def f32(ap):
            return ap.bitcast(F32)

        def bank_end(k, n):
            return min(k // 2 * 2 + 2, n)

        qv = act[:, :, 0:NH * QH].rearrange("p t (h d) -> p t h d", h=NH)
        kvv = act[:, :, NH * QH:NH * QH + NH * 256].rearrange("p t (h d) -> p t h d", h=NH)
        down = wide[:, 0:NT * 704].rearrange("p (t n) -> p t n", t=NT)
        sq = wide[:, 1408:1408 + NT * 1536].rearrange("p (t n) -> p t n", t=NT)
        kr1 = small[:, 0:128].rearrange("p (t n) -> p t n", t=NT)
        qrb = xn[:, :, 0:512].rearrange("p t (h d) -> p t h d", h=NH)
        krb = xn[:, :, 512:1024].rearrange("p t (h d) -> p t h d", h=NH)
        qnT = wide[:, 0:2048].rearrange("p (h n) -> p h n", h=NH)
        knT = wide[:, 2048:4096].rearrange("p (h n) -> p h n", h=NH)
        qrT = wide[:, 4096:5120].rearrange("p (h n) -> p h n", h=4)
        krT = wide[:, 5120:6144].rearrange("p (h n) -> p h n", h=4)
        hT2 = wide[:, 0:13 * TOK].rearrange("p (g n) -> p g n", g=13)
        bias2 = wide[:, 3328:3328 + NB2 * 2 * TOK].rearrange("p (h q n) -> p h q n", h=NB2, q=2)
        vp = wide[:, 0:KD * 258].rearrange("p (k n) -> p k n", k=KD)
        cv = wide[:, 2064:2064 + 2 * 256].rearrange("p (b n) -> p b n", b=2)
        cy = wide[:, 2576:2576 + 2 * 256].rearrange("p (b n) -> p b n", b=2)

        block = ctx.enter_context(nc.Block())

        @block.sync
        def _(sp):
            sp.dma_start(x[:, :, :], x_in.rearrange("(t p) d -> p t d", p=P)).then_inc(sem("x_in"), 16)
            for p in range(RAW):
                sp.dma_start(raw[:, p, :], weights[p]).then_inc(raw_full[p], 16)
            panels = TOTAL // 2
            rounds = (panels - RAW) // RAW

            def load(p, i):
                sp.wait_ge(lo_done, 2 * (p - RAW) + 2 + i * ROUND)
                src = weights[p] if isinstance(i, int) else weights[bass.ds(i * RAW + p, 1)].rearrange("a p n -> (a p) n")
                sp.dma_start(raw[:, p % RAW, :], src).then_inc(raw_full[p % RAW], 16)

            with sp.Fori(0, rounds) as i:
                for p in range(RAW, 2 * RAW):
                    load(p, i)
            for p in range(RAW + rounds * RAW, panels):
                load(p, 0)
            sp.wait_ge(sem("x_final"), 4)
            sp.dma_start(out.rearrange("(t p) d -> p t d", p=P), x[:, :, :]).then_inc(sem("stored"), 16)
            sp.wait_ge(sem("stored"), 16)

        @block.gpsimd
        def _(pool):
            g = nc.gpsimd
            pool.dma_start(fixed[:, :], fixed_in).then_inc(sem("fixed_in"), 16)
            pool.dma_start(cols[:, :], cols_in).then_inc(sem("cols_in"), 16)
            pool.dma_start(rows[:, :], rows_in.to_broadcast((P, NROWS))).then_inc(sem("rows_in"), 16)
            pool.dma_start(posi[:, :], pos_in).then_inc(sem("pos_in"), 16)
            pool.dma_start(relb[:, :], relb_in).then_inc(sem("rel_in"), 16)
            pool.dma_start(onehot, onehot_in).then_inc(sem("rel_in"), 16)

            g.memset(half[:, :], -0.5).then_inc(sem("half"), 1)
            pool.wait_ge(sem("half"), 1)

            def rsqrt(tag, a, b, n):
                g.tensor_scalar(sst[:, a:b], ss[:, a:b], 1.0 / n, EPS, ALU.mult, ALU.add).then_inc(sem(tag + "_ms"), 1)

            def power(tag, a, b):
                pool.wait_ge(sem(tag + "_ms"), 1)
                g.tensor_tensor(rs[:, a:b], sst[:, a:b], half[:, 0:b - a], ALU.pow).then_inc(sem(tag + "_rs"), 1)

            def norm_rs(tag):
                pool.wait_ge(sem("norm_ss"), NT * (nth(tag) + 1))
                g.tensor_scalar(sst[:, 0:NT], ss[:, 0:NT], 1.0 / D, EPS, ALU.mult, ALU.add).then_inc(sem("norm_ms"), 1)
                pool.wait_ge(sem("norm_ms"), nth(tag) + 1)
                g.tensor_tensor(rs[:, 0:NT], sst[:, 0:NT], half[:, 0:NT], ALU.pow).then_inc(sem("norm_rs"), 1)

            norm_rs("mix0")
            pool.wait_ge(sem("cv_v"), 2)
            norm_rs("ffn0")
            norm_rs("mix1")
            pool.wait_ge(sem("lora_ss"), 2 * NT)
            g.tensor_scalar(sst[:, 0:NT], ss[:, 0:NT], 1.0 / QR, EPS, ALU.mult, ALU.add).then_inc(sem("lora_m1"), 1)
            g.tensor_scalar(sst[:, NT:2 * NT], ss[:, NT:2 * NT], 1.0 / KVR, EPS, ALU.mult, ALU.add).then_inc(sem("lora_m2"), 1)
            pool.wait_ge(sem("lora_m1"), 1)
            pool.wait_ge(sem("lora_m2"), 1)
            g.tensor_tensor(rs[:, 0:2 * NT], sst[:, 0:2 * NT], half[:, 0:2 * NT], ALU.pow).then_inc(sem("lora_rs"), 1)
            pool.wait_ge(sem("qk_ss"), 1)
            rsqrt("qk", 0, 32, QH)
            power("qk", 0, 32)
            norm_rs("ffn1")
            norm_rs("attn2")
            pool.wait_ge(sem("h2_ss"), 1)
            rsqrt("h2", 0, 52, HD)
            power("h2", 0, 52)
            for h in range(NB2):
                pool.wait_ge(sem("ob_ss"), 2 * h + 2)
                g.tensor_scalar(sst[:, 2 * h:2 * h + 2], ss[:, 2 * h:2 * h + 2], 1.0 / VD, EPS, ALU.mult, ALU.add)\
                 .then_inc(sem("ob_ms"), 1)
                pool.wait_ge(sem("ob_ms"), h + 1)
                g.tensor_tensor(rs[:, 2 * h:2 * h + 2], sst[:, 2 * h:2 * h + 2], half[:, 0:2], ALU.pow)\
                 .then_inc(sem("ob_rs"), 1)
            norm_rs("mlp2")

        @block.tensor
        def _(pe):
            mm = nc.tensor.matmul

            def mm3(o, lh, ll, wi, sl, start, stop):
                mm(o, lh, wh[:, wi, sl], start=start, stop=False)
                mm(o, lh, wl[:, wi, sl], start=False, stop=False)
                return mm(o, ll, wh[:, wi, sl], start=False, stop=stop)

            def xt(k, t):
                return xth[:, k, t * P:(t + 1) * P], xtl[:, k, t * P:(t + 1) * P]

            def product(c, i, ks, width, banks, k_first, k_last, k0=0):
                pe.wait_ge(lo_done, c + 1 + ROUND * i)
                for n, k in enumerate(ks):
                    for t in range(NT):
                        last = mm3(banks[t][:, 0:width], *xt(k0 + k, t), c % SPLIT, slice(n * width, (n + 1) * width),
                                   k == k_first, k == k_last)
                last.then_inc(unit_used, 1)

            def chunk512(c, i, banks):
                for u in range(4):
                    product(c + u, i, (2 * u, 2 * u + 1), WIDE, banks, 0, KD - 1)

            def turn_norm(tag):
                pe.wait_ge(sem("norm_xn"), NT * (nth(tag) + 1))
                for k in range(KD):
                    for t in range(NT):
                        last = nc.tensor.transpose(bank[4 + k // 2][:, (k % 2) * 256 + t * P:(k % 2) * 256 + (t + 1) * P],
                                                   xn[:, t, k * P:(k + 1) * P], ident)
                    last.then_inc(sem("norm_T"), 1)

            def ffn(tag, c0, nf, U, loops, width, nd, i0, f0=0):
                nj = width // P
                ug = 4

                def up(c, i):
                    for u in range(ug):
                        product(c + u, i, (2 * u, 2 * u + 1), WIDE, bank[0:2], 0, KD - 1)

                def turn(fc, fv):
                    for t in range(NT):
                        pe.wait_ge(sem(tag + "_h"), 2 * fc + t + 1 + fv * 2)
                        for j in range(nj):
                            last = nc.tensor.transpose(bank[2 + t][:, j * P:(j + 1) * P], hbuf[:, t, j * P:(j + 1) * P], ident)
                        last.then_inc(sem(tag + "_hT"), 1)

                def down_(c, i, fc, fv, first, final):
                    pe.wait_ge(sem(tag + "_hTl"), 2 * fc + 2 + fv * 2)
                    for j in range(nd):
                        pe.wait_ge(lo_done, c + j + 1 + ROUND * i)
                        for t in range(NT):
                            for n in range(2):
                                last = mm3(bank[4 + 2 * t + n][:, :], hth[:, j, t * P:(t + 1) * P],
                                           htl[:, j, t * P:(t + 1) * P], (c + j) % SPLIT, slice(n * WIDE, (n + 1) * WIDE),
                                           first and j == 0, final and j == nd - 1)
                        last.then_inc(unit_used, 1)

                fb = nf * f0
                up(c0, i0)
                turn(0, fb)
                up(c0 + ug, i0)
                down_(c0 + 2 * ug, i0, 0, fb, True, False)
                turn(1, fb)
                c = c0 + 2 * ug + nd
                with pe.Fori(0, loops) as it:
                    ii = i0 + it * (U * (ug + nd) // ROUND)
                    for s in range(U):
                        up(c + s * (ug + nd), ii)
                        down_(c + s * (ug + nd) + ug, ii, 1 + s, fb + it * U, False, False)
                        turn(2 + s, fb + it * U)
                c += loops * U * (ug + nd)
                for f in range(2 + loops * U, nf):
                    up(c, i0)
                    down_(c + ug, i0, f - 1, fb, False, False)
                    turn(f, fb)
                    c += ug + nd
                down_(c, i0, nf - 1, fb, False, True)

            pe.wait_ge(sem("rel_w"), 1)
            pe.wait_ge(sem("rel_in"), 32)
            for h in range(NB2):
                mm(bank[h][:, :], relw[:, h, :], onehot, start=True, stop=True).then_inc(sem("rel_T"), 1)

            pe.wait_ge(sem("fixed_in"), 16)
            turn_norm("mix0")
            pe.wait_ge(sem("norm_l"), KD * (nth("mix0") + 1))
            pe.wait_ge(sem("rel_c"), NB2)
            with pe.Fori(0, 2) as i:
                for j in range(3):
                    if j == 0:
                        pass
                    pe.wait_ge(sem("in_go"), 3 * i + j + 1)
                    chunk512(U_IN + 4 * j, i, bank[2 * j:2 * j + 2])
            pe.wait_ge(sem("in_c"), 2 * 6)
            pe.wait_ge(sem("cv_v"), 2)
            for s, src in enumerate((xn, act)):
                for k in range(KD):
                    for t in range(NT):
                        last = nc.tensor.transpose(bank[4 * s + k // 2][:, (k % 2) * 256 + t * P:(k % 2) * 256 + (t + 1) * P],
                                                   src[:, t, k * P:(k + 1) * P], ident)
                    last.then_inc(sem("cv_T"), 1)
            pe.wait_ge(sem("cv_l"), KD)
            for n in range(2):
                chunk512(U_OUT + 4 * n, 0, bank[2 * n:2 * n + 2])

            turn_norm("ffn0")
            pe.wait_ge(sem("norm_l"), KD * (nth("ffn0") + 1))
            pe.wait_ge(sem("out_r"), 4)
            ffn("f1", U_FF1, FF1 // FG, 2, 4, FG, 2, 0)

            turn_norm("mix1")
            pe.wait_ge(sem("norm_l"), KD * (nth("mix1") + 1))
            pe.wait_ge(sem("f1_r"), 4)
            chunk512(U_DOWN, 0, bank[0:2])
            for u in range(2):
                product(U_DOWN + 4 + u, 0, range(4 * u, 4 * u + 4), 192, bank[2:4], 0, KD - 1)
            pe.wait_ge(sem("lora_xn"), 2 * NT)
            for k in range(5):
                for t in range(NT):
                    last = nc.tensor.transpose(bank[4 + k // 2][:, (k % 2) * 256 + t * P:(k % 2) * 256 + (t + 1) * P],
                                               xn[:, t, k * P:(k + 1) * P], ident)
                last.then_inc(sem("lora_T"), 1)
            pe.wait_ge(sem("lora_l"), 5)
            pe.wait_ge(sem("down_c"), 4)
            for n in range(7):
                if n >= 2:
                    pe.wait_ge(sem("quv_c"), 2 * (n - 1))
                b = bank[2 * (n % 2):2 * (n % 2) + 2]
                if n < 3:
                    product(U_UQ + 2 * n, 0, (0, 1), WIDE, b, 0, 2)
                    product(U_UQ + 2 * n + 1, 0, (2,), WIDE, b, 0, 2)
                else:
                    product(U_UKV + n - 3, 0, (0, 1), WIDE, b, 0, 1, k0=3)
            pe.wait_ge(sem("quv_c"), 14)
            for n in range(12):
                if n == 0:
                    pe.wait_ge(sem("q_ready"), 1)
                if n == 4:
                    pe.wait_ge(sem("k_ready"), 1)
                if n >= 8:
                    pe.wait_ge(sem("qkT_a"), (n - 8) // 2 + 1 if n % 2 == 0 else (n - 9) // 2 + 1)
                    pe.wait_ge(sem("qkT_d"), (n - 8 + 1) // 2 if n > 8 else 1)
                for m in range(2):
                    for t in range(NT):
                        if n < 4:
                            src = qv[:, t, 2 * n + m, 0:NOPE]
                        elif n < 8:
                            src = kvv[:, t, 2 * (n - 4) + m, 0:NOPE]
                        elif n < 10:
                            src = xn[:, t, (2 * (n - 8) + m) * P:(2 * (n - 8) + m + 1) * P]
                        else:
                            src = xn[:, t, 512 + (2 * (n - 10) + m) * P:512 + (2 * (n - 10) + m + 1) * P]
                        last = nc.tensor.transpose(bank[n % 8][:, m * 256 + t * P:m * 256 + (t + 1) * P], src, ident)
                last.then_inc(sem("qk_T"), 1)
            pe.wait_ge(sem("qkT_a"), 6)
            pe.wait_ge(sem("qkT_d"), 6)
            for s in range(NH + 2):
                if s < NH:
                    h = s
                    if h >= 2:
                        pe.wait_ge(sem("m_sc"), h - 1)
                    r0 = (h % 2) * 64
                    for qb, (a, n) in enumerate(((0, P), (P, 2 * P))):
                        o = bank[h % 2][:, a:a + n]
                        mm(o, qnT[:, h, qb * P:(qb + 1) * P], knT[:, h, 0:n], start=True, stop=False)
                        last = mm(o, qrT[r0:r0 + 64, h // 2, qb * P:(qb + 1) * P], krT[r0:r0 + 64, h // 2, 0:n],
                                  start=False, stop=True)
                    last.then_inc(sem("m_S"), 1)
                if 1 <= s <= NH:
                    h = s - 1
                    pe.wait_ge(sem("m_p"), h + 1)
                    if h >= 2:
                        pe.wait_ge(sem("m_pT"), h - 1)
                    for j in range(3):
                        last = nc.tensor.transpose(bank[2 + h % 2][:, j * P:(j + 1) * P], ebuf[:, h % 2, j * P:(j + 1) * P], ident)
                    last.then_inc(sem("m_PT"), 1)
                if s >= 2:
                    h = s - 2
                    pe.wait_ge(sem("m_pT"), h + 1)
                    if h >= 2:
                        pe.wait_ge(sem("m_ol"), h - 1)
                    mm(bank[4 + h % 2][:, 0:P], kvv[:, 0, h, NOPE:256], hbuf[:, h % 2, 0:P], start=True, stop=True)
                    mm(bank[4 + h % 2][:, P:256], kvv[:, 0, h, NOPE:256], hbuf[:, h % 2, P:256], start=True, stop=False)
                    mm(bank[4 + h % 2][:, P:256], kvv[:, 1, h, NOPE:256], hbuf[:, h % 2, 256:384], start=False, stop=True)\
                        .then_inc(sem("m_O"), 1)
            pe.wait_ge(sem("m_ol"), NH)
            for n in range(2):
                chunk512(U_WO + 4 * n, 0, bank[2 * n:2 * n + 2])

            turn_norm("ffn1")
            pe.wait_ge(sem("norm_l"), KD * (nth("ffn1") + 1))
            pe.wait_ge(sem("wo_r"), 4)
            pe.wait_ge(sem("rt_l"), 1)
            for t in range(NT):
                for k in range(KD):
                    h, l = xt(k, t)
                    o = bank[t][:, 0:NE]
                    mm(o, h, rth[:, k * NE:(k + 1) * NE], start=(k == 0), stop=False)
                    mm(o, h, rtl[:, k * NE:(k + 1) * NE], start=False, stop=False)
                    last = mm(o, l, rth[:, k * NE:(k + 1) * NE], start=False, stop=(k == KD - 1))
                last.then_inc(sem("rt_S"), 1)
            pe.wait_ge(sem("rt_c"), 2)
            with pe.Fori(0, NE) as e:
                pe.wait_ge(sem("moe_go"), e * 4 + 4)
                ffn("fe", U_MOE, FFE // FG, 2, 3, FG, 2, e * 4, e)

            turn_norm("attn2")
            pe.wait_ge(sem("norm_l"), KD * (nth("attn2") + 1))
            pe.wait_ge(sem("moe_go"), 4 * NE + 4)
            for n in range(5):
                if n >= 2:
                    pe.wait_ge(sem("in2_c"), 2 * (n - 1))
                b = bank[2 * (n % 2):2 * (n % 2) + 2]
                if n < 4:
                    chunk512(U_IN2 + 4 * n, 0, b)
                else:
                    for u in range(2):
                        product(U_IN2 + 16 + u, 0, range(4 * u, 4 * u + 4), 256, b, 0, KD - 1)
            pe.wait_ge(sem("in2_c"), 10)
            for g in range(13):
                if g == 0:
                    pe.wait_ge(sem("a_ready"), 1)
                if g == 5:
                    pe.wait_ge(sem("b_ready"), 1)
                for t in range(NT):
                    if g < 5:
                        src = xn[:, t, g * P:(g + 1) * P]
                    else:
                        src = act[:, t, 768 + (g - 5) * P:768 + (g - 4) * P]
                    last = nc.tensor.transpose(bank[g // 2][:, (g % 2) * 256 + t * P:(g % 2) * 256 + (t + 1) * P], src, ident)
                last.then_inc(sem("h2_T"), 1)
            pe.wait_ge(sem("h2T_c"), 13)
            for s in range(NH + 2):
                if s < NH:
                    h = s
                    if h >= 2:
                        pe.wait_ge(sem("a_sc"), h - 1)
                    r0 = (h // 4) * 64
                    for qb in range(2):
                        last = mm(bank[h % 2][:, qb * 256:(qb + 1) * 256], hT2[r0:r0 + 64, h % 4, qb * P:(qb + 1) * P],
                                  hT2[r0:r0 + 64, 4, :], start=True, stop=True)
                    last.then_inc(sem("a_S"), 1)
                if 1 <= s <= NH:
                    h = s - 1
                    pe.wait_ge(sem("a_p"), h + 1)
                    if h >= 2:
                        pe.wait_ge(sem("a_pT"), h - 1)
                    for kb in range(2):
                        for qb in range(2):
                            last = nc.tensor.transpose(bank[2 + h % 2][:, kb * 256 + qb * P:kb * 256 + (qb + 1) * P],
                                                       ebuf[:, h % 2, qb * 256 + kb * P:qb * 256 + (kb + 1) * P], ident)
                    last.then_inc(sem("a_PT"), 1)
                if s >= 2:
                    h = s - 2
                    pe.wait_ge(sem("a_pT"), h + 1)
                    if h >= 4 and h % 2 == 0:
                        pe.wait_ge(sem("a_ol"), h // 2 - 1)
                    r0 = (h % 2) * 64
                    v0 = 640 + (h // 4) * 64
                    for kb in range(2):
                        last = mm(bank[4 + (h // 2) % 2][r0:r0 + 64, 0:256], act[:, kb, v0:v0 + 64],
                                  hbuf[:, h % 2, kb * 256:(kb + 1) * 256], start=(kb == 0), stop=(kb == 1))
                    last.then_inc(sem("a_O"), 1)
            pe.wait_ge(sem("a_ol"), 4)
            for s in range(NB2 + 1):
                if s < NB2:
                    h = s
                    for c in range(2):
                        if h >= 2:
                            pe.wait_ge(sem("b_sc"), 2 * (h - 2) + c + 1)
                        for qb in range(2):
                            last = mm(bank[2 * (h % 2) + c][:, qb * 256:(qb + 1) * 256],
                                      hT2[c * 64:c * 64 + 64, 5 + h, qb * P:(qb + 1) * P],
                                      hT2[c * 64:c * 64 + 64, 9 + h, :], start=True, stop=True)
                        last.then_inc(sem("b_S"), 1)
                if s >= 1:
                    h = s - 1
                    pe.wait_ge(sem("b_p"), h + 1)
                    if h >= 2:
                        pe.wait_ge(sem("b_pT"), h - 1)
                    for kb in range(2):
                        for qb in range(2):
                            last = nc.tensor.transpose(bank[4 + h % 2][:, kb * 256 + qb * P:kb * 256 + (qb + 1) * P],
                                                       hbuf[:, 0, qb * 256 + kb * P:qb * 256 + (kb + 1) * P], ident)
                    last.then_inc(sem("b_PT"), 1)
                    pe.wait_ge(sem("b_pT"), h + 1)
                    if h >= 2:
                        pe.wait_ge(sem("ob_c"), 2 * (h - 1))
                    for qb in range(2):
                        for kb in range(2):
                            last = mm(bank[6 + h % 2][:, qb * P:(qb + 1) * P],
                                      hbuf[:, 1, kb * 256 + qb * P:kb * 256 + (qb + 1) * P],
                                      act[:, kb, 1792 + h * P:1792 + (h + 1) * P], start=(kb == 0), stop=(kb == 1))
                    last.then_inc(sem("b_O"), 1)
            pe.wait_ge(sem("ob_c"), 2 * NB2)
            for h in range(NB2):
                for t in range(NT):
                    last = nc.tensor.transpose(bank[4 + h // 2][:, (h % 2) * 256 + t * P:(h % 2) * 256 + (t + 1) * P],
                                               xn[:, t, h * P:(h + 1) * P], ident)
                last.then_inc(sem("ob_T"), 1)
            pe.wait_ge(sem("ob_l"), NB2)
            for n in range(2):
                chunk512(U_OUT2 + 4 * n, 0, bank[2 * n:2 * n + 2])

            turn_norm("mlp2")
            pe.wait_ge(sem("norm_l"), KD * (nth("mlp2") + 1))
            pe.wait_ge(sem("out2_r"), 4)
            ffn("f2", U_FF2, FF2 // FM, 3, 2, FM, 4, 0)

        @block.scalar
        def _(sc):
            A = nc.scalar.activation

            def split_hi(c, i):
                sc.wait_ge(raw_full[(c // 2) % RAW], 16 * (c // ROUND + 1) + 16 * i)
                if c >= SPLIT:
                    sc.wait_ge(unit_used, c - SPLIT + 1 + ROUND * i)
                A(wh[:, c % SPLIT, :], raw[:, (c // 2) % RAW, (c % 2) * UNIT:(c % 2 + 1) * UNIT], ACT.Copy).then_inc(hi_done, 1)

            def follow(c, n, i):
                for u in range(c, c + n):
                    if u + SPLIT < TOTAL:
                        split_hi(u + SPLIT, i)
                    else:
                        sc.wait_ge(unit_used, u + 1 + ROUND * i)

            def norm(tag, ready, n):
                sc.wait_ge(sem(ready), n)
                for t in range(NT):
                    A(xn[:, t, :], x[:, t, :], ACT.Square, accum_out=ss[:, t:t + 1]).then_inc(sem("norm_ss"), 1)
                sc.wait_ge(sem("norm_rs"), nth(tag) + 1)
                A(xn[:, 1, :], x[:, 1, :], ACT.Copy, scale=rs[:, 1:2]).then_inc(sem("norm_xn"), 1)
                for k in range(KD):
                    sc.wait_ge(sem("norm_T"), KD * nth(tag) + bank_end(k, KD))
                    A(xth[:, k, :], bank[4 + k // 2][:, (k % 2) * 256:(k % 2 + 1) * 256], ACT.Copy, scale=col(tag, k))\
                        .then_inc(sem("norm_hi"), 1)

            def ffn(tag, c0, nf, U, loops, width, nd, i0, f0=0):
                nj = width // P
                ug = 4

                def evac(fc, fv):
                    for t in range(NT):
                        if nd == 2:
                            A(ebuf[:, t, 0:FG], bank[t][:, 0:FG], ACT.Tanh, scale=0.5).then_inc(sem(tag + "_e"), 1)
                        else:
                            A(ebuf[:, t, :], bank[t][:, :], ACT.Relu).then_inc(sem(tag + "_e"), 1)

                def turned(fc, fv):
                    for t in range(NT):
                        sc.wait_ge(sem(tag + "_hT"), 2 * fc + t + 1 + fv * 2)
                        A(hth[:, 0:nj, t * P:(t + 1) * P], bank[2 + t][:, 0:width].rearrange("p (j n) -> p j n", j=nj),
                          ACT.Copy).then_inc(sem(tag + "_hTh"), 1)

                fb = nf * f0
                follow(c0, ug, i0)
                evac(0, fb)
                turned(0, fb)
                follow(c0 + ug, ug, i0)
                evac(1, fb)
                follow(c0 + 2 * ug, nd, i0)
                turned(1, fb)
                c = c0 + 2 * ug + nd
                with sc.Fori(0, loops) as it:
                    ii = i0 + it * (U * (ug + nd) // ROUND)
                    for s in range(U):
                        follow(c + s * (ug + nd), ug, ii)
                        evac(2 + s, fb + it * U)
                        follow(c + s * (ug + nd) + ug, nd, ii)
                        turned(2 + s, fb + it * U)
                c += loops * U * (ug + nd)
                for f in range(2 + loops * U, nf):
                    follow(c, ug, i0)
                    evac(f, fb)
                    follow(c + ug, nd, i0)
                    turned(f, fb)
                    c += ug + nd
                follow(c, nd, i0)

            for c in range(SPLIT):
                split_hi(c, 0)
            sc.wait_ge(sem("cols_in"), 16)
            norm("mix0", "x_in", 16)
            for h in range(NB2):
                sc.wait_ge(sem("rel_T"), h + 1)
                A(act[:, 0, h * WIDE:(h + 1) * WIDE], bank[h][:, :], ACT.Copy).then_inc(sem("rel_c"), 1)
            sc.wait_ge(sem("rel_c"), NB2)
            sc.dma_start(scratch[0:NB2 * P, :].rearrange("(h p) n -> p h n", p=P), act[:, 0, 0:NB2 * WIDE].rearrange("p (h n) -> p h n", h=NB2))\
              .then_inc(sem("rel_st"), 16)
            sc.wait_ge(sem("rel_st"), 16)
            with sc.Fori(0, 2) as i:
                for j in range(3):
                    follow(U_IN + 4 * j, 4, i)
                    for t in range(NT):
                        A(act[:, t, bass.ds(i * 1536 + j * WIDE, WIDE)], bank[2 * j + t][:, :], ACT.Copy).then_inc(sem("in_c"), 1)
            for k in range(KD):
                sc.wait_ge(sem("cv_T"), bank_end(k, KD))
                sc.wait_ge(sem("cv_z"), 1)
                A(vp[:, k, 2:258], bank[k // 2][:, (k % 2) * 256:(k % 2 + 1) * 256], ACT.Copy).then_inc(sem("cv_p"), 1)
            for k in range(KD):
                sc.wait_ge(sem("cv_y"), k + 1)
                A(xth[:, k, :], cy[:, k % 2, :], ACT.Copy).then_inc(sem("cv_hi"), 1)
            follow(U_OUT, 8, 0)

            norm("ffn0", "out_r", 4)
            ffn("f1", U_FF1, FF1 // FG, 2, 4, FG, 2, 0)

            norm("mix1", "f1_r", 4)
            sc.wait_ge(sem("ang"), 1)
            A(trig[:, :, :, :], trig[:, :, :, :], ACT.Sin).then_inc(sem("trig"), 1)
            follow(U_DOWN, 4, 0)
            for t in range(NT):
                A(down[:, t, 0:WIDE], bank[t][:, :], ACT.Copy).then_inc(sem("down_c"), 1)
            follow(U_DOWN + 4, 2, 0)
            for t in range(NT):
                A(down[:, t, WIDE:704], bank[2 + t][:, 0:192], ACT.Copy).then_inc(sem("down_c"), 1)
            sc.wait_ge(sem("down_c"), 4)
            for t in range(NT):
                A(xn[:, t, 0:QR], down[:, t, 0:QR], ACT.Square, accum_out=ss[:, t:t + 1]).then_inc(sem("lora_ss"), 1)
                A(xn[:, t, QR:QR + KVR], down[:, t, QR:QR + KVR], ACT.Square, accum_out=ss[:, NT + t:NT + t + 1])\
                    .then_inc(sem("lora_ss"), 1)
            for k in range(5):
                sc.wait_ge(sem("lora_T"), bank_end(k, 5))
                A(xth[:, k, :], bank[4 + k // 2][:, (k % 2) * 256:(k % 2 + 1) * 256], ACT.Copy,
                  scale=col("qa", k) if k < 3 else col("kva", k - 3)).then_inc(sem("lora_hi"), 1)
            for n in range(7):
                if n < 3:
                    follow(U_UQ + 2 * n, 2, 0)
                else:
                    follow(U_UKV + n - 3, 1, 0)
                for t in range(NT):
                    A(act[:, t, n * WIDE:(n + 1) * WIDE], bank[2 * (n % 2) + t][:, :], ACT.Copy).then_inc(sem("quv_c"), 1)
            sc.wait_ge(sem("quv_c"), 14)
            sc.wait_ge(sem("kr1"), 1)
            for t in range(NT):
                A(sq[:, t, :], act[:, t, 0:NH * QH], ACT.Square).then_inc(sem("q_sq"), 1)
            for t in range(NT):
                sc.wait_ge(sem("q_sr"), t + 1)
                A(sq[:, t, 0:1024].rearrange("p (h d) -> p h d", h=NH), kvv[:, t, :, 0:NOPE], ACT.Square).then_inc(sem("k_sq"), 1)
            for n in range(0, 12, 2):
                sc.wait_ge(sem("qk_T"), n + 1)
                g = {"scale": col("qn")} if n < 4 else {"scale": col("kn")} if n < 8 else {}
                A(wide[:, n * WIDE:(n + 1) * WIDE], bank[n % 8][:, :], ACT.Copy, **g).then_inc(sem("qkT_a"), 1)
            for s in range(NH + 2):
                if s < NH:
                    h = s
                    sc.wait_ge(sem("m_nm"), h + 1)
                    for qb, (a, n) in enumerate(((0, P), (P, 2 * P))):
                        A(ebuf[:, h % 2, a:a + n], ebuf[:, h % 2, a:a + n], ACT.Exp,
                          bias=small[:, 64 + 2 * (h % 2) + qb:65 + 2 * (h % 2) + qb],
                          accum_out=small[:, 72 + 2 * (h % 2) + qb:73 + 2 * (h % 2) + qb]).then_inc(sem("m_e"), 1)
                if 1 <= s <= NH:
                    h = s - 1
                    sc.wait_ge(sem("m_PT"), h + 1)
                    if h >= 2:
                        sc.wait_ge(sem("m_O"), h - 1)
                    A(hbuf[:, h % 2, 0:384], bank[2 + h % 2][:, 0:384], ACT.Copy).then_inc(sem("m_pT"), 1)
                if s >= 2:
                    h = s - 2
                    sc.wait_ge(sem("m_O"), h + 1)
                    A(xth[:, h, :], bank[4 + h % 2][:, 0:256], ACT.Copy).then_inc(sem("m_oh"), 1)
            follow(U_WO, 8, 0)

            A(rth[:, :], cols[:, COLS["router"]:COLS["router"] + 64], ACT.Copy).then_inc(sem("rt_h"), 1)
            norm("ffn1", "wo_r", 4)
            for t in range(NT):
                sc.wait_ge(sem("rt_m"), t + 1)
                A(small[:, 32 * t:32 * t + NE], small[:, 32 * t:32 * t + NE], ACT.Exp,
                  bias=small[:, 32 * t + 8:32 * t + 9], accum_out=small[:, 32 * t + 9:32 * t + 10]).then_inc(sem("rt_e"), 1)
            with sc.Fori(0, NE) as e:
                ffn("fe", U_MOE, FFE // FG, 2, 3, FG, 2, e * 4, e)

            norm("attn2", "moe_go", 4 * NE + 4)
            for h in range(NB2):
                for qb in range(2):
                    at = h * P * WIDE + TOK - 1 - P * qb
                    src = scratch.rearrange("r n -> (r n)")[at:at + P * (WIDE - 1)]
                    sc.dma_start(bias2[:, h, qb, :], src.rearrange("(p n) -> p n", p=P)[:, 0:256]).then_inc(sem("bias_in"), 16)
            for n in range(5):
                w = WIDE if n < 4 else 256
                follow(U_IN2 + 4 * n, 4 if n < 4 else 2, 0)
                for t in range(NT):
                    A(act[:, t, n * WIDE:n * WIDE + w], bank[2 * (n % 2) + t][:, 0:w], ACT.Copy).then_inc(sem("in2_c"), 1)
            sc.wait_ge(sem("lam_s"), 2)
            A(lam[:, 2:4], lam[:, 0:2], ACT.Exp).then_inc(sem("lam_e"), 1)
            for g in range(13):
                sc.wait_ge(sem("h2_T"), bank_end(g, 13))
                gg = {} if g < 5 else {"scale": col("bq" if g < 9 else "bk")}
                A(hT2[:, g, :], bank[g // 2][:, (g % 2) * 256:(g % 2 + 1) * 256], ACT.Copy, **gg).then_inc(sem("h2T_c"), 1)
            for s in range(NH + 2):
                if s < NH:
                    h = s
                    sc.wait_ge(sem("a_nm"), h + 1)
                    if h >= 2:
                        sc.wait_ge(sem("a_PT"), h - 1)
                    for qb in range(2):
                        A(ebuf[:, h % 2, qb * 256:(qb + 1) * 256], bank[h % 2][:, qb * 256:(qb + 1) * 256], ACT.Exp,
                          scale=HD ** -0.5, bias=small[:, 64 + 2 * (h % 2) + qb:65 + 2 * (h % 2) + qb],
                          accum_out=small[:, 72 + 2 * (h % 2) + qb:73 + 2 * (h % 2) + qb]).then_inc(sem("a_e"), 1)
                if 1 <= s <= NH:
                    h = s - 1
                    sc.wait_ge(sem("a_PT"), h + 1)
                    if h >= 2:
                        sc.wait_ge(sem("a_O"), h - 1)
                    A(hbuf[:, h % 2, :], bank[2 + h % 2][:, :], ACT.Copy).then_inc(sem("a_pT"), 1)
                if s >= 2 and s % 2 == 1:
                    j = (s - 2) // 2
                    sc.wait_ge(sem("a_O"), 2 * j + 2)
                    A(xth[:, j, :], bank[4 + j % 2][:, 0:256], ACT.Copy).then_inc(sem("a_oh"), 1)
            for s in range(NB2 + 1):
                if s < NB2:
                    h = s
                    for c in range(2):
                        sc.wait_ge(sem("b_nm"), 2 * h + c + 1)
                        for qb in range(2):
                            m = 4 * (h % 2) + 2 * c + qb
                            A(act[:, h % 2, 2304 + c * 512 + qb * 256:2304 + c * 512 + (qb + 1) * 256],
                              act[:, h % 2, 2304 + c * 512 + qb * 256:2304 + c * 512 + (qb + 1) * 256],
                              ACT.Exp, bias=small[:, 80 + m:81 + m], accum_out=small[:, 96 + m:97 + m]).then_inc(sem("b_e"), 1)
                if s >= 1:
                    h = s - 1
                    sc.wait_ge(sem("b_PT"), h + 1)
                    if h >= 1:
                        sc.wait_ge(sem("b_O"), h)
                    A(hbuf[:, 1, :], bank[4 + h % 2][:, :], ACT.Copy).then_inc(sem("b_pT"), 1)
                    sc.wait_ge(sem("b_O"), h + 1)
                    for t in range(NT):
                        A(xn[:, t, h * P:(h + 1) * P], bank[6 + h % 2][:, t * P:(t + 1) * P], ACT.Square,
                          accum_out=ss[:, 2 * h + t:2 * h + t + 1]).then_inc(sem("ob_ss"), 1)
            for h in range(NB2):
                sc.wait_ge(sem("ob_T"), bank_end(h, NB2))
                sc.wait_ge(sem("sub_g"), 1)
                A(xth[:, 4 + h, :], bank[4 + h // 2][:, (h % 2) * 256:(h % 2 + 1) * 256], ACT.Copy, scale=lam[:, 5:6])\
                    .then_inc(sem("ob_h"), 1)
            follow(U_OUT2, 8, 0)

            norm("mlp2", "out2_r", 4)
            ffn("f2", U_FF2, FF2 // FM, 3, 2, FM, 4, 0)

        @block.vector
        def _(dv):
            V = nc.vector
            chain = [0]
            dve_chain = sem("dve_chain")

            def link(ins):
                chain[0] += 1
                ins.then_inc(dve_chain, 1)
                dv.wait_ge(dve_chain, chain[0])

            def split_lo(c, i):
                dv.wait_ge(hi_done, c + 1 + ROUND * i)
                V.tensor_tensor(wl[:, c % SPLIT, :], raw[:, (c // 2) % RAW, (c % 2) * UNIT:(c % 2 + 1) * UNIT],
                                f32(wh[:, c % SPLIT, :]), ALU.subtract).then_inc(lo_done, 1)

            def follow(c, n, i):
                for u in range(c, c + n):
                    if u + SPLIT < TOTAL:
                        split_lo(u + SPLIT, i)
                    else:
                        dv.wait_ge(unit_used, u + 1 + ROUND * i)

            def follow_used(c, n, i):
                follow(c, n, i)
                dv.wait_ge(unit_used, c + n + ROUND * i)

            def norm(tag):
                dv.wait_ge(sem("norm_rs"), nth(tag) + 1)
                V.tensor_scalar(xn[:, 0, :], x[:, 0, :], rs[:, 0:1], None, ALU.mult).then_inc(sem("norm_xn"), 1)
                for k in range(KD):
                    dv.wait_ge(sem("norm_hi"), KD * nth(tag) + bank_end(k, KD))
                    V.scalar_tensor_tensor(out=xtl[:, k, :], in0=bank[4 + k // 2][:, (k % 2) * 256:(k % 2 + 1) * 256],
                                           scalar=col(tag, k), in1=f32(xth[:, k, :]), op0=ALU.mult, op1=ALU.subtract)\
                     .then_inc(sem("norm_l"), 1)

            def residual(c0, tag):
                for n in range(2):
                    follow_used(c0 + 4 * n, 4, 0)
                    for t in range(NT):
                        V.tensor_tensor(x[:, t, n * WIDE:(n + 1) * WIDE], x[:, t, n * WIDE:(n + 1) * WIDE],
                                        bank[2 * n + t][:, :], ALU.add).then_inc(sem(tag), 1)

            def ffn(tag, c0, nf, U, loops, width, nd, i0, f0=0):
                nj = width // P
                ug = 4

                def evac(fc, fv):
                    for t in range(NT):
                        dv.wait_ge(sem(tag + "_e"), 2 * fc + t + 1 + fv * 2)
                        if nd == 2:
                            step = sem(tag + "_s")
                            e, g, u, h = ebuf[:, t, 0:FG], bank[t][:, 0:FG], bank[t][:, FG:2 * FG], hbuf[:, t, 0:FG]
                            V.scalar_tensor_tensor(out=e, in0=e, scalar=1.0, in1=g, op0=ALU.add, op1=ALU.mult).then_inc(step, 1)
                            dv.wait_ge(step, 2 * fc + t + 1 + fv * 2)
                            V.scalar_tensor_tensor(out=h, in0=e, scalar=0.5, in1=u, op0=ALU.mult, op1=ALU.mult)\
                             .then_inc(sem(tag + "_h"), 1)
                        else:
                            V.tensor_tensor(hbuf[:, t, :], ebuf[:, t, :], ebuf[:, t, :], ALU.mult).then_inc(sem(tag + "_h"), 1)

                def turned(fc, fv):
                    for t in range(NT):
                        dv.wait_ge(sem(tag + "_hTh"), 2 * fc + t + 1 + fv * 2)
                        V.tensor_tensor(htl[:, 0:nj, t * P:(t + 1) * P], bank[2 + t][:, 0:width].rearrange("p (j n) -> p j n", j=nj),
                                        f32(hth[:, 0:nj, t * P:(t + 1) * P]), ALU.subtract).then_inc(sem(tag + "_hTl"), 1)

                fb = nf * f0
                follow(c0, ug, i0)
                evac(0, fb)
                turned(0, fb)
                follow(c0 + ug, ug, i0)
                evac(1, fb)
                follow(c0 + 2 * ug, nd, i0)
                turned(1, fb)
                c = c0 + 2 * ug + nd
                with dv.Fori(0, loops) as it:
                    ii = i0 + it * (U * (ug + nd) // ROUND)
                    for s in range(U):
                        follow(c + s * (ug + nd), ug, ii)
                        evac(2 + s, fb + it * U)
                        follow(c + s * (ug + nd) + ug, nd, ii)
                        turned(2 + s, fb + it * U)
                c += loops * U * (ug + nd)
                for f in range(2 + loops * U, nf):
                    follow(c, ug, i0)
                    evac(f, fb)
                    follow(c + ug, nd, i0)
                    turned(f, fb)
                    c += ug + nd
                follow_used(c, nd, i0)

            def rotate(dst, src, cs, sn, heads, t):
                def b3(ap):
                    return ap[:, None, :].to_broadcast((P, heads, 32))
                a, b = src[:, :, 0:32], src[:, :, 32:64]
                t1 = sq[:, 0, 0:heads * 32].rearrange("p (h d) -> p h d", h=heads)
                t2 = sq[:, 0, 512:512 + heads * 32].rearrange("p (h d) -> p h d", h=heads)
                t3 = sq[:, 1, 0:heads * 32].rearrange("p (h d) -> p h d", h=heads)
                t4 = sq[:, 1, 512:512 + heads * 32].rearrange("p (h d) -> p h d", h=heads)
                link(V.tensor_tensor(t1, a, b3(cs), ALU.mult))
                link(V.tensor_tensor(t2, b, b3(sn), ALU.mult))
                link(V.tensor_tensor(t3, b, b3(cs), ALU.mult))
                link(V.tensor_tensor(t4, a, b3(sn), ALU.mult))
                link(V.tensor_tensor(dst[:, :, 0:32], t1, t2, ALU.subtract))
                link(V.tensor_tensor(dst[:, :, 32:64], t3, t4, ALU.add))

            dv.wait_ge(sem("rel_in"), 32)
            V.tensor_copy(relw[:, :, :], relb[:, :, None].to_broadcast((BUCKETS, NB2, P))).then_inc(sem("rel_w"), 1)
            for c in range(SPLIT):
                split_lo(c, 0)
            norm("mix0")
            for j in range(3):
                dv.sem_inc(sem("in_go"), 1)
            dv.wait_ge(sem("in_go"), 3)
            with dv.Fori(0, 2) as i:
                for j in range(3):
                    follow(U_IN + 4 * j, 4, i)
                    dv.wait_ge(sem("in_c"), 2 * j + 2 + 6 * i)
                    dv.sem_inc(sem("in_go"), 1)
            dv.wait_ge(sem("in_go"), 9)
            for t in range(NT):
                V.tensor_tensor(xn[:, t, :], act[:, t, D:2 * D], act[:, t, 2 * D:3 * D], ALU.mult).then_inc(sem("cv_v"), 1)
            V.memset(vp[:, :, 0:2], 0.0).then_inc(sem("cv_z"), 1)
            dv.wait_ge(sem("cols_in"), 16)
            for k in range(KD):
                dv.wait_ge(sem("cv_p"), k + 1)
                w = [col("conv", 8 * n + k) for n in range(3)]
                v = cv[:, k % 2, :]
                link(V.tensor_scalar(v, vp[:, k, 0:256], w[0], None, ALU.mult))
                link(V.scalar_tensor_tensor(out=v, in0=vp[:, k, 1:257], scalar=w[1], in1=v, op0=ALU.mult, op1=ALU.add))
                link(V.scalar_tensor_tensor(out=v, in0=vp[:, k, 2:258], scalar=w[2], in1=v, op0=ALU.mult, op1=ALU.add))
                dv.wait_ge(sem("cv_T"), KD + bank_end(k, KD))
                V.tensor_tensor(cy[:, k % 2, :], v, bank[4 + k // 2][:, (k % 2) * 256:(k % 2 + 1) * 256], ALU.mult)\
                 .then_inc(sem("cv_y"), 1)
                dv.wait_ge(sem("cv_hi"), k + 1)
                V.tensor_tensor(xtl[:, k, :], cy[:, k % 2, :], f32(xth[:, k, :]), ALU.subtract).then_inc(sem("cv_l"), 1)
            residual(U_OUT, "out_r")

            def add_sums(tag):
                for t in range(NT):
                    V.tensor_tensor(x[:, t, :].rearrange("p (n c) -> p n c", n=2)[:, 0, :], x[:, t, 0:WIDE], bank[4 + 2 * t][:, :],
                                    ALU.add).then_inc(sem(tag), 1)
                    V.tensor_tensor(x[:, t, WIDE:D], x[:, t, WIDE:D], bank[5 + 2 * t][:, :], ALU.add).then_inc(sem(tag), 1)

            norm("ffn0")
            ffn("f1", U_FF1, FF1 // FG, 2, 4, FG, 2, 0)
            add_sums("f1_r")

            dv.wait_ge(sem("pos_in"), 16)
            dv.wait_ge(sem("fixed_in"), 16)
            dv.wait_ge(sem("rows_in"), 16)
            link(V.tensor_copy(posf[:, :], posi[:, :]))
            ang = sq[:, 0, 0:64].rearrange("p (t n) -> p t n", t=NT)
            for t in range(NT):
                link(V.tensor_scalar(ang[:, t, :], fixed[:, FIXED["freq"]:FIXED["freq"] + 32], posf[:, t:t + 1], None, ALU.mult))
            for w, quarter in ((0, 0.25), (1, 0.0)):
                turns = sq[:, 0, 64 + 64 * w:128 + 64 * w].rearrange("p (t n) -> p t n", t=NT)
                link(V.tensor_scalar(turns, ang, 1.0 / TWO_PI, quarter, ALU.mult, ALU.add))
                link(V.tensor_scalar(turns, turns, ROUNDER, None, ALU.add))
                link(V.tensor_scalar(turns, turns, ROUNDER, None, ALU.subtract))
                r = trig[:, w, :, :]
                link(V.scalar_tensor_tensor(out=r, in0=turns, scalar=-PI_A, in1=ang, op0=ALU.mult, op1=ALU.add))
                link(V.scalar_tensor_tensor(out=r, in0=turns, scalar=-PI_B, in1=r, op0=ALU.mult, op1=ALU.add))
                link(V.scalar_tensor_tensor(out=r, in0=turns, scalar=-PI_C, in1=r, op0=ALU.mult, op1=ALU.add))
                link(V.tensor_scalar(r, r, quarter * TWO_PI, PI_IN, ALU.add, ALU.min))
                if w == 0:
                    link(V.tensor_scalar(r, r, -PI_IN, None, ALU.max))
                else:
                    V.tensor_scalar(r, r, -PI_IN, None, ALU.max).then_inc(sem("ang"), 1)
            norm("mix1")
            follow(U_DOWN, 6, 0)
            dv.wait_ge(sem("lora_rs"), 1)
            for t in range(NT):
                V.tensor_scalar(xn[:, t, 0:QR], down[:, t, 0:QR], rs[:, t:t + 1], None, ALU.mult).then_inc(sem("lora_xn"), 1)
                V.tensor_scalar(xn[:, t, QR:QR + KVR], down[:, t, QR:QR + KVR], rs[:, NT + t:NT + t + 1], None, ALU.mult)\
                 .then_inc(sem("lora_xn"), 1)
            dv.wait_ge(sem("trig"), 1)
            krs = down[:, :, 640:704]
            link(V.tensor_tensor(sq[:, 0, 0:128].rearrange("p (t d) -> p t d", t=NT), krs, krs, ALU.mult))
            link(V.tensor_reduce(ss[:, 32:34], sq[:, 0, 0:128].rearrange("p (t d) -> p t d", t=NT), AX.X, ALU.add))
            link(V.tensor_tensor(krs, krs, rows[:, None, ROWS["kr"]:ROWS["kr"] + 64].to_broadcast((P, NT, 64)), ALU.mult))
            for t in range(NT):
                rotate(kr1[:, t:t + 1, :], down[:, t:t + 1, 640:704], trig[:, 0, t, :], trig[:, 1, t, :], 1, t)
            dv.sem_inc(sem("kr1"), 1)
            for k in range(5):
                dv.wait_ge(sem("lora_hi"), bank_end(k, 5))
                V.scalar_tensor_tensor(out=xtl[:, k, :], in0=bank[4 + k // 2][:, (k % 2) * 256:(k % 2 + 1) * 256],
                                       scalar=col("qa", k) if k < 3 else col("kva", k - 3), in1=f32(xth[:, k, :]),
                                       op0=ALU.mult, op1=ALU.subtract).then_inc(sem("lora_l"), 1)
            follow(U_UQ, 10, 0)
            for t in range(NT):
                dv.wait_ge(sem("q_sq"), t + 1)
                V.tensor_reduce(ss[:, 8 * t:8 * t + 8], sq[:, t, :].rearrange("p (h d) -> p h d", h=NH), AX.X, ALU.add)\
                 .then_inc(sem("q_sr"), 1)
            for t in range(NT):
                dv.wait_ge(sem("k_sq"), t + 1)
                link(V.tensor_reduce(ss[:, 16 + 8 * t:24 + 8 * t], sq[:, t, 0:1024].rearrange("p (h d) -> p h d", h=NH),
                                     AX.X, ALU.add))
            link(V.tensor_scalar(ss[:, 16:24], ss[:, 16:24], ss[:, 32:33], None, ALU.add))
            V.tensor_scalar(ss[:, 24:32], ss[:, 24:32], ss[:, 33:34], None, ALU.add).then_inc(sem("qk_ss"), 1)
            dv.wait_ge(sem("qk_rs"), 1)
            for t in range(NT):
                link(V.tensor_tensor(qv[:, t, :, :], qv[:, t, :, :], rs[:, 8 * t:8 * t + 8, None].to_broadcast((P, NH, QH)), ALU.mult))
            for t in range(NT):
                link(V.tensor_tensor(qv[:, t, :, NOPE:QH], qv[:, t, :, NOPE:QH],
                                     rows[:, None, ROWS["qr"]:ROWS["qr"] + 64].to_broadcast((P, NH, 64)), ALU.mult))
                rotate(qrb[:, t, :, :], qv[:, t, :, NOPE:QH], trig[:, 0, t, :], trig[:, 1, t, :], NH, t)
            dv.sem_inc(sem("q_ready"), 1)
            for t in range(NT):
                rk = rs[:, 16 + 8 * t:24 + 8 * t, None]
                link(V.tensor_tensor(kvv[:, t, :, 0:NOPE], kvv[:, t, :, 0:NOPE], rk.to_broadcast((P, NH, NOPE)), ALU.mult))
                link(V.tensor_tensor(krb[:, t, :, :], kr1[:, t:t + 1, :].to_broadcast((P, NH, 64)), rk.to_broadcast((P, NH, 64)),
                                     ALU.mult))
            dv.sem_inc(sem("k_ready"), 1)
            for n in range(1, 12, 2):
                dv.wait_ge(sem("qk_T"), n + 1)
                if n < 8:
                    V.tensor_scalar(wide[:, n * WIDE:(n + 1) * WIDE], bank[n % 8][:, :], col("qn" if n < 4 else "kn"), None,
                                    ALU.mult).then_inc(sem("qkT_d"), 1)
                else:
                    V.tensor_copy(wide[:, n * WIDE:(n + 1) * WIDE], bank[n % 8][:, :]).then_inc(sem("qkT_d"), 1)
            for s in range(NH + 2):
                if s < NH:
                    h = s
                    dv.wait_ge(sem("m_S"), h + 1)
                    if h >= 2:
                        dv.wait_ge(sem("m_PT"), h - 1)
                    b = h % 2
                    V.scalar_tensor_tensor(out=ebuf[:, b, 0:384], in0=bank[b][:, 0:384], scalar=QH ** -0.5, in1=maskt,
                                           op0=ALU.mult, op1=ALU.add).then_inc(sem("m_sc"), 1)
                    dv.wait_ge(sem("m_sc"), h + 1)
                    link(V.tensor_reduce(small[:, 68 + 0:68 + 1], ebuf[:, b, 0:P], AX.X, ALU.max))
                    link(V.tensor_reduce(small[:, 68 + 1:68 + 2], ebuf[:, b, P:384], AX.X, ALU.max))
                    V.tensor_scalar(small[:, 64 + 2 * b:66 + 2 * b], small[:, 68:70], -1.0, None, ALU.mult).then_inc(sem("m_nm"), 1)
                if 1 <= s <= NH:
                    h = s - 1
                    b = h % 2
                    dv.wait_ge(sem("m_e"), 2 * h + 2)
                    link(V.reciprocal(small[:, 76:78], small[:, 72 + 2 * b:74 + 2 * b]))
                    link(V.tensor_scalar(ebuf[:, b, 0:P], ebuf[:, b, 0:P], small[:, 76:77], None, ALU.mult))
                    V.tensor_scalar(ebuf[:, b, P:384], ebuf[:, b, P:384], small[:, 77:78], None, ALU.mult).then_inc(sem("m_p"), 1)
                if s >= 2:
                    h = s - 2
                    dv.wait_ge(sem("m_oh"), h + 1)
                    V.tensor_tensor(xtl[:, h, :], bank[4 + h % 2][:, 0:256], f32(xth[:, h, :]), ALU.subtract).then_inc(sem("m_ol"), 1)
            residual(U_WO, "wo_r")

            dv.wait_ge(sem("rt_h"), 1)
            V.tensor_tensor(rtl[:, :], cols[:, COLS["router"]:COLS["router"] + 64], f32(rth[:, :]), ALU.subtract).then_inc(sem("rt_l"), 1)
            norm("ffn1")
            for t in range(NT):
                lg = small[:, 32 * t:32 * t + NE]
                mx = small[:, 32 * t + 16:32 * t + 24]
                fi = small[:, 32 * t + 24:32 * t + 32]
                dv.wait_ge(sem("rt_S"), t + 1)
                V.tensor_copy(lg, bank[t][:, 0:NE]).then_inc(sem("rt_c"), 1)
                dv.wait_ge(sem("rt_c"), t + 1)
                link(V.tensor_reduce(small[:, 32 * t + 10:32 * t + 11], lg, AX.X, ALU.max))
                V.tensor_scalar(small[:, 32 * t + 8:32 * t + 9], small[:, 32 * t + 10:32 * t + 11], -1.0, None, ALU.mult)\
                 .then_inc(sem("rt_m"), 1)
                dv.wait_ge(sem("rt_e"), t + 1)
                link(V.reciprocal(small[:, 32 * t + 11:32 * t + 12], small[:, 32 * t + 9:32 * t + 10]))
                link(V.tensor_scalar(lg, lg, small[:, 32 * t + 11:32 * t + 12], None, ALU.mult))
                link(V.max(mx, lg))
                link(V.max_index(topi[:, t, :], mx, lg))
                link(V.tensor_copy(fi, topi[:, t, :]))
                link(V.tensor_tensor(small[:, 32 * t + 12:32 * t + 13], mx[:, 0:1], mx[:, 1:2], ALU.add))
                link(V.reciprocal(small[:, 32 * t + 13:32 * t + 14], small[:, 32 * t + 12:32 * t + 13]))
                link(V.tensor_scalar(mx[:, 0:2], mx[:, 0:2], small[:, 32 * t + 13:32 * t + 14], None, ALU.mult))
                io = fixed[:, FIXED["iota"]:FIXED["iota"] + 8]
                link(V.tensor_scalar(lg, io, fi[:, 0:1], mx[:, 0:1], ALU.is_equal, ALU.mult))
                link(V.tensor_scalar(gates[:, t, :], io, fi[:, 1:2], mx[:, 1:2], ALU.is_equal, ALU.mult))
                link(V.tensor_tensor(gates[:, t, :], gates[:, t, :], lg, ALU.add))
            for j in range(4):
                dv.sem_inc(sem("moe_go"), 1)
            dv.wait_ge(sem("moe_go"), 4)
            with dv.Fori(0, NE) as e:
                ffn("fe", U_MOE, FFE // FG, 2, 3, FG, 2, e * 4, e)
                for t in range(NT):
                    gate = gates[:, t, bass.ds(e, 1)]
                    for n in range(2):
                        V.scalar_tensor_tensor(out=x[:, t, n * WIDE:(n + 1) * WIDE], in0=bank[4 + 2 * t + n][:, :], scalar=gate,
                                               in1=x[:, t, n * WIDE:(n + 1) * WIDE], op0=ALU.mult, op1=ALU.add)\
                         .then_inc(sem("moe_go"), 1)
            for n in range(2):
                a, b = ROWS[("lq1", "lq2")[n]], ROWS[("lk1", "lk2")[n]]
                link(V.tensor_tensor(small[:, 0:64], rows[:, a:a + 64], rows[:, b:b + 64], ALU.mult))
                V.tensor_reduce(lam[:, n:n + 1], small[:, 0:64], AX.X, ALU.add).then_inc(sem("lam_s"), 1)
                dv.wait_ge(sem("lam_s"), n + 1)
            V.tensor_scalar(lam[:, 5:6], col("sub"), 1.0 - LAMBDA0, None, ALU.mult).then_inc(sem("sub_g"), 1)
            norm("attn2")
            follow(U_IN2, 18, 0)
            dv.wait_ge(sem("in2_c"), 10)
            for t in range(NT):
                link(V.tensor_tensor(xn[:, t, 0:640], act[:, t, 0:640], act[:, t, 0:640], ALU.mult))
                link(V.tensor_reduce(ss[:, 26 * t:26 * t + 10], xn[:, t, 0:640].rearrange("p (h d) -> p h d", d=HD), AX.X, ALU.add))
                link(V.tensor_tensor(xn[:, t, :], act[:, t, 768:1792], act[:, t, 768:1792], ALU.mult))
                r = V.tensor_reduce(ss[:, 26 * t + 10:26 * t + 26], xn[:, t, :].rearrange("p (h d) -> p h d", d=HD), AX.X, ALU.add)
                if t == 0:
                    link(r)
                else:
                    r.then_inc(sem("h2_ss"), 1)
            dv.wait_ge(sem("h2_rs"), 1)
            for t in range(NT):
                qa = act[:, t, 0:512].rearrange("p (h d) -> p h d", d=HD)
                ka = act[:, t, 512:640].rearrange("p (h d) -> p h d", d=HD)
                both = act[:, t, 0:640].rearrange("p (h d) -> p h d", d=HD)
                link(V.tensor_tensor(both, both, rs[:, 26 * t:26 * t + 10, None].to_broadcast((P, 10, HD)), ALU.mult))
                link(V.tensor_tensor(qa, qa, rows[:, None, ROWS["aq"]:ROWS["aq"] + 64].to_broadcast((P, 8, HD)), ALU.mult))
                link(V.tensor_tensor(ka, ka, rows[:, None, ROWS["ak"]:ROWS["ak"] + 64].to_broadcast((P, 2, HD)), ALU.mult))
                C = fixed[:, FIXED["ctab"] + 64 * t:FIXED["ctab"] + 64 * (t + 1)]
                S = fixed[:, FIXED["stab"] + 64 * t:FIXED["stab"] + 64 * (t + 1)]
                sw = wide[:, 0:640].rearrange("p (h d) -> p h d", d=HD)
                for j in range(4):
                    o = (1, 0, 3, 2)[j]
                    link(V.tensor_tensor(sw[:, :, 16 * j:16 * j + 16], both[:, :, 16 * o:16 * o + 16],
                                         S[:, None, 16 * j:16 * j + 16].to_broadcast((P, 10, 16)), ALU.mult))
                link(V.tensor_tensor(both, both, C[:, None, :].to_broadcast((P, 10, HD)), ALU.mult))
                link(V.tensor_tensor(xn[:, t, 0:512].rearrange("p (j s d) -> p s j d", s=2, d=HD),
                                     act[:, t, 0:512].rearrange("p (s j d) -> p s j d", s=2, d=HD),
                                     wide[:, 0:512].rearrange("p (s j d) -> p s j d", s=2, d=HD), ALU.add))
                link(V.tensor_tensor(xn[:, t, 512:640].rearrange("p (h d) -> p h d", d=HD), ka, sw[:, 8:10, :], ALU.add))
            dv.sem_inc(sem("a_ready"), 1)
            for t in range(NT):
                qk = act[:, t, 768:1792].rearrange("p (h d) -> p h d", d=HD)
                link(V.tensor_tensor(qk, qk, rs[:, 26 * t + 10:26 * t + 26, None].to_broadcast((P, 16, HD)), ALU.mult))
            dv.sem_inc(sem("b_ready"), 1)
            dv.wait_ge(sem("lam_e"), 1)
            link(V.tensor_tensor(lam[:, 4:5], lam[:, 3:4], lam[:, 2:3], ALU.subtract))
            link(V.tensor_scalar(lam[:, 4:5], lam[:, 4:5], LAMBDA0, None, ALU.subtract))
            for s in range(NH + 2):
                if s < NH:
                    h = s
                    b = h % 2
                    dv.wait_ge(sem("a_S"), h + 1)
                    if h >= 1:
                        dv.wait_ge(sem("a_nm"), h)
                    V.tensor_reduce(small[:, 68:70], bank[b][:, :].rearrange("p (q n) -> p q n", q=2), AX.X, ALU.max)\
                     .then_inc(sem("a_mx"), 1)
                    dv.wait_ge(sem("a_mx"), h + 1)
                    V.tensor_scalar(small[:, 64 + 2 * b:66 + 2 * b], small[:, 68:70], -(HD ** -0.5), None, ALU.mult)\
                     .then_inc(sem("a_nm"), 1)
                if 1 <= s <= NH:
                    h = s - 1
                    b = h % 2
                    dv.wait_ge(sem("a_e"), 2 * h + 2)
                    if h >= 1:
                        dv.wait_ge(sem("a_p"), h)
                    V.reciprocal(small[:, 76:78], small[:, 72 + 2 * b:74 + 2 * b]).then_inc(sem("a_sc"), 1)
                    dv.wait_ge(sem("a_sc"), h + 1)
                    link(V.tensor_scalar(ebuf[:, b, 0:256], ebuf[:, b, 0:256], small[:, 76:77], None, ALU.mult))
                    V.tensor_scalar(ebuf[:, b, 256:512], ebuf[:, b, 256:512], small[:, 77:78], None, ALU.mult).then_inc(sem("a_p"), 1)
                if s >= 2 and s % 2 == 1:
                    j = (s - 2) // 2
                    dv.wait_ge(sem("a_oh"), j + 1)
                    V.tensor_tensor(xtl[:, j, :], bank[4 + j % 2][:, 0:256], f32(xth[:, j, :]), ALU.subtract).then_inc(sem("a_ol"), 1)
            dv.wait_ge(sem("bias_in"), 16 * 8)
            for s in range(NB2 + 1):
                if s < NB2:
                    h = s
                    for c in range(2):
                        dv.wait_ge(sem("b_S"), 2 * h + c + 1)
                        m = 4 * (h % 2) + 2 * c
                        e = act[:, h % 2, 2304 + c * 512:2304 + (c + 1) * 512]
                        V.scalar_tensor_tensor(out=e, in0=bank[2 * (h % 2) + c][:, :], scalar=HD ** -0.5,
                                               in1=bias2[:, h, :, :].rearrange("p q n -> p (q n)"), op0=ALU.mult, op1=ALU.add)\
                         .then_inc(sem("b_sc"), 1)
                        dv.wait_ge(sem("b_sc"), 2 * h + c + 1)
                        if h + c >= 1:
                            dv.wait_ge(sem("b_nm"), 2 * h + c)
                        link(V.tensor_reduce(small[:, 68:70], e.rearrange("p (q n) -> p q n", q=2), AX.X, ALU.max))
                        V.tensor_scalar(small[:, 80 + m:82 + m], small[:, 68:70], -1.0, None, ALU.mult).then_inc(sem("b_nm"), 1)
                if s >= 1:
                    h = s - 1
                    m = 4 * (h % 2)
                    dv.wait_ge(sem("b_e"), 4 * h + 4)
                    if h >= 1:
                        dv.wait_ge(sem("b_p"), h)
                    link(V.reciprocal(small[:, 112:116], small[:, 96 + m:100 + m]))
                    link(V.tensor_scalar(small[:, 114:116], small[:, 114:116], lam[:, 4:5], None, ALU.mult))
                    if h >= 1:
                        dv.wait_ge(sem("b_PT"), h)
                    for qb in range(2):
                        a = act[:, h % 2, 2304 + qb * 256:2304 + (qb + 1) * 256]
                        b = act[:, h % 2, 2816 + qb * 256:2816 + (qb + 1) * 256]
                        link(V.tensor_scalar(a, a, small[:, 112 + qb:113 + qb], None, ALU.mult))
                        r = V.scalar_tensor_tensor(out=hbuf[:, 0, qb * 256:(qb + 1) * 256], in0=b,
                                                   scalar=small[:, 114 + qb:115 + qb], in1=a, op0=ALU.mult, op1=ALU.add)
                        if qb == 0:
                            link(r)
                        else:
                            r.then_inc(sem("b_p"), 1)
                    dv.wait_ge(sem("ob_rs"), h + 1)
                    for t in range(NT):
                        V.tensor_scalar(xn[:, t, h * P:(h + 1) * P], bank[6 + h % 2][:, t * P:(t + 1) * P],
                                        rs[:, 2 * h + t:2 * h + t + 1], None, ALU.mult).then_inc(sem("ob_c"), 1)
            for h in range(NB2):
                dv.wait_ge(sem("ob_h"), bank_end(h, NB2))
                V.scalar_tensor_tensor(out=xtl[:, 4 + h, :], in0=bank[4 + h // 2][:, (h % 2) * 256:(h % 2 + 1) * 256],
                                       scalar=lam[:, 5:6], in1=f32(xth[:, 4 + h, :]), op0=ALU.mult, op1=ALU.subtract)\
                 .then_inc(sem("ob_l"), 1)
            residual(U_OUT2, "out2_r")

            norm("mlp2")
            ffn("f2", U_FF2, FF2 // FM, 3, 2, FM, 4, 0)
            add_sums("x_final")


def weight_stream(w):
    units = np.zeros((U_END + 2, P, UNIT), np.float32)

    def pairs(u, m):
        k, n = m.shape
        v = m.reshape(k // 256, 2, P, n // WIDE, WIDE).transpose(3, 0, 2, 1, 4)
        units[u:u + k // 256 * (n // WIDE)] = v.reshape(-1, P, UNIT)

    def narrow(u, m):
        k, n = m.shape
        units[u:u + k // 512, :, 0:4 * n] = m.reshape(k // 512, 4, P, n).transpose(0, 2, 1, 3).reshape(k // 512, P, 4 * n)

    def gate_up_down(u, wg, wu, wd):
        nf = wg.shape[1] // FG
        g = np.stack([wg.reshape(4, 2, P, nf, FG), wu.reshape(4, 2, P, nf, FG)], 4)
        g = g.transpose(3, 0, 2, 1, 4, 5).reshape(nf, 4, P, UNIT)
        d = wd.reshape(nf, 2, P, D)
        interleave(u, g, d)

    def interleave(u, g, d):
        nf, ug, ud = g.shape[0], g.shape[1], d.shape[1]
        units[u:u + ug] = g[0]
        u += ug
        for f in range(1, nf):
            units[u:u + ug] = g[f]
            units[u + ug:u + ug + ud] = d[f - 1]
            u += ug + ud
        units[u:u + ud] = d[nf - 1]

    pairs(U_IN, w["conv_w_in"][0])
    pairs(U_OUT, w["conv_w_out"][0])
    gate_up_down(U_FF1, w["ffn_w_gate"][0], w["ffn_w_up"][0], w["ffn_w_down"][0])
    pairs(U_DOWN, w["mla_w_down"][0][:, :WIDE])
    narrow(U_DOWN + 4, w["mla_w_down"][0][:, WIDE:])
    for n in range(3):
        m = w["mla_w_uq"][0][:, n * WIDE:(n + 1) * WIDE]
        pairs(U_UQ + 2 * n, m[0:256])
        units[U_UQ + 2 * n + 1, :, 0:WIDE] = m[256:384]
    pairs(U_UKV, w["mla_w_ukv"][0])
    pairs(U_WO, w["mla_w_o"][0])
    for e in range(NE):
        gate_up_down(U_MOE + 48 * e, w["moe_w_gate"][0, e], w["moe_w_up"][0, e], w["moe_w_down"][0, e])
    pairs(U_IN2, w["w_in_2"][0][:, :2048])
    narrow(U_IN2 + 16, w["w_in_2"][0][:, 2048:])
    pairs(U_OUT2, w["w_out_2"][0])
    up = w["w_up_2"][0].reshape(4, 2, P, 8, FM).transpose(3, 0, 2, 1, 4).reshape(8, 4, P, UNIT)
    interleave(U_FF2, up, w["w_down_2"][0].reshape(8, 4, P, D))
    return units.reshape(-1, 2, P, UNIT).transpose(0, 2, 1, 3).reshape(-1, P, 2 * UNIT)


def shape_tables():
    f = np.zeros((P, NFIXED), np.float32)
    f[:, 0:P] = np.eye(P)
    causal = np.where(np.arange(P)[None, :] <= np.arange(P)[:, None], 0.0, -3.0e38)
    f[:, FIXED["mask"]:FIXED["mask"] + P] = causal
    f[:, FIXED["mask"] + 2 * P:FIXED["mask"] + 3 * P] = causal
    inv = 1.0 / (np.float32(10000.0) ** (np.arange(0, 32, 2, dtype=np.float32) / np.float32(32)))
    tok = np.arange(TOK)
    ar = (tok // 64).astype(np.float32)[:, None] * inv[None, :].astype(np.float32)
    ac = (tok % 64).astype(np.float32)[:, None] * inv[None, :].astype(np.float32)
    ct = np.concatenate([np.cos(ar), np.cos(ar), np.cos(ac), np.cos(ac)], 1)
    st = np.concatenate([-np.sin(ar), np.sin(ar), -np.sin(ac), np.sin(ac)], 1)
    f[:, FIXED["ctab"]:FIXED["ctab"] + 128] = ct.reshape(2, P, 64).transpose(1, 0, 2).reshape(P, 128)
    f[:, FIXED["stab"]:FIXED["stab"] + 128] = st.reshape(2, P, 64).transpose(1, 0, 2).reshape(P, 128)
    f[:, FIXED["freq"]:FIXED["freq"] + 32] = np.float32(10000.0) ** (-np.arange(0, 64, 2, dtype=np.float32) / np.float32(64))
    f[:, FIXED["iota"]:FIXED["iota"] + 8] = np.arange(8)
    r = np.arange(-255, 257)
    n = np.abs(r)
    far = 8 + (np.log(np.maximum(n, 1).astype(np.float32) / np.float32(8)) / np.float32(np.log(16.0)) * np.float32(8)).astype(np.int32)
    bucket = (r > 0) * 16 + np.where(n < 8, n, np.minimum(far, 15))
    onehot = (np.arange(BUCKETS)[:, None] == bucket[None, :]).astype(np.float32)
    return f, onehot


def kernel(**inputs):
    import concourse.bacc as _bacc
    from concourse.bass_utils import run_bass_kernel_spmd as _run

    w = {k: np.asarray(v) for k, v in inputs.items()}

    def column(v):
        return v.reshape(-1, P).T

    two = lambda v: np.concatenate([v, v]).reshape(P, 1)
    cols = np.concatenate([
        column(w["norm_mix"][0]), column(w["norm_ffn"][0]), column(w["norm_mix"][1]), column(w["norm_ffn"][1]),
        column(w["attn_norm_g_2"][0]), column(w["mlp_norm_g_2"][0]), column(w["mla_q_a_norm"][0]),
        column(w["mla_kv_a_norm"][0]), column(w["mla_q_norm"][0][:NOPE]), column(w["mla_k_norm"][0][:NOPE]),
        column(w["conv_w"][0]), two(w["b_q_norm_g_2"][0]), two(w["b_k_norm_g_2"][0]), column(w["b_subln_g_2"][0]),
        w["moe_router"][0].reshape(KD, P, NE).transpose(1, 0, 2).reshape(P, KD * NE)], 1)
    rows = np.concatenate([
        w["mla_q_norm"][0][NOPE:], w["mla_k_norm"][0][NOPE:], w["a_q_norm_g_2"][0], w["a_k_norm_g_2"][0],
        w["lambda_q1_2"][0], w["lambda_k1_2"][0], w["lambda_q2_2"][0], w["lambda_k2_2"][0]]).reshape(1, NROWS)
    fixed, onehot = shape_tables()
    arrays = {
        "x_dram": w["x"][0], "pos_dram": w["positions"].reshape(NT, P).T, "weights_dram": weight_stream(w),
        "cols_dram": cols, "rows_dram": rows, "fixed_dram": fixed, "onehot_dram": onehot, "relb_dram": w["rel_bias_2"],
    }
    arrays = {k: np.ascontiguousarray(v) for k, v in arrays.items()}
    nc = _bacc.Bacc("TRN2", target_bir_lowering=False, num_devices=1)
    args = [nc.dram_tensor(k, v.shape, mybir.dt.from_np(v.dtype), kind="ExternalInput").ap() for k, v in arrays.items()]
    out = nc.dram_tensor("out_dram", (TOK, D), F32, kind="ExternalOutput").ap()
    build(nc, *args, out)
    r = _run(nc, [arrays], core_ids=[0])
    return r.results[0]["out_dram"].reshape(1, TOK, D)
```

```python
from contextlib import ExitStack

import numpy as np
import concourse.bass as bass
from concourse import mybir

F32 = mybir.dt.float32
F32R = mybir.dt.float32r
I32 = mybir.dt.int32
U32 = mybir.dt.uint32
ALU = mybir.AluOpType
ACT = mybir.ActivationFunctionType
AX = mybir.AxisListType

P = 128
D = 1024
TOK = 256
NT = TOK // P
KD = D // P
EPS = 1e-6
UNIT = 1024
WIDE = 512
RAW = 6
SPLIT = 6
ROUND = 2 * RAW

NH = 8
NOPE, ROPE, VD = 128, 64, 128
QH = NOPE + ROPE
QR, KVR = 384, 256
HD = 64
AQ, AKV, BQK, BV = 512, 128, 512, 512
IN2 = AQ + 2 * AKV + 2 * BQK + BV
NB2 = 4
BUCKETS = 32
LAMBDA0 = 0.8 - 0.6 * 1.0
FF1, FFE, FF2, NE = 2816, 2048, 4096, 8
FG = 256
CAP = P
FM = 512

U_IN = 0
U_OUT = U_IN + 24
U_FF1 = U_OUT + 8
U_DOWN = U_FF1 + 6 * (FF1 // FG)
U_UQ = U_DOWN + 6
U_UKV = U_UQ + 6
U_WO = U_UKV + 4
U_MOE = U_WO + 8
U_IN2 = U_MOE + NE * 6 * (FFE // FG)
U_OUT2 = U_IN2 + 18
U_FF2 = U_OUT2 + 8
U_END = U_FF2 + 8 * (FF2 // FM)
TOTAL = U_END + 2

DONE_FF1 = NT * (FF1 // FG)
DONE_MOE = DONE_FF1 + NE * (FFE // FG)

COLS = {}
_at = 0
for _name, _n in (("mix0", 8), ("ffn0", 8), ("mix1", 8), ("ffn1", 8), ("attn2", 8), ("mlp2", 8), ("qa", 3), ("kva", 2),
                  ("qn", 1), ("kn", 1), ("conv", 24), ("bq", 1), ("bk", 1), ("sub", 1), ("router", 64)):
    COLS[_name] = _at
    _at += _n
NCOLS = _at
ROWS = {}
_at = 0
for _name, _n in (("qr", 64), ("kr", 64), ("aq", 64), ("ak", 64), ("lq1", 64), ("lk1", 64), ("lq2", 64), ("lk2", 64)):
    ROWS[_name] = _at
    _at += _n
NROWS = _at
FIXED = {}
_at = 0
for _name, _n in (("ident", 128), ("mask", 384), ("ctab", 128), ("stab", 128), ("freq", 32), ("iota", 8),
                  ("before", 128), ("slots", 128), ("every", 128)):
    FIXED[_name] = _at
    _at += _n
NFIXED = _at

TWO_PI = 2.0 * np.pi
PI_A = 6.28125
PI_B = float(np.float32(np.round((TWO_PI - PI_A) * 2.0 ** 21) / 2.0 ** 21))
PI_C = float(TWO_PI - PI_A - PI_B)
ROUNDER = 1.5 * 2.0 ** 23
PI_IN = 3.1415925


def build(nc, x_in, pos_in, weights, cols_in, rows_in, fixed_in, onehot_in, relb_in, out):
    ctx = ExitStack()
    with ctx:
        def sb(name, shape, dt=F32):
            return ctx.enter_context(nc.sbuf_tensor(name, shape, dt))

        sems = {}

        def sem(name):
            if name not in sems:
                sems[name] = ctx.enter_context(nc.semaphore(name))
            return sems[name]

        raw = sb("raw", [P, RAW, 2 * UNIT])
        wh = sb("wh", [P, SPLIT, UNIT], F32R)
        wl = sb("wl", [P, SPLIT, UNIT], F32R)
        x = sb("x", [P, NT, D])
        xn = sb("xn", [P, NT, D])
        xth = sb("xth", [P, KD, TOK], F32R)
        xtl = sb("xtl", [P, KD, TOK], F32R)
        act = sb("act", [P, NT, 3584])
        wide = sb("wide", [P, 6144])
        hth = sb("hth", [P, 4, TOK], F32R)
        htl = sb("htl", [P, 4, TOK], F32R)
        ebuf = sb("ebuf", [P, NT, WIDE])
        hbuf = sb("hbuf", [P, NT, WIDE])
        cols = sb("cols", [P, NCOLS])
        rows = sb("rows", [P, NROWS])
        fixed = sb("fixed", [P, NFIXED])
        posi = sb("posi", [P, NT], I32)
        posf = sb("posf", [P, NT])
        relb = sb("relb", [BUCKETS, NB2])
        ss = sb("ss", [P, 64])
        rs = sb("rs", [P, 64])
        sst = sb("sst", [P, 64])
        trig = sb("trig", [P, 2, NT, 32])
        gates = sb("gates", [P, NT, NE + 1])
        chosen = sb("chosen", [P, NT, NE + 1])
        place = sb("place", [P, NT, NE + 1])
        queue = sb("queue", [P, 2 * NE + 8])
        order = sb("order", [P, 16], U32)
        sel = act[:, 1, 0:TOK].rearrange("p (t n) -> p t n", t=NT)
        ones = act[:, 1, TOK:TOK + P]
        selt = sb("selt", [P, TOK], F32R)
        rth = sb("rth", [P, KD * NE], F32R)
        rtl = sb("rtl", [P, KD * NE], F32R)
        small = sb("small", [P, 128])
        topi = sb("topi", [P, NT, 8], U32)
        lam = sb("lam", [P, 8])
        half = sb("half", [P, 64])
        bank = [ctx.enter_context(nc.psum_tensor(f"bank{i}", [P, WIDE], F32)) for i in range(8)]
        scratch = nc.dram_tensor("bias_scratch", (NB2 * P + 1, WIDE), F32).ap()

        ident = fixed[:, FIXED["ident"]:FIXED["ident"] + P]
        maskt = fixed[:, FIXED["mask"]:FIXED["mask"] + 384]
        onehot = ebuf[0:BUCKETS, 0, :]
        relw = ebuf[0:BUCKETS, 1, :].rearrange("p (h n) -> p h n", h=NB2)

        NORMS = ("mix0", "ffn0", "mix1", "ffn1", "attn2", "mlp2")

        def nth(tag):
            return NORMS.index(tag)

        raw_full = [sem(f"raw_full{i}") for i in range(RAW)]
        hi_done, lo_done, unit_used = sem("hi_done"), sem("lo_done"), sem("unit_used")

        def col(name, k=0):
            return cols[:, COLS[name] + k:COLS[name] + k + 1]

        def f32(ap):
            return ap.bitcast(F32)

        def bank_end(k, n):
            return min(k // 2 * 2 + 2, n)

        qv = act[:, :, 0:NH * QH].rearrange("p t (h d) -> p t h d", h=NH)
        kvv = act[:, :, NH * QH:NH * QH + NH * 256].rearrange("p t (h d) -> p t h d", h=NH)
        down = wide[:, 0:NT * 704].rearrange("p (t n) -> p t n", t=NT)
        sq = wide[:, 1408:1408 + NT * 1536].rearrange("p (t n) -> p t n", t=NT)
        kr1 = small[:, 0:128].rearrange("p (t n) -> p t n", t=NT)
        qrb = xn[:, :, 0:512].rearrange("p t (h d) -> p t h d", h=NH)
        krb = xn[:, :, 512:1024].rearrange("p t (h d) -> p t h d", h=NH)
        qnT = wide[:, 0:2048].rearrange("p (h n) -> p h n", h=NH)
        knT = wide[:, 2048:4096].rearrange("p (h n) -> p h n", h=NH)
        qrT = wide[:, 4096:5120].rearrange("p (h n) -> p h n", h=4)
        krT = wide[:, 5120:6144].rearrange("p (h n) -> p h n", h=4)
        hT2 = wide[:, 0:13 * TOK].rearrange("p (g n) -> p g n", g=13)
        bias2 = wide[:, 3328:3328 + NB2 * 2 * TOK].rearrange("p (h q n) -> p h q n", h=NB2, q=2)
        opanel = wide[:, :].rearrange("p (s n) -> p s n", s=3)
        oact = act[:, 0, :]
        osel = oact[:, 0:256].rearrange("p (t n) -> p t n", t=NT)
        oselt = oact[:, 256:512]
        oxt = oact[:, 512:1536].rearrange("p (k n) -> p k n", k=KD)
        oht = oact[:, 1536:1792].rearrange("p (j n) -> p j n", j=2)
        oy = oact[:, 1792:2816]
        vp = wide[:, 0:KD * 258].rearrange("p (k n) -> p k n", k=KD)
        cv = wide[:, 2064:2064 + 2 * 256].rearrange("p (b n) -> p b n", b=2)
        cy = wide[:, 2576:2576 + 2 * 256].rearrange("p (b n) -> p b n", b=2)

        block = ctx.enter_context(nc.Block())

        @block.sync
        def _(sp):
            sp.dma_start(x[:, :, :], x_in.rearrange("(t p) d -> p t d", p=P)).then_inc(sem("x_in"), 16)
            for p in range(RAW):
                sp.dma_start(raw[:, p, :], weights[p]).then_inc(raw_full[p], 16)
            panels = TOTAL // 2
            rounds = (panels - RAW) // RAW

            def load(p, i):
                sp.wait_ge(lo_done, 2 * (p - RAW) + 2 + i * ROUND)
                src = weights[p] if isinstance(i, int) else weights[bass.ds(i * RAW + p, 1)].rearrange("a p n -> (a p) n")
                sp.dma_start(raw[:, p % RAW, :], src).then_inc(raw_full[p % RAW], 16)

            with sp.Fori(0, rounds) as i:
                for p in range(RAW, 2 * RAW):
                    load(p, i)
            for p in range(RAW + rounds * RAW, panels):
                load(p, 0)
            sp.wait_ge(sem("order"), 1)
            sp.wait_ge(sem("moe_go"), 4 * NE + 4)
            passes = sp.value_load(order[0:1, 8:9], min_val=0, max_val=3)
            with sp.If(passes > 0):
                with sp.Fori(0, passes) as v:
                    e = sp.value_load(order[0:1, bass.ds(v, 1)], min_val=0, max_val=NE - 1)
                    sp.wait_ge(sem("o_sel"), v + 1)
                    first = U_MOE // 2 + e * 24
                    for f in range(8):
                        if f > 0:
                            sp.wait_ge(sem("o_gu"), v * 8 + f)
                        for q in range(2):
                            at = first + (3 * f - 1 if f else 0) + q
                            sp.dma_start(opanel[:, q, :], weights[bass.ds(at, 1)].rearrange("a p n -> (a p) n"))\
                              .then_inc(sem("o_up"), 16)
                        if f > 0:
                            sp.wait_ge(sem("o_d"), v * 8 + f)
                        at = first + (3 * f + 4 if f < 7 else 23)
                        sp.dma_start(opanel[:, 2, :], weights[bass.ds(at, 1)].rearrange("a p n -> (a p) n"))\
                          .then_inc(sem("o_down"), 16)
            sp.wait_ge(sem("x_final"), 4)
            sp.dma_start(out.rearrange("(t p) d -> p t d", p=P), x[:, :, :]).then_inc(sem("stored"), 16)
            sp.wait_ge(sem("stored"), 16)

        @block.gpsimd
        def _(pool):
            g = nc.gpsimd
            pool.dma_start(fixed[:, :], fixed_in).then_inc(sem("fixed_in"), 16)
            pool.dma_start(cols[:, :], cols_in).then_inc(sem("cols_in"), 16)
            pool.dma_start(rows[:, :], rows_in.to_broadcast((P, NROWS))).then_inc(sem("rows_in"), 16)
            pool.dma_start(posi[:, :], pos_in).then_inc(sem("pos_in"), 16)
            pool.dma_start(relb[:, :], relb_in).then_inc(sem("rel_in"), 16)
            pool.dma_start(onehot, onehot_in).then_inc(sem("rel_in"), 16)

            g.memset(half[:, :], -0.5).then_inc(sem("half"), 1)
            pool.wait_ge(sem("half"), 1)

            def rsqrt(tag, a, b, n):
                g.tensor_scalar(sst[:, a:b], ss[:, a:b], 1.0 / n, EPS, ALU.mult, ALU.add).then_inc(sem(tag + "_ms"), 1)

            def power(tag, a, b):
                pool.wait_ge(sem(tag + "_ms"), 1)
                g.tensor_tensor(rs[:, a:b], sst[:, a:b], half[:, 0:b - a], ALU.pow).then_inc(sem(tag + "_rs"), 1)

            def norm_rs(tag):
                pool.wait_ge(sem("norm_ss"), NT * (nth(tag) + 1))
                g.tensor_scalar(sst[:, 0:NT], ss[:, 0:NT], 1.0 / D, EPS, ALU.mult, ALU.add).then_inc(sem("norm_ms"), 1)
                pool.wait_ge(sem("norm_ms"), nth(tag) + 1)
                g.tensor_tensor(rs[:, 0:NT], sst[:, 0:NT], half[:, 0:NT], ALU.pow).then_inc(sem("norm_rs"), 1)

            norm_rs("mix0")
            pool.wait_ge(sem("cv_v"), 2)
            norm_rs("ffn0")
            norm_rs("mix1")
            pool.wait_ge(sem("lora_ss"), 2 * NT)
            g.tensor_scalar(sst[:, 0:NT], ss[:, 0:NT], 1.0 / QR, EPS, ALU.mult, ALU.add).then_inc(sem("lora_m1"), 1)
            g.tensor_scalar(sst[:, NT:2 * NT], ss[:, NT:2 * NT], 1.0 / KVR, EPS, ALU.mult, ALU.add).then_inc(sem("lora_m2"), 1)
            pool.wait_ge(sem("lora_m1"), 1)
            pool.wait_ge(sem("lora_m2"), 1)
            g.tensor_tensor(rs[:, 0:2 * NT], sst[:, 0:2 * NT], half[:, 0:2 * NT], ALU.pow).then_inc(sem("lora_rs"), 1)
            pool.wait_ge(sem("qk_ss"), 1)
            rsqrt("qk", 0, 32, QH)
            power("qk", 0, 32)
            norm_rs("ffn1")
            norm_rs("attn2")
            pool.wait_ge(sem("h2_ss"), 1)
            rsqrt("h2", 0, 52, HD)
            power("h2", 0, 52)
            for h in range(NB2):
                pool.wait_ge(sem("ob_ss"), 2 * h + 2)
                g.tensor_scalar(sst[:, 2 * h:2 * h + 2], ss[:, 2 * h:2 * h + 2], 1.0 / VD, EPS, ALU.mult, ALU.add)\
                 .then_inc(sem("ob_ms"), 1)
                pool.wait_ge(sem("ob_ms"), h + 1)
                g.tensor_tensor(rs[:, 2 * h:2 * h + 2], sst[:, 2 * h:2 * h + 2], half[:, 0:2], ALU.pow)\
                 .then_inc(sem("ob_rs"), 1)
            norm_rs("mlp2")

        @block.tensor
        def _(pe):
            mm = nc.tensor.matmul

            def mm3(o, lh, ll, wi, sl, start, stop):
                mm(o, lh, wh[:, wi, sl], start=start, stop=False)
                mm(o, lh, wl[:, wi, sl], start=False, stop=False)
                return mm(o, ll, wh[:, wi, sl], start=False, stop=stop)

            def xt(k, t):
                return xth[:, k, t * P:(t + 1) * P], xtl[:, k, t * P:(t + 1) * P]

            def product(c, i, ks, width, banks, k_first, k_last, k0=0, nt=NT):
                pe.wait_ge(lo_done, c + 1 + ROUND * i)
                for n, k in enumerate(ks):
                    for t in range(nt):
                        last = mm3(banks[t][:, 0:width], *xt(k0 + k, t), c % SPLIT, slice(n * width, (n + 1) * width),
                                   k == k_first, k == k_last)
                last.then_inc(unit_used, 1)

            def chunk512(c, i, banks):
                for u in range(4):
                    product(c + u, i, (2 * u, 2 * u + 1), WIDE, banks, 0, KD - 1)

            def turn_norm(tag):
                pe.wait_ge(sem("norm_xn"), NT * (nth(tag) + 1))
                for k in range(KD):
                    for t in range(NT):
                        last = nc.tensor.transpose(bank[4 + k // 2][:, (k % 2) * 256 + t * P:(k % 2) * 256 + (t + 1) * P],
                                                   xn[:, t, k * P:(k + 1) * P], ident)
                    last.then_inc(sem("norm_T"), 1)

            def ffn(tag, c0, nf, U, loops, width, nd, i0, f0=0, nt=NT, early=None, late=None, done=0):
                nj = width // P
                ug = 4

                def up(c, i):
                    for u in range(ug):
                        product(c + u, i, (2 * u, 2 * u + 1), WIDE, bank[0:2], 0, KD - 1, nt=nt)

                def turn(fc, fv):
                    for t in range(nt):
                        pe.wait_ge(sem(tag + "_h"), done + nt * fc + t + 1 + fv * nt)
                        for j in range(nj):
                            last = nc.tensor.transpose(bank[2 + t][:, j * P:(j + 1) * P], hbuf[:, t, j * P:(j + 1) * P], ident)
                        last.then_inc(sem(tag + "_hT"), 1)

                def down_(c, i, fc, fv, first, final):
                    pe.wait_ge(sem(tag + "_hTl"), done + nt * fc + nt + fv * nt)
                    for j in range(nd):
                        pe.wait_ge(lo_done, c + j + 1 + ROUND * i)
                        for t in range(nt):
                            for n in range(2):
                                last = mm3(bank[4 + 2 * t + n][:, :], hth[:, j, t * P:(t + 1) * P],
                                           htl[:, j, t * P:(t + 1) * P], (c + j) % SPLIT, slice(n * WIDE, (n + 1) * WIDE),
                                           first and j == 0, final and j == nd - 1)
                        last.then_inc(unit_used, 1)

                fb = nf * f0
                up(c0, i0)
                if early:
                    early()
                turn(0, fb)
                up(c0 + ug, i0)
                if late:
                    pe.wait_ge(sem("moe_selc"), f0 + 1)
                down_(c0 + 2 * ug, i0, 0, fb, True, False)
                turn(1, fb)
                c = c0 + 2 * ug + nd
                with pe.Fori(0, loops) as it:
                    ii = i0 + it * (U * (ug + nd) // ROUND)
                    for s in range(U):
                        up(c + s * (ug + nd), ii)
                        down_(c + s * (ug + nd) + ug, ii, 1 + s, fb + it * U, False, False)
                        turn(2 + s, fb + it * U)
                c += loops * U * (ug + nd)
                for f in range(2 + loops * U, nf):
                    up(c, i0)
                    down_(c + ug, i0, f - 1, fb, False, False)
                    turn(f, fb)
                    c += ug + nd
                if late:
                    late()
                down_(c, i0, nf - 1, fb, False, True)

            pe.wait_ge(sem("rel_w"), 1)
            pe.wait_ge(sem("rel_in"), 32)
            for h in range(NB2):
                mm(bank[h][:, :], relw[:, h, :], onehot, start=True, stop=True).then_inc(sem("rel_T"), 1)

            pe.wait_ge(sem("fixed_in"), 16)
            turn_norm("mix0")
            pe.wait_ge(sem("norm_l"), KD * (nth("mix0") + 1))
            pe.wait_ge(sem("rel_c"), NB2)
            with pe.Fori(0, 2) as i:
                for j in range(3):
                    if j == 0:
                        pass
                    pe.wait_ge(sem("in_go"), 3 * i + j + 1)
                    chunk512(U_IN + 4 * j, i, bank[2 * j:2 * j + 2])
            pe.wait_ge(sem("in_c"), 2 * 6)
            pe.wait_ge(sem("cv_v"), 2)
            for s, src in enumerate((xn, act)):
                for k in range(KD):
                    for t in range(NT):
                        last = nc.tensor.transpose(bank[4 * s + k // 2][:, (k % 2) * 256 + t * P:(k % 2) * 256 + (t + 1) * P],
                                                   src[:, t, k * P:(k + 1) * P], ident)
                    last.then_inc(sem("cv_T"), 1)
            pe.wait_ge(sem("cv_l"), KD)
            for n in range(2):
                chunk512(U_OUT + 4 * n, 0, bank[2 * n:2 * n + 2])

            turn_norm("ffn0")
            pe.wait_ge(sem("norm_l"), KD * (nth("ffn0") + 1))
            pe.wait_ge(sem("out_r"), 4)
            ffn("ff", U_FF1, FF1 // FG, 2, 4, FG, 2, 0)

            turn_norm("mix1")
            pe.wait_ge(sem("norm_l"), KD * (nth("mix1") + 1))
            pe.wait_ge(sem("f1_r"), 4)
            chunk512(U_DOWN, 0, bank[0:2])
            for u in range(2):
                product(U_DOWN + 4 + u, 0, range(4 * u, 4 * u + 4), 192, bank[2:4], 0, KD - 1)
            pe.wait_ge(sem("lora_xn"), 2 * NT)
            for k in range(5):
                for t in range(NT):
                    last = nc.tensor.transpose(bank[4 + k // 2][:, (k % 2) * 256 + t * P:(k % 2) * 256 + (t + 1) * P],
                                               xn[:, t, k * P:(k + 1) * P], ident)
                last.then_inc(sem("lora_T"), 1)
            pe.wait_ge(sem("lora_l"), 5)
            pe.wait_ge(sem("down_c"), 4)
            for n in range(7):
                if n >= 2:
                    pe.wait_ge(sem("quv_c"), 2 * (n - 1))
                b = bank[2 * (n % 2):2 * (n % 2) + 2]
                if n < 3:
                    product(U_UQ + 2 * n, 0, (0, 1), WIDE, b, 0, 2)
                    product(U_UQ + 2 * n + 1, 0, (2,), WIDE, b, 0, 2)
                else:
                    product(U_UKV + n - 3, 0, (0, 1), WIDE, b, 0, 1, k0=3)
            pe.wait_ge(sem("quv_c"), 14)
            for n in range(12):
                if n == 0:
                    pe.wait_ge(sem("q_ready"), 1)
                if n == 4:
                    pe.wait_ge(sem("k_ready"), 1)
                if n >= 8:
                    pe.wait_ge(sem("qkT_a"), (n - 8) // 2 + 1 if n % 2 == 0 else (n - 9) // 2 + 1)
                    pe.wait_ge(sem("qkT_d"), (n - 8 + 1) // 2 if n > 8 else 1)
                for m in range(2):
                    for t in range(NT):
                        if n < 4:
                            src = qv[:, t, 2 * n + m, 0:NOPE]
                        elif n < 8:
                            src = kvv[:, t, 2 * (n - 4) + m, 0:NOPE]
                        elif n < 10:
                            src = xn[:, t, (2 * (n - 8) + m) * P:(2 * (n - 8) + m + 1) * P]
                        else:
                            src = xn[:, t, 512 + (2 * (n - 10) + m) * P:512 + (2 * (n - 10) + m + 1) * P]
                        last = nc.tensor.transpose(bank[n % 8][:, m * 256 + t * P:m * 256 + (t + 1) * P], src, ident)
                last.then_inc(sem("qk_T"), 1)
            pe.wait_ge(sem("qkT_a"), 6)
            pe.wait_ge(sem("qkT_d"), 6)
            for s in range(NH + 2):
                if s < NH:
                    h = s
                    if h >= 2:
                        pe.wait_ge(sem("head_sc"), h - 1)
                    r0 = (h % 2) * 64
                    for qb, (a, n) in enumerate(((0, P), (P, 2 * P))):
                        o = bank[h % 2][:, a:a + n]
                        mm(o, qnT[:, h, qb * P:(qb + 1) * P], knT[:, h, 0:n], start=True, stop=False)
                        last = mm(o, qrT[r0:r0 + 64, h // 2, qb * P:(qb + 1) * P], krT[r0:r0 + 64, h // 2, 0:n],
                                  start=False, stop=True)
                    last.then_inc(sem("head_S"), 1)
                if 1 <= s <= NH:
                    h = s - 1
                    pe.wait_ge(sem("head_p"), h + 1)
                    if h >= 2:
                        pe.wait_ge(sem("head_pT"), h - 1)
                    for j in range(3):
                        last = nc.tensor.transpose(bank[2 + h % 2][:, j * P:(j + 1) * P], ebuf[:, h % 2, j * P:(j + 1) * P], ident)
                    last.then_inc(sem("head_PT"), 1)
                if s >= 2:
                    h = s - 2
                    pe.wait_ge(sem("head_pT"), h + 1)
                    if h >= 2:
                        pe.wait_ge(sem("head_ol"), h - 1)
                    mm(bank[4 + h % 2][:, 0:P], kvv[:, 0, h, NOPE:256], hbuf[:, h % 2, 0:P], start=True, stop=True)
                    mm(bank[4 + h % 2][:, P:256], kvv[:, 0, h, NOPE:256], hbuf[:, h % 2, P:256], start=True, stop=False)
                    mm(bank[4 + h % 2][:, P:256], kvv[:, 1, h, NOPE:256], hbuf[:, h % 2, 256:384], start=False, stop=True)\
                        .then_inc(sem("head_O"), 1)
            pe.wait_ge(sem("head_ol"), NH)
            for n in range(2):
                chunk512(U_WO + 4 * n, 0, bank[2 * n:2 * n + 2])

            turn_norm("ffn1")
            pe.wait_ge(sem("norm_l"), KD * (nth("ffn1") + 1))
            pe.wait_ge(sem("wo_r"), 4)
            pe.wait_ge(sem("rt_l"), 1)
            for t in range(NT):
                for k in range(KD):
                    h, l = xt(k, t)
                    o = bank[t][:, 0:NE]
                    mm(o, h, rth[:, k * NE:(k + 1) * NE], start=(k == 0), stop=False)
                    mm(o, h, rtl[:, k * NE:(k + 1) * NE], start=False, stop=False)
                    last = mm(o, l, rth[:, k * NE:(k + 1) * NE], start=False, stop=(k == KD - 1))
                last.then_inc(sem("rt_S"), 1)
            before = fixed[:, FIXED["before"]:FIXED["before"] + P]
            pe.wait_ge(sem("chosen"), NT)
            mm(bank[0][:, 0:NE], before, chosen[:, 0, 0:NE], start=True, stop=True)
            mm(bank[0][:, 16:16 + NE], before, chosen[:, 1, 0:NE], start=True, stop=False)
            mm(bank[0][:, 16:16 + NE], ones, chosen[:, 0, 0:NE], start=False, stop=True)
            mm(bank[0][:, 32:32 + NE], ones, chosen[:, 0, 0:NE], start=True, stop=False)
            mm(bank[0][:, 32:32 + NE], ones, chosen[:, 1, 0:NE], start=False, stop=True).then_inc(sem("places"), 1)

            def gather(tag, source, lot):
                pe.wait_ge(sem(tag + "_sel"), lot)
                for k in range(KD):
                    for t in range(NT):
                        last = mm(bank[6 + k // 4][:, (k % 4) * P:(k % 4 + 1) * P], xn[:, t, k * P:(k + 1) * P],
                                  source[:, t, :], start=(t == 0), stop=(t == NT - 1))
                    if k % 4 == 3:
                        last.then_inc(sem(tag + "_g"), 1)

            def turn_sel(e):
                pe.wait_ge(sem("moe_sel"), e + 1)
                for t in range(NT):
                    last = nc.tensor.transpose(bank[5][:, t * P:(t + 1) * P], sel[:, t, :], ident)
                last.then_inc(sem("moe_selT"), 1)

            def scatter(e):
                pe.wait_ge(sem("moe_yl"), e * 2 + 2)
                for t in range(NT):
                    for n in range(2):
                        o = bank[(1, 3, 6, 7)[2 * t + n]][:, :]
                        yh, yl = (v[:, 4 * n:4 * n + 4, P:TOK] for v in (xth, xtl))
                        mm(o, selt[:, t * P:(t + 1) * P], yh, start=True, stop=False)
                        mm(o, selt[:, t * P:(t + 1) * P], yl, start=False, stop=True).then_inc(sem("moe_S"), 1)

            def scatter_and_turn(e):
                scatter(e)
                turn_sel(e)

            def gather_next(e):
                pe.wait_ge(sem("moe_go"), e * 4 + 4)
                gather("moe", sel, e + 2)

            gather("moe", sel, 1)
            with pe.Fori(0, NE) as e:
                pe.wait_ge(sem("moe_gl"), e * KD + KD)
                ffn("ff", U_MOE, FFE // FG, 2, 3, FG, 2, e * 4, e, nt=1, done=DONE_FF1,
                    early=lambda: scatter_and_turn(e), late=lambda: gather_next(e))
            pe.wait_ge(sem("moe_gl"), NE * KD + KD)
            scatter(NE)

            pe.wait_ge(sem("order"), 1)
            pe.wait_ge(sem("moe_go"), 4 * NE + 4)
            passes = pe.value_load(order[0:1, 8:9], min_val=0, max_val=3)
            with pe.If(passes > 0):
                with pe.Fori(0, passes) as v:
                    gather("o", osel, v + 1)
                    for t in range(NT):
                        last = nc.tensor.transpose(bank[3][:, t * P:(t + 1) * P], osel[:, t, :], ident)
                    last.then_inc(sem("o_selT"), 1)
                    pe.wait_ge(sem("o_xt"), v * 2 + 2)
                    for f in range(8):
                        pe.wait_ge(sem("o_up"), v * 256 + 32 * (f + 1))
                        for k in range(KD):
                            last = mm(bank[0][:, :], oxt[:, k, :], opanel[:, k // 4, (k % 4) * WIDE:(k % 4 + 1) * WIDE],
                                      start=(k == 0), stop=(k == KD - 1))
                        last.then_inc(sem("o_gu"), 1)
                        pe.wait_ge(sem("o_h"), v * 8 + f + 1)
                        for j in range(2):
                            last = nc.tensor.transpose(bank[2][:, j * P:(j + 1) * P], hbuf[:, 0, j * P:(j + 1) * P], ident)
                        last.then_inc(sem("o_hT"), 1)
                        pe.wait_ge(sem("o_hc"), v * 8 + f + 1)
                        pe.wait_ge(sem("o_down"), v * 128 + 16 * (f + 1))
                        for j in range(2):
                            for n in range(2):
                                last = mm(bank[4 + n][:, :], oht[:, j, :],
                                          opanel[:, 2, j * D + n * WIDE:j * D + (n + 1) * WIDE],
                                          start=(f == 0 and j == 0), stop=(f == 7 and j == 1))
                        last.then_inc(sem("o_d"), 1)
                    pe.wait_ge(sem("o_y"), v * 2 + 2)
                    for t in range(NT):
                        for n in range(2):
                            mm(bank[(2, 3, 1, 4)[2 * t + n]][:, :], oselt[:, t * P:(t + 1) * P],
                               oy[:, n * WIDE:(n + 1) * WIDE], start=True, stop=True).then_inc(sem("o_S"), 1)
                    pe.wait_ge(sem("o_x"), v * 4 + 4)

            turn_norm("attn2")
            pe.wait_ge(sem("norm_l"), KD * (nth("attn2") + 1))
            pe.wait_ge(sem("moe_go"), 4 * NE + 4)
            for n in range(5):
                if n >= 2:
                    pe.wait_ge(sem("in2_c"), 2 * (n - 1))
                b = bank[2 * (n % 2):2 * (n % 2) + 2]
                if n < 4:
                    chunk512(U_IN2 + 4 * n, 0, b)
                else:
                    for u in range(2):
                        product(U_IN2 + 16 + u, 0, range(4 * u, 4 * u + 4), 256, b, 0, KD - 1)
            pe.wait_ge(sem("in2_c"), 10)
            for g in range(13):
                if g == 0:
                    pe.wait_ge(sem("a_ready"), 1)
                if g == 5:
                    pe.wait_ge(sem("b_ready"), 1)
                for t in range(NT):
                    if g < 5:
                        src = xn[:, t, g * P:(g + 1) * P]
                    else:
                        src = act[:, t, 768 + (g - 5) * P:768 + (g - 4) * P]
                    last = nc.tensor.transpose(bank[g // 2][:, (g % 2) * 256 + t * P:(g % 2) * 256 + (t + 1) * P], src, ident)
                last.then_inc(sem("h2_T"), 1)
            pe.wait_ge(sem("h2T_c"), 13)
            for s in range(NH + 2):
                if s < NH:
                    h = s
                    if h >= 2:
                        pe.wait_ge(sem("head_sc"), NH + h - 1)
                    r0 = (h // 4) * 64
                    for qb in range(2):
                        last = mm(bank[h % 2][:, qb * 256:(qb + 1) * 256], hT2[r0:r0 + 64, h % 4, qb * P:(qb + 1) * P],
                                  hT2[r0:r0 + 64, 4, :], start=True, stop=True)
                    last.then_inc(sem("head_S"), 1)
                if 1 <= s <= NH:
                    h = s - 1
                    pe.wait_ge(sem("head_p"), NH + h + 1)
                    if h >= 2:
                        pe.wait_ge(sem("head_pT"), NH + h - 1)
                    for kb in range(2):
                        for qb in range(2):
                            last = nc.tensor.transpose(bank[2 + h % 2][:, kb * 256 + qb * P:kb * 256 + (qb + 1) * P],
                                                       ebuf[:, h % 2, qb * 256 + kb * P:qb * 256 + (kb + 1) * P], ident)
                    last.then_inc(sem("head_PT"), 1)
                if s >= 2:
                    h = s - 2
                    pe.wait_ge(sem("head_pT"), NH + h + 1)
                    if h >= 4 and h % 2 == 0:
                        pe.wait_ge(sem("head_ol"), NH + h // 2 - 1)
                    r0 = (h % 2) * 64
                    v0 = 640 + (h // 4) * 64
                    for kb in range(2):
                        last = mm(bank[4 + (h // 2) % 2][r0:r0 + 64, 0:256], act[:, kb, v0:v0 + 64],
                                  hbuf[:, h % 2, kb * 256:(kb + 1) * 256], start=(kb == 0), stop=(kb == 1))
                    last.then_inc(sem("head_O"), 1)
            pe.wait_ge(sem("head_ol"), NH + 4)
            for s in range(NB2 + 1):
                if s < NB2:
                    h = s
                    for c in range(2):
                        if h >= 2:
                            pe.wait_ge(sem("b_sc"), 2 * (h - 2) + c + 1)
                        for qb in range(2):
                            last = mm(bank[2 * (h % 2) + c][:, qb * 256:(qb + 1) * 256],
                                      hT2[c * 64:c * 64 + 64, 5 + h, qb * P:(qb + 1) * P],
                                      hT2[c * 64:c * 64 + 64, 9 + h, :], start=True, stop=True)
                        last.then_inc(sem("b_S"), 1)
                if s >= 1:
                    h = s - 1
                    pe.wait_ge(sem("b_p"), h + 1)
                    if h >= 2:
                        pe.wait_ge(sem("b_pT"), h - 1)
                    for kb in range(2):
                        for qb in range(2):
                            last = nc.tensor.transpose(bank[4 + h % 2][:, kb * 256 + qb * P:kb * 256 + (qb + 1) * P],
                                                       hbuf[:, 0, qb * 256 + kb * P:qb * 256 + (kb + 1) * P], ident)
                    last.then_inc(sem("b_PT"), 1)
                    pe.wait_ge(sem("b_pT"), h + 1)
                    if h >= 2:
                        pe.wait_ge(sem("ob_c"), 2 * (h - 1))
                    for qb in range(2):
                        for kb in range(2):
                            last = mm(bank[6 + h % 2][:, qb * P:(qb + 1) * P],
                                      hbuf[:, 1, kb * 256 + qb * P:kb * 256 + (qb + 1) * P],
                                      act[:, kb, 1792 + h * P:1792 + (h + 1) * P], start=(kb == 0), stop=(kb == 1))
                    last.then_inc(sem("b_O"), 1)
            pe.wait_ge(sem("ob_c"), 2 * NB2)
            for h in range(NB2):
                for t in range(NT):
                    last = nc.tensor.transpose(bank[4 + h // 2][:, (h % 2) * 256 + t * P:(h % 2) * 256 + (t + 1) * P],
                                               xn[:, t, h * P:(h + 1) * P], ident)
                last.then_inc(sem("ob_T"), 1)
            pe.wait_ge(sem("ob_l"), NB2)
            for n in range(2):
                chunk512(U_OUT2 + 4 * n, 0, bank[2 * n:2 * n + 2])

            turn_norm("mlp2")
            pe.wait_ge(sem("norm_l"), KD * (nth("mlp2") + 1))
            pe.wait_ge(sem("out2_r"), 4)
            ffn("ff", U_FF2, FF2 // FM, 3, 2, FM, 4, 0, done=DONE_MOE)

        @block.scalar
        def _(sc):
            A = nc.scalar.activation

            def split_hi(c, i):
                sc.wait_ge(raw_full[(c // 2) % RAW], 16 * (c // ROUND + 1) + 16 * i)
                if c >= SPLIT:
                    sc.wait_ge(unit_used, c - SPLIT + 1 + ROUND * i)
                A(wh[:, c % SPLIT, :], raw[:, (c // 2) % RAW, (c % 2) * UNIT:(c % 2 + 1) * UNIT], ACT.Copy).then_inc(hi_done, 1)

            def follow(c, n, i):
                for u in range(c, c + n):
                    if u + SPLIT < TOTAL:
                        split_hi(u + SPLIT, i)
                    else:
                        sc.wait_ge(unit_used, u + 1 + ROUND * i)

            def followed(c, n, i, step):
                follow(c, n - 1, i)
                sc.wait_ge(unit_used, c + n + ROUND * i)
                step()
                follow(c + n - 1, 1, i)

            def norm(tag, ready, n):
                sc.wait_ge(sem(ready), n)
                for t in range(NT):
                    A(xn[:, t, :], x[:, t, :], ACT.Square, accum_out=ss[:, t:t + 1]).then_inc(sem("norm_ss"), 1)
                sc.wait_ge(sem("norm_rs"), nth(tag) + 1)
                A(xn[:, 1, :], x[:, 1, :], ACT.Copy, scale=rs[:, 1:2]).then_inc(sem("norm_xn"), 1)
                for k in range(KD):
                    sc.wait_ge(sem("norm_T"), KD * nth(tag) + bank_end(k, KD))
                    A(xth[:, k, :], bank[4 + k // 2][:, (k % 2) * 256:(k % 2 + 1) * 256], ACT.Copy, scale=col(tag, k))\
                        .then_inc(sem("norm_hi"), 1)

            def ffn(tag, c0, nf, U, loops, width, nd, i0, f0=0, nt=NT, early=None, late=None, done=0):
                nj = width // P
                ug = 4

                def evac(fc, fv):
                    for t in range(nt):
                        if nd == 2:
                            A(ebuf[:, t, 0:FG], bank[t][:, 0:FG], ACT.Tanh, scale=0.5).then_inc(sem(tag + "_e"), 1)
                        else:
                            A(ebuf[:, t, :], bank[t][:, :], ACT.Relu).then_inc(sem(tag + "_e"), 1)

                def turned(fc, fv):
                    for t in range(nt):
                        sc.wait_ge(sem(tag + "_hT"), done + nt * fc + t + 1 + fv * nt)
                        A(hth[:, 0:nj, t * P:(t + 1) * P], bank[2 + t][:, 0:width].rearrange("p (j n) -> p j n", j=nj),
                          ACT.Copy).then_inc(sem(tag + "_hTh"), 1)

                fb = nf * f0
                followed(c0, ug, i0, lambda: evac(0, fb))
                if early:
                    early()
                turned(0, fb)
                followed(c0 + ug, ug, i0, lambda: evac(1, fb))
                follow(c0 + 2 * ug, nd, i0)
                turned(1, fb)
                c = c0 + 2 * ug + nd
                with sc.Fori(0, loops) as it:
                    ii = i0 + it * (U * (ug + nd) // ROUND)
                    for s in range(U):
                        followed(c + s * (ug + nd), ug, ii, lambda: evac(2 + s, fb + it * U))
                        follow(c + s * (ug + nd) + ug, nd, ii)
                        turned(2 + s, fb + it * U)
                c += loops * U * (ug + nd)
                for f in range(2 + loops * U, nf):
                    followed(c, ug, i0, lambda: evac(f, fb))
                    follow(c + ug, nd, i0)
                    turned(f, fb)
                    c += ug + nd
                if late:
                    late[0]()
                    followed(c, nd, i0, late[1])
                else:
                    follow(c, nd, i0)

            for c in range(SPLIT):
                split_hi(c, 0)
            sc.wait_ge(sem("cols_in"), 16)
            norm("mix0", "x_in", 16)
            for h in range(NB2):
                sc.wait_ge(sem("rel_T"), h + 1)
                A(act[:, 0, h * WIDE:(h + 1) * WIDE], bank[h][:, :], ACT.Copy).then_inc(sem("rel_c"), 1)
            sc.wait_ge(sem("rel_c"), NB2)
            sc.dma_start(scratch[0:NB2 * P, :].rearrange("(h p) n -> p h n", p=P), act[:, 0, 0:NB2 * WIDE].rearrange("p (h n) -> p h n", h=NB2))\
              .then_inc(sem("rel_st"), 16)
            sc.wait_ge(sem("rel_st"), 16)
            with sc.Fori(0, 2) as i:
                for j in range(3):
                    follow(U_IN + 4 * j, 4, i)
                    for t in range(NT):
                        A(act[:, t, bass.ds(i * 1536 + j * WIDE, WIDE)], bank[2 * j + t][:, :], ACT.Copy).then_inc(sem("in_c"), 1)
            for k in range(KD):
                sc.wait_ge(sem("cv_T"), bank_end(k, KD))
                sc.wait_ge(sem("cv_z"), 1)
                A(vp[:, k, 2:258], bank[k // 2][:, (k % 2) * 256:(k % 2 + 1) * 256], ACT.Copy).then_inc(sem("cv_p"), 1)
            for k in range(KD):
                sc.wait_ge(sem("cv_y"), k + 1)
                A(xth[:, k, :], cy[:, k % 2, :], ACT.Copy).then_inc(sem("cv_hi"), 1)
            follow(U_OUT, 8, 0)

            norm("ffn0", "out_r", 4)
            ffn("ff", U_FF1, FF1 // FG, 2, 4, FG, 2, 0)

            norm("mix1", "f1_r", 4)
            sc.wait_ge(sem("ang"), 1)
            A(trig[:, :, :, :], trig[:, :, :, :], ACT.Sin).then_inc(sem("trig"), 1)
            follow(U_DOWN, 4, 0)
            for t in range(NT):
                A(down[:, t, 0:WIDE], bank[t][:, :], ACT.Copy).then_inc(sem("down_c"), 1)
            follow(U_DOWN + 4, 2, 0)
            for t in range(NT):
                A(down[:, t, WIDE:704], bank[2 + t][:, 0:192], ACT.Copy).then_inc(sem("down_c"), 1)
            sc.wait_ge(sem("down_c"), 4)
            for t in range(NT):
                A(xn[:, t, 0:QR], down[:, t, 0:QR], ACT.Square, accum_out=ss[:, t:t + 1]).then_inc(sem("lora_ss"), 1)
                A(xn[:, t, QR:QR + KVR], down[:, t, QR:QR + KVR], ACT.Square, accum_out=ss[:, NT + t:NT + t + 1])\
                    .then_inc(sem("lora_ss"), 1)
            for k in range(5):
                sc.wait_ge(sem("lora_T"), bank_end(k, 5))
                A(xth[:, k, :], bank[4 + k // 2][:, (k % 2) * 256:(k % 2 + 1) * 256], ACT.Copy,
                  scale=col("qa", k) if k < 3 else col("kva", k - 3)).then_inc(sem("lora_hi"), 1)
            for n in range(7):
                if n < 3:
                    follow(U_UQ + 2 * n, 2, 0)
                else:
                    follow(U_UKV + n - 3, 1, 0)
                for t in range(NT):
                    A(act[:, t, n * WIDE:(n + 1) * WIDE], bank[2 * (n % 2) + t][:, :], ACT.Copy).then_inc(sem("quv_c"), 1)
            sc.wait_ge(sem("quv_c"), 14)
            sc.wait_ge(sem("kr1"), 1)
            for t in range(NT):
                A(sq[:, t, :], act[:, t, 0:NH * QH], ACT.Square).then_inc(sem("q_sq"), 1)
            for t in range(NT):
                sc.wait_ge(sem("q_sr"), t + 1)
                A(sq[:, t, 0:1024].rearrange("p (h d) -> p h d", h=NH), kvv[:, t, :, 0:NOPE], ACT.Square).then_inc(sem("k_sq"), 1)
            for n in range(0, 12, 2):
                sc.wait_ge(sem("qk_T"), n + 1)
                g = {"scale": col("qn")} if n < 4 else {"scale": col("kn")} if n < 8 else {}
                A(wide[:, n * WIDE:(n + 1) * WIDE], bank[n % 8][:, :], ACT.Copy, **g).then_inc(sem("qkT_a"), 1)
            for s in range(NH + 2):
                if s < NH:
                    h = s
                    sc.wait_ge(sem("head_nm"), h + 1)
                    for qb, (a, n) in enumerate(((0, P), (P, 2 * P))):
                        A(ebuf[:, h % 2, a:a + n], ebuf[:, h % 2, a:a + n], ACT.Exp,
                          bias=small[:, 64 + 2 * (h % 2) + qb:65 + 2 * (h % 2) + qb],
                          accum_out=small[:, 72 + 2 * (h % 2) + qb:73 + 2 * (h % 2) + qb]).then_inc(sem("head_e"), 1)
                if 1 <= s <= NH:
                    h = s - 1
                    sc.wait_ge(sem("head_PT"), h + 1)
                    if h >= 2:
                        sc.wait_ge(sem("head_O"), h - 1)
                    A(hbuf[:, h % 2, 0:384], bank[2 + h % 2][:, 0:384], ACT.Copy).then_inc(sem("head_pT"), 1)
                if s >= 2:
                    h = s - 2
                    sc.wait_ge(sem("head_O"), h + 1)
                    A(xth[:, h, :], bank[4 + h % 2][:, 0:256], ACT.Copy).then_inc(sem("head_oh"), 1)
            follow(U_WO, 8, 0)

            A(rth[:, :], cols[:, COLS["router"]:COLS["router"] + 64], ACT.Copy).then_inc(sem("rt_h"), 1)
            norm("ffn1", "wo_r", 4)
            for t in range(NT):
                sc.wait_ge(sem("rt_m"), t + 1)
                A(small[:, 32 * t:32 * t + NE], small[:, 32 * t:32 * t + NE], ACT.Exp,
                  bias=small[:, 32 * t + 8:32 * t + 9], accum_out=small[:, 32 * t + 9:32 * t + 10]).then_inc(sem("rt_e"), 1)

            def gathered(lot):
                for k in range(KD):
                    if k % 4 == 0:
                        sc.wait_ge(sem("moe_g"), lot * 2 + k // 4 + 1)
                    A(xth[:, k, 0:P], bank[6 + k // 4][:, (k % 4) * P:(k % 4 + 1) * P], ACT.Copy, scale=col("ffn1", k))\
                        .then_inc(sem("moe_gh"), 1)

            def turned_sel(e):
                sc.wait_ge(sem("moe_selT"), e + 1)
                A(selt[:, :], bank[5][:, 0:TOK], ACT.Copy).then_inc(sem("moe_selc"), 1)

            def outputs():
                for n in range(2):
                    A(xth[:, 4 * n:4 * n + 4, P:TOK], bank[4 + n][:, :].rearrange("p (k n) -> p k n", k=4), ACT.Copy)\
                        .then_inc(sem("moe_yh"), 1)

            gathered(0)
            with sc.Fori(0, NE) as e:
                ffn("ff", U_MOE, FFE // FG, 2, 3, FG, 2, e * 4, e, nt=1, done=DONE_FF1, early=lambda: turned_sel(e),
                    late=(lambda: gathered(e + 1), outputs))

            sc.wait_ge(sem("order"), 1)
            sc.wait_ge(sem("moe_go"), 4 * NE + 4)
            passes = sc.value_load(order[0:1, 8:9], min_val=0, max_val=3)
            with sc.If(passes > 0):
                with sc.Fori(0, passes) as v:
                    for b in range(2):
                        sc.wait_ge(sem("o_g"), v * 2 + b + 1)
                        for k in range(4 * b, 4 * b + 4):
                            last = A(oxt[:, k, :], bank[6 + b][:, (k % 4) * P:(k % 4 + 1) * P], ACT.Copy, scale=col("ffn1", k))
                        last.then_inc(sem("o_xt"), 1)
                    sc.wait_ge(sem("o_selT"), v + 1)
                    A(oselt, bank[3][:, 0:TOK], ACT.Copy)
                    for f in range(8):
                        sc.wait_ge(sem("o_gu"), v * 8 + f + 1)
                        A(ebuf[:, 0, 0:FG], bank[0][:, 0:FG], ACT.Tanh, scale=0.5).then_inc(sem("o_e"), 1)
                        sc.wait_ge(sem("o_hT"), v * 8 + f + 1)
                        A(oht[:, :, :], bank[2][:, 0:FG].rearrange("p (j n) -> p j n", j=2), ACT.Copy).then_inc(sem("o_hc"), 1)
                    sc.wait_ge(sem("o_d"), v * 8 + 8)
                    for n in range(2):
                        A(oy[:, n * WIDE:(n + 1) * WIDE], bank[4 + n][:, :], ACT.Copy).then_inc(sem("o_y"), 1)

            norm("attn2", "moe_all", 1)
            for h in range(NB2):
                for qb in range(2):
                    at = h * P * WIDE + TOK - 1 - P * qb
                    src = scratch.rearrange("r n -> (r n)")[at:at + P * (WIDE - 1)]
                    sc.dma_start(bias2[:, h, qb, :], src.rearrange("(p n) -> p n", p=P)[:, 0:256]).then_inc(sem("bias_in"), 16)
            for n in range(5):
                w = WIDE if n < 4 else 256
                follow(U_IN2 + 4 * n, 4 if n < 4 else 2, 0)
                for t in range(NT):
                    A(act[:, t, n * WIDE:n * WIDE + w], bank[2 * (n % 2) + t][:, 0:w], ACT.Copy).then_inc(sem("in2_c"), 1)
            sc.wait_ge(sem("lam_s"), 2)
            A(lam[:, 2:4], lam[:, 0:2], ACT.Exp).then_inc(sem("lam_e"), 1)
            for g in range(13):
                sc.wait_ge(sem("h2_T"), bank_end(g, 13))
                gg = {} if g < 5 else {"scale": col("bq" if g < 9 else "bk")}
                A(hT2[:, g, :], bank[g // 2][:, (g % 2) * 256:(g % 2 + 1) * 256], ACT.Copy, **gg).then_inc(sem("h2T_c"), 1)
            for s in range(NH + 2):
                if s < NH:
                    h = s
                    sc.wait_ge(sem("head_nm"), NH + h + 1)
                    if h >= 2:
                        sc.wait_ge(sem("head_PT"), NH + h - 1)
                    for qb in range(2):
                        A(ebuf[:, h % 2, qb * 256:(qb + 1) * 256], bank[h % 2][:, qb * 256:(qb + 1) * 256], ACT.Exp,
                          scale=HD ** -0.5, bias=small[:, 64 + 2 * (h % 2) + qb:65 + 2 * (h % 2) + qb],
                          accum_out=small[:, 72 + 2 * (h % 2) + qb:73 + 2 * (h % 2) + qb]).then_inc(sem("head_e"), 1)
                if 1 <= s <= NH:
                    h = s - 1
                    sc.wait_ge(sem("head_PT"), NH + h + 1)
                    if h >= 2:
                        sc.wait_ge(sem("head_O"), NH + h - 1)
                    A(hbuf[:, h % 2, :], bank[2 + h % 2][:, :], ACT.Copy).then_inc(sem("head_pT"), 1)
                if s >= 2 and s % 2 == 1:
                    j = (s - 2) // 2
                    sc.wait_ge(sem("head_O"), NH + 2 * j + 2)
                    A(xth[:, j, :], bank[4 + j % 2][:, 0:256], ACT.Copy).then_inc(sem("head_oh"), 1)
            for s in range(NB2 + 1):
                if s < NB2:
                    h = s
                    for c in range(2):
                        sc.wait_ge(sem("b_nm"), 2 * h + c + 1)
                        for qb in range(2):
                            m = 4 * (h % 2) + 2 * c + qb
                            A(act[:, h % 2, 2304 + c * 512 + qb * 256:2304 + c * 512 + (qb + 1) * 256],
                              act[:, h % 2, 2304 + c * 512 + qb * 256:2304 + c * 512 + (qb + 1) * 256],
                              ACT.Exp, bias=small[:, 80 + m:81 + m], accum_out=small[:, 96 + m:97 + m]).then_inc(sem("b_e"), 1)
                if s >= 1:
                    h = s - 1
                    sc.wait_ge(sem("b_PT"), h + 1)
                    if h >= 1:
                        sc.wait_ge(sem("b_O"), h)
                    A(hbuf[:, 1, :], bank[4 + h % 2][:, :], ACT.Copy).then_inc(sem("b_pT"), 1)
                    sc.wait_ge(sem("b_O"), h + 1)
                    for t in range(NT):
                        A(xn[:, t, h * P:(h + 1) * P], bank[6 + h % 2][:, t * P:(t + 1) * P], ACT.Square,
                          accum_out=ss[:, 2 * h + t:2 * h + t + 1]).then_inc(sem("ob_ss"), 1)
            for h in range(NB2):
                sc.wait_ge(sem("ob_T"), bank_end(h, NB2))
                sc.wait_ge(sem("sub_g"), 1)
                A(xth[:, 4 + h, :], bank[4 + h // 2][:, (h % 2) * 256:(h % 2 + 1) * 256], ACT.Copy, scale=lam[:, 5:6])\
                    .then_inc(sem("ob_h"), 1)
            follow(U_OUT2, 8, 0)

            norm("mlp2", "out2_r", 4)
            ffn("ff", U_FF2, FF2 // FM, 3, 2, FM, 4, 0, done=DONE_MOE)

        @block.vector
        def _(dv):
            V = nc.vector
            chain = [0]
            dve_chain = sem("dve_chain")

            def link(ins):
                chain[0] += 1
                ins.then_inc(dve_chain, 1)
                dv.wait_ge(dve_chain, chain[0])

            def split_lo(c, i):
                dv.wait_ge(hi_done, c + 1 + ROUND * i)
                V.tensor_tensor(wl[:, c % SPLIT, :], raw[:, (c // 2) % RAW, (c % 2) * UNIT:(c % 2 + 1) * UNIT],
                                f32(wh[:, c % SPLIT, :]), ALU.subtract).then_inc(lo_done, 1)

            def follow(c, n, i):
                for u in range(c, c + n):
                    if u + SPLIT < TOTAL:
                        split_lo(u + SPLIT, i)
                    else:
                        dv.wait_ge(unit_used, u + 1 + ROUND * i)

            def followed(c, n, i, step):
                follow(c, n - 1, i)
                step()
                follow(c + n - 1, 1, i)

            def follow_used(c, n, i):
                follow(c, n, i)
                dv.wait_ge(unit_used, c + n + ROUND * i)

            def norm(tag):
                dv.wait_ge(sem("norm_rs"), nth(tag) + 1)
                V.tensor_scalar(xn[:, 0, :], x[:, 0, :], rs[:, 0:1], None, ALU.mult).then_inc(sem("norm_xn"), 1)
                for k in range(KD):
                    dv.wait_ge(sem("norm_hi"), KD * nth(tag) + bank_end(k, KD))
                    V.scalar_tensor_tensor(out=xtl[:, k, :], in0=bank[4 + k // 2][:, (k % 2) * 256:(k % 2 + 1) * 256],
                                           scalar=col(tag, k), in1=f32(xth[:, k, :]), op0=ALU.mult, op1=ALU.subtract)\
                     .then_inc(sem("norm_l"), 1)

            def residual(c0, tag):
                for n in range(2):
                    follow_used(c0 + 4 * n, 4, 0)
                    for t in range(NT):
                        V.tensor_tensor(x[:, t, n * WIDE:(n + 1) * WIDE], x[:, t, n * WIDE:(n + 1) * WIDE],
                                        bank[2 * n + t][:, :], ALU.add).then_inc(sem(tag), 1)

            def ffn(tag, c0, nf, U, loops, width, nd, i0, f0=0, nt=NT, early=None, late=None, done=0):
                nj = width // P
                ug = 4

                def evac(fc, fv):
                    for t in range(nt):
                        dv.wait_ge(sem(tag + "_e"), done + nt * fc + t + 1 + fv * nt)
                        if nd == 2:
                            step = sem(tag + "_s")
                            e, g, u, h = ebuf[:, t, 0:FG], bank[t][:, 0:FG], bank[t][:, FG:2 * FG], hbuf[:, t, 0:FG]
                            V.scalar_tensor_tensor(out=e, in0=e, scalar=1.0, in1=g, op0=ALU.add, op1=ALU.mult).then_inc(step, 1)
                            dv.wait_ge(step, done + nt * fc + t + 1 + fv * nt)
                            V.scalar_tensor_tensor(out=h, in0=e, scalar=0.5, in1=u, op0=ALU.mult, op1=ALU.mult)\
                             .then_inc(sem(tag + "_h"), 1)
                        else:
                            V.tensor_tensor(hbuf[:, t, :], ebuf[:, t, :], ebuf[:, t, :], ALU.mult).then_inc(sem(tag + "_h"), 1)

                def turned(fc, fv):
                    for t in range(nt):
                        dv.wait_ge(sem(tag + "_hTh"), done + nt * fc + t + 1 + fv * nt)
                        V.tensor_tensor(htl[:, 0:nj, t * P:(t + 1) * P], bank[2 + t][:, 0:width].rearrange("p (j n) -> p j n", j=nj),
                                        f32(hth[:, 0:nj, t * P:(t + 1) * P]), ALU.subtract).then_inc(sem(tag + "_hTl"), 1)

                fb = nf * f0
                followed(c0, ug, i0, lambda: evac(0, fb))
                if early:
                    early()
                turned(0, fb)
                followed(c0 + ug, ug, i0, lambda: evac(1, fb))
                follow(c0 + 2 * ug, nd, i0)
                turned(1, fb)
                c = c0 + 2 * ug + nd
                with dv.Fori(0, loops) as it:
                    ii = i0 + it * (U * (ug + nd) // ROUND)
                    for s in range(U):
                        followed(c + s * (ug + nd), ug, ii, lambda: evac(2 + s, fb + it * U))
                        follow(c + s * (ug + nd) + ug, nd, ii)
                        turned(2 + s, fb + it * U)
                c += loops * U * (ug + nd)
                for f in range(2 + loops * U, nf):
                    followed(c, ug, i0, lambda: evac(f, fb))
                    follow(c + ug, nd, i0)
                    turned(f, fb)
                    c += ug + nd
                if late:
                    late[0]()
                    followed(c, nd, i0, late[1])
                else:
                    follow_used(c, nd, i0)

            def rotate(dst, src, cs, sn, heads, t):
                def b3(ap):
                    return ap[:, None, :].to_broadcast((P, heads, 32))
                a, b = src[:, :, 0:32], src[:, :, 32:64]
                t1 = sq[:, 0, 0:heads * 32].rearrange("p (h d) -> p h d", h=heads)
                t2 = sq[:, 0, 512:512 + heads * 32].rearrange("p (h d) -> p h d", h=heads)
                t3 = sq[:, 1, 0:heads * 32].rearrange("p (h d) -> p h d", h=heads)
                t4 = sq[:, 1, 512:512 + heads * 32].rearrange("p (h d) -> p h d", h=heads)
                link(V.tensor_tensor(t1, a, b3(cs), ALU.mult))
                link(V.tensor_tensor(t2, b, b3(sn), ALU.mult))
                link(V.tensor_tensor(t3, b, b3(cs), ALU.mult))
                link(V.tensor_tensor(t4, a, b3(sn), ALU.mult))
                link(V.tensor_tensor(dst[:, :, 0:32], t1, t2, ALU.subtract))
                link(V.tensor_tensor(dst[:, :, 32:64], t3, t4, ALU.add))

            dv.wait_ge(sem("rel_in"), 32)
            V.tensor_copy(relw[:, :, :], relb[:, :, None].to_broadcast((BUCKETS, NB2, P))).then_inc(sem("rel_w"), 1)
            for c in range(SPLIT):
                split_lo(c, 0)
            norm("mix0")
            for j in range(3):
                dv.sem_inc(sem("in_go"), 1)
            dv.wait_ge(sem("in_go"), 3)
            with dv.Fori(0, 2) as i:
                for j in range(3):
                    follow(U_IN + 4 * j, 4, i)
                    dv.wait_ge(sem("in_c"), 2 * j + 2 + 6 * i)
                    dv.sem_inc(sem("in_go"), 1)
            dv.wait_ge(sem("in_go"), 9)
            for t in range(NT):
                V.tensor_tensor(xn[:, t, :], act[:, t, D:2 * D], act[:, t, 2 * D:3 * D], ALU.mult).then_inc(sem("cv_v"), 1)
            V.memset(vp[:, :, 0:2], 0.0).then_inc(sem("cv_z"), 1)
            dv.wait_ge(sem("cols_in"), 16)
            for k in range(KD):
                dv.wait_ge(sem("cv_p"), k + 1)
                w = [col("conv", 8 * n + k) for n in range(3)]
                v = cv[:, k % 2, :]
                link(V.tensor_scalar(v, vp[:, k, 0:256], w[0], None, ALU.mult))
                link(V.scalar_tensor_tensor(out=v, in0=vp[:, k, 1:257], scalar=w[1], in1=v, op0=ALU.mult, op1=ALU.add))
                link(V.scalar_tensor_tensor(out=v, in0=vp[:, k, 2:258], scalar=w[2], in1=v, op0=ALU.mult, op1=ALU.add))
                dv.wait_ge(sem("cv_T"), KD + bank_end(k, KD))
                V.tensor_tensor(cy[:, k % 2, :], v, bank[4 + k // 2][:, (k % 2) * 256:(k % 2 + 1) * 256], ALU.mult)\
                 .then_inc(sem("cv_y"), 1)
                dv.wait_ge(sem("cv_hi"), k + 1)
                V.tensor_tensor(xtl[:, k, :], cy[:, k % 2, :], f32(xth[:, k, :]), ALU.subtract).then_inc(sem("cv_l"), 1)
            residual(U_OUT, "out_r")

            def add_sums(tag):
                for t in range(NT):
                    V.tensor_tensor(x[:, t, :].rearrange("p (n c) -> p n c", n=2)[:, 0, :], x[:, t, 0:WIDE], bank[4 + 2 * t][:, :],
                                    ALU.add).then_inc(sem(tag), 1)
                    V.tensor_tensor(x[:, t, WIDE:D], x[:, t, WIDE:D], bank[5 + 2 * t][:, :], ALU.add).then_inc(sem(tag), 1)

            norm("ffn0")
            ffn("ff", U_FF1, FF1 // FG, 2, 4, FG, 2, 0)
            add_sums("f1_r")

            dv.wait_ge(sem("pos_in"), 16)
            dv.wait_ge(sem("fixed_in"), 16)
            dv.wait_ge(sem("rows_in"), 16)
            link(V.tensor_copy(posf[:, :], posi[:, :]))
            ang = sq[:, 0, 0:64].rearrange("p (t n) -> p t n", t=NT)
            for t in range(NT):
                link(V.tensor_scalar(ang[:, t, :], fixed[:, FIXED["freq"]:FIXED["freq"] + 32], posf[:, t:t + 1], None, ALU.mult))
            for w, quarter in ((0, 0.25), (1, 0.0)):
                turns = sq[:, 0, 64 + 64 * w:128 + 64 * w].rearrange("p (t n) -> p t n", t=NT)
                link(V.tensor_scalar(turns, ang, 1.0 / TWO_PI, quarter, ALU.mult, ALU.add))
                link(V.tensor_scalar(turns, turns, ROUNDER, None, ALU.add))
                link(V.tensor_scalar(turns, turns, ROUNDER, None, ALU.subtract))
                r = trig[:, w, :, :]
                link(V.scalar_tensor_tensor(out=r, in0=turns, scalar=-PI_A, in1=ang, op0=ALU.mult, op1=ALU.add))
                link(V.scalar_tensor_tensor(out=r, in0=turns, scalar=-PI_B, in1=r, op0=ALU.mult, op1=ALU.add))
                link(V.scalar_tensor_tensor(out=r, in0=turns, scalar=-PI_C, in1=r, op0=ALU.mult, op1=ALU.add))
                link(V.tensor_scalar(r, r, quarter * TWO_PI, PI_IN, ALU.add, ALU.min))
                if w == 0:
                    link(V.tensor_scalar(r, r, -PI_IN, None, ALU.max))
                else:
                    V.tensor_scalar(r, r, -PI_IN, None, ALU.max).then_inc(sem("ang"), 1)
            norm("mix1")
            follow(U_DOWN, 6, 0)
            dv.wait_ge(sem("lora_rs"), 1)
            for t in range(NT):
                V.tensor_scalar(xn[:, t, 0:QR], down[:, t, 0:QR], rs[:, t:t + 1], None, ALU.mult).then_inc(sem("lora_xn"), 1)
                V.tensor_scalar(xn[:, t, QR:QR + KVR], down[:, t, QR:QR + KVR], rs[:, NT + t:NT + t + 1], None, ALU.mult)\
                 .then_inc(sem("lora_xn"), 1)
            dv.wait_ge(sem("trig"), 1)
            krs = down[:, :, 640:704]
            link(V.tensor_tensor(sq[:, 0, 0:128].rearrange("p (t d) -> p t d", t=NT), krs, krs, ALU.mult))
            link(V.tensor_reduce(ss[:, 32:34], sq[:, 0, 0:128].rearrange("p (t d) -> p t d", t=NT), AX.X, ALU.add))
            link(V.tensor_tensor(krs, krs, rows[:, None, ROWS["kr"]:ROWS["kr"] + 64].to_broadcast((P, NT, 64)), ALU.mult))
            for t in range(NT):
                rotate(kr1[:, t:t + 1, :], down[:, t:t + 1, 640:704], trig[:, 0, t, :], trig[:, 1, t, :], 1, t)
            dv.sem_inc(sem("kr1"), 1)
            for k in range(5):
                dv.wait_ge(sem("lora_hi"), bank_end(k, 5))
                V.scalar_tensor_tensor(out=xtl[:, k, :], in0=bank[4 + k // 2][:, (k % 2) * 256:(k % 2 + 1) * 256],
                                       scalar=col("qa", k) if k < 3 else col("kva", k - 3), in1=f32(xth[:, k, :]),
                                       op0=ALU.mult, op1=ALU.subtract).then_inc(sem("lora_l"), 1)
            follow(U_UQ, 10, 0)
            for t in range(NT):
                dv.wait_ge(sem("q_sq"), t + 1)
                V.tensor_reduce(ss[:, 8 * t:8 * t + 8], sq[:, t, :].rearrange("p (h d) -> p h d", h=NH), AX.X, ALU.add)\
                 .then_inc(sem("q_sr"), 1)
            for t in range(NT):
                dv.wait_ge(sem("k_sq"), t + 1)
                link(V.tensor_reduce(ss[:, 16 + 8 * t:24 + 8 * t], sq[:, t, 0:1024].rearrange("p (h d) -> p h d", h=NH),
                                     AX.X, ALU.add))
            link(V.tensor_scalar(ss[:, 16:24], ss[:, 16:24], ss[:, 32:33], None, ALU.add))
            V.tensor_scalar(ss[:, 24:32], ss[:, 24:32], ss[:, 33:34], None, ALU.add).then_inc(sem("qk_ss"), 1)
            dv.wait_ge(sem("qk_rs"), 1)
            for t in range(NT):
                link(V.tensor_tensor(qv[:, t, :, :], qv[:, t, :, :], rs[:, 8 * t:8 * t + 8, None].to_broadcast((P, NH, QH)), ALU.mult))
            for t in range(NT):
                link(V.tensor_tensor(qv[:, t, :, NOPE:QH], qv[:, t, :, NOPE:QH],
                                     rows[:, None, ROWS["qr"]:ROWS["qr"] + 64].to_broadcast((P, NH, 64)), ALU.mult))
                rotate(qrb[:, t, :, :], qv[:, t, :, NOPE:QH], trig[:, 0, t, :], trig[:, 1, t, :], NH, t)
            dv.sem_inc(sem("q_ready"), 1)
            for t in range(NT):
                rk = rs[:, 16 + 8 * t:24 + 8 * t, None]
                link(V.tensor_tensor(kvv[:, t, :, 0:NOPE], kvv[:, t, :, 0:NOPE], rk.to_broadcast((P, NH, NOPE)), ALU.mult))
                link(V.tensor_tensor(krb[:, t, :, :], kr1[:, t:t + 1, :].to_broadcast((P, NH, 64)), rk.to_broadcast((P, NH, 64)),
                                     ALU.mult))
            dv.sem_inc(sem("k_ready"), 1)
            for n in range(1, 12, 2):
                dv.wait_ge(sem("qk_T"), n + 1)
                if n < 8:
                    V.tensor_scalar(wide[:, n * WIDE:(n + 1) * WIDE], bank[n % 8][:, :], col("qn" if n < 4 else "kn"), None,
                                    ALU.mult).then_inc(sem("qkT_d"), 1)
                else:
                    V.tensor_copy(wide[:, n * WIDE:(n + 1) * WIDE], bank[n % 8][:, :]).then_inc(sem("qkT_d"), 1)
            for s in range(NH + 2):
                if s < NH:
                    h = s
                    dv.wait_ge(sem("head_S"), h + 1)
                    if h >= 2:
                        dv.wait_ge(sem("head_PT"), h - 1)
                    b = h % 2
                    V.scalar_tensor_tensor(out=ebuf[:, b, 0:384], in0=bank[b][:, 0:384], scalar=QH ** -0.5, in1=maskt,
                                           op0=ALU.mult, op1=ALU.add).then_inc(sem("head_sc"), 1)
                    dv.wait_ge(sem("head_sc"), h + 1)
                    link(V.tensor_reduce(small[:, 68 + 0:68 + 1], ebuf[:, b, 0:P], AX.X, ALU.max))
                    link(V.tensor_reduce(small[:, 68 + 1:68 + 2], ebuf[:, b, P:384], AX.X, ALU.max))
                    V.tensor_scalar(small[:, 64 + 2 * b:66 + 2 * b], small[:, 68:70], -1.0, None, ALU.mult).then_inc(sem("head_nm"), 1)
                if 1 <= s <= NH:
                    h = s - 1
                    b = h % 2
                    dv.wait_ge(sem("head_e"), 2 * h + 2)
                    link(V.reciprocal(small[:, 76:78], small[:, 72 + 2 * b:74 + 2 * b]))
                    link(V.tensor_scalar(ebuf[:, b, 0:P], ebuf[:, b, 0:P], small[:, 76:77], None, ALU.mult))
                    V.tensor_scalar(ebuf[:, b, P:384], ebuf[:, b, P:384], small[:, 77:78], None, ALU.mult).then_inc(sem("head_p"), 1)
                if s >= 2:
                    h = s - 2
                    dv.wait_ge(sem("head_oh"), h + 1)
                    V.tensor_tensor(xtl[:, h, :], bank[4 + h % 2][:, 0:256], f32(xth[:, h, :]), ALU.subtract).then_inc(sem("head_ol"), 1)
            residual(U_WO, "wo_r")

            dv.wait_ge(sem("rt_h"), 1)
            V.tensor_tensor(rtl[:, :], cols[:, COLS["router"]:COLS["router"] + 64], f32(rth[:, :]), ALU.subtract).then_inc(sem("rt_l"), 1)
            norm("ffn1")
            link(V.memset(ones, 1.0))
            link(V.memset(gates[:, :, :], 0.0))
            link(V.memset(f32(selt[:, :]), 0.0))
            for t in range(NT):
                lg = small[:, 32 * t:32 * t + NE]
                mx = small[:, 32 * t + 16:32 * t + 24]
                fi = small[:, 32 * t + 24:32 * t + 32]
                dv.wait_ge(sem("rt_S"), t + 1)
                V.tensor_copy(lg, bank[t][:, 0:NE]).then_inc(sem("rt_c"), 1)
                dv.wait_ge(sem("rt_c"), t + 1)
                link(V.tensor_reduce(small[:, 32 * t + 10:32 * t + 11], lg, AX.X, ALU.max))
                V.tensor_scalar(small[:, 32 * t + 8:32 * t + 9], small[:, 32 * t + 10:32 * t + 11], -1.0, None, ALU.mult)\
                 .then_inc(sem("rt_m"), 1)
                dv.wait_ge(sem("rt_e"), t + 1)
                link(V.reciprocal(small[:, 32 * t + 11:32 * t + 12], small[:, 32 * t + 9:32 * t + 10]))
                link(V.tensor_scalar(lg, lg, small[:, 32 * t + 11:32 * t + 12], None, ALU.mult))
                link(V.max(mx, lg))
                link(V.max_index(topi[:, t, :], mx, lg))
                link(V.tensor_copy(fi, topi[:, t, :]))
                link(V.tensor_tensor(small[:, 32 * t + 12:32 * t + 13], mx[:, 0:1], mx[:, 1:2], ALU.add))
                link(V.reciprocal(small[:, 32 * t + 13:32 * t + 14], small[:, 32 * t + 12:32 * t + 13]))
                link(V.tensor_scalar(mx[:, 0:2], mx[:, 0:2], small[:, 32 * t + 13:32 * t + 14], None, ALU.mult))
                io = fixed[:, FIXED["iota"]:FIXED["iota"] + 8]
                link(V.tensor_scalar(lg, io, fi[:, 0:1], mx[:, 0:1], ALU.is_equal, ALU.mult))
                link(V.tensor_scalar(gates[:, t, 1:NE + 1], io, fi[:, 1:2], mx[:, 1:2], ALU.is_equal, ALU.mult))
                link(V.tensor_tensor(gates[:, t, 1:NE + 1], gates[:, t, 1:NE + 1], lg, ALU.add))
                link(V.tensor_scalar(lg, io, fi[:, 0:1], None, ALU.is_equal))
                link(V.memset(chosen[:, t, :], 0.0))
                V.scalar_tensor_tensor(out=chosen[:, t, 0:NE], in0=io, scalar=fi[:, 1:2], in1=lg, op0=ALU.is_equal,
                                       op1=ALU.add).then_inc(sem("chosen"), 1)
            link(V.memset(place[:, :, :], 0.0))
            dv.wait_ge(sem("places"), 1)
            link(V.tensor_copy(place[:, :, 0:NE], bank[0][:, 0:32].rearrange("p (t n) -> p t n", t=NT)[:, :, 0:NE]))
            link(V.tensor_copy(queue[:, 0:NE], bank[0][:, 32:32 + NE]))

            slots = fixed[:, FIXED["slots"]:FIXED["slots"] + P]
            every = fixed[:, FIXED["every"]:FIXED["every"] + P]

            def gathered(lot):
                for k in range(KD):
                    dv.wait_ge(sem("moe_gh"), lot * KD + k // 4 * 4 + 4)
                    V.scalar_tensor_tensor(out=xtl[:, k, 0:P], in0=bank[6 + k // 4][:, (k % 4) * P:(k % 4 + 1) * P],
                                           scalar=col("ffn1", k), in1=f32(xth[:, k, 0:P]), op0=ALU.mult, op1=ALU.subtract)\
                     .then_inc(sem("moe_gl"), 1)

            for t in range(NT):
                ins = V.tensor_scalar(sel[:, t, :], slots, place[:, t, 0:1], chosen[:, t, 0:1], ALU.is_equal, ALU.mult)
            ins.then_inc(sem("moe_sel"), 1)
            link(V.max(queue[:, NE:2 * NE], queue[:, 0:NE]))
            link(V.max_index(order[:, 0:8], queue[:, NE:2 * NE], queue[:, 0:NE]))
            link(V.tensor_scalar(queue[:, 0:NE], queue[:, 0:NE], float(CAP), None, ALU.is_gt))
            link(V.tensor_reduce(queue[:, 2 * NE:2 * NE + 1], queue[:, 0:NE], AX.X, ALU.add))
            V.tensor_copy(order[:, 8:9], queue[:, 2 * NE:2 * NE + 1]).then_inc(sem("order"), 1)
            gathered(0)
            for j in range(2):
                dv.sem_inc(sem("moe_yl"), 1)

            def next_sel(e):
                dv.wait_ge(sem("moe_selT"), e + 1)
                for t in range(NT):
                    ins = V.tensor_scalar(sel[:, t, :], slots, place[:, t, bass.ds(e + 1, 1)], chosen[:, t, bass.ds(e + 1, 1)],
                                          ALU.is_equal, ALU.mult)
                ins.then_inc(sem("moe_sel"), 1)

            def add_scattered(e):
                for t in range(NT):
                    gate = gates[:, t, bass.ds(e, 1)] if not isinstance(e, int) else gates[:, t, e:e + 1]
                    for n in range(2):
                        dv.wait_ge(sem("moe_S"), e * 4 + 2 * t + n + 1)
                        V.scalar_tensor_tensor(out=x[:, t, n * WIDE:(n + 1) * WIDE], in0=bank[(1, 3, 6, 7)[2 * t + n]][:, :],
                                               scalar=gate, in1=x[:, t, n * WIDE:(n + 1) * WIDE], op0=ALU.mult, op1=ALU.add)\
                         .then_inc(sem("moe_go"), 1)

            def outputs(e):
                for n in range(2):
                    dv.wait_ge(sem("moe_yh"), e * 2 + n + 1)
                    V.tensor_tensor(xtl[:, 4 * n:4 * n + 4, P:TOK], bank[4 + n][:, :].rearrange("p (k n) -> p k n", k=4),
                                    f32(xth[:, 4 * n:4 * n + 4, P:TOK]), ALU.subtract).then_inc(sem("moe_yl"), 1)

            def add_and_select(e):
                add_scattered(e)
                next_sel(e)

            with dv.Fori(0, NE) as e:
                ffn("ff", U_MOE, FFE // FG, 2, 3, FG, 2, e * 4, e, nt=1, done=DONE_FF1, early=lambda: add_and_select(e),
                    late=(lambda: gathered(e + 1), lambda: outputs(e)))
            add_scattered(NE)
            dv.wait_ge(sem("moe_go"), 4 * NE + 4)
            passes = dv.value_load(order[0:1, 8:9], min_val=0, max_val=3)
            with dv.If(passes > 0):
                with dv.Fori(0, passes) as v:
                    e = dv.value_load(order[0:1, bass.ds(v, 1)], min_val=0, max_val=NE - 1)
                    at = small[:, 80:80 + NT]
                    for t in range(NT):
                        V.tensor_scalar(at[:, t:t + 1], place[:, t, bass.ds(e, 1)], float(CAP), None, ALU.subtract)\
                         .then_inc(sem("o_at"), 1)
                    dv.wait_ge(sem("o_at"), v * 2 + 2)
                    for t in range(NT):
                        ins = V.tensor_scalar(osel[:, t, :], every, at[:, t:t + 1], chosen[:, t, bass.ds(e, 1)],
                                              ALU.is_equal, ALU.mult)
                    ins.then_inc(sem("o_sel"), 1)
                    for f in range(8):
                        g, u, h = bank[0][:, 0:FG], bank[0][:, FG:2 * FG], hbuf[:, 0, 0:FG]
                        dv.wait_ge(sem("o_e"), v * 8 + f + 1)
                        V.scalar_tensor_tensor(out=ebuf[:, 0, 0:FG], in0=ebuf[:, 0, 0:FG], scalar=1.0, in1=g, op0=ALU.add,
                                               op1=ALU.mult).then_inc(sem("o_s"), 1)
                        dv.wait_ge(sem("o_s"), v * 8 + f + 1)
                        V.scalar_tensor_tensor(out=h, in0=ebuf[:, 0, 0:FG], scalar=0.5, in1=u, op0=ALU.mult, op1=ALU.mult)\
                         .then_inc(sem("o_h"), 1)
                    for t in range(NT):
                        gate = gates[:, t, bass.ds(e + 1, 1)]
                        for n in range(2):
                            dv.wait_ge(sem("o_S"), v * 4 + 2 * t + n + 1)
                            V.scalar_tensor_tensor(out=x[:, t, n * WIDE:(n + 1) * WIDE],
                                                   in0=bank[(2, 3, 1, 4)[2 * t + n]][:, :], scalar=gate,
                                                   in1=x[:, t, n * WIDE:(n + 1) * WIDE], op0=ALU.mult, op1=ALU.add)\
                             .then_inc(sem("o_x"), 1)
                    dv.wait_ge(sem("o_x"), v * 4 + 4)
            dv.sem_inc(sem("moe_all"), 1)
            for n in range(2):
                a, b = ROWS[("lq1", "lq2")[n]], ROWS[("lk1", "lk2")[n]]
                link(V.tensor_tensor(small[:, 0:64], rows[:, a:a + 64], rows[:, b:b + 64], ALU.mult))
                V.tensor_reduce(lam[:, n:n + 1], small[:, 0:64], AX.X, ALU.add).then_inc(sem("lam_s"), 1)
                dv.wait_ge(sem("lam_s"), n + 1)
            V.tensor_scalar(lam[:, 5:6], col("sub"), 1.0 - LAMBDA0, None, ALU.mult).then_inc(sem("sub_g"), 1)
            norm("attn2")
            follow(U_IN2, 18, 0)
            dv.wait_ge(sem("in2_c"), 10)
            for t in range(NT):
                link(V.tensor_tensor(xn[:, t, 0:640], act[:, t, 0:640], act[:, t, 0:640], ALU.mult))
                link(V.tensor_reduce(ss[:, 26 * t:26 * t + 10], xn[:, t, 0:640].rearrange("p (h d) -> p h d", d=HD), AX.X, ALU.add))
                link(V.tensor_tensor(xn[:, t, :], act[:, t, 768:1792], act[:, t, 768:1792], ALU.mult))
                r = V.tensor_reduce(ss[:, 26 * t + 10:26 * t + 26], xn[:, t, :].rearrange("p (h d) -> p h d", d=HD), AX.X, ALU.add)
                if t == 0:
                    link(r)
                else:
                    r.then_inc(sem("h2_ss"), 1)
            dv.wait_ge(sem("h2_rs"), 1)
            for t in range(NT):
                qa = act[:, t, 0:512].rearrange("p (h d) -> p h d", d=HD)
                ka = act[:, t, 512:640].rearrange("p (h d) -> p h d", d=HD)
                both = act[:, t, 0:640].rearrange("p (h d) -> p h d", d=HD)
                link(V.tensor_tensor(both, both, rs[:, 26 * t:26 * t + 10, None].to_broadcast((P, 10, HD)), ALU.mult))
                link(V.tensor_tensor(qa, qa, rows[:, None, ROWS["aq"]:ROWS["aq"] + 64].to_broadcast((P, 8, HD)), ALU.mult))
                link(V.tensor_tensor(ka, ka, rows[:, None, ROWS["ak"]:ROWS["ak"] + 64].to_broadcast((P, 2, HD)), ALU.mult))
                C = fixed[:, FIXED["ctab"] + 64 * t:FIXED["ctab"] + 64 * (t + 1)]
                S = fixed[:, FIXED["stab"] + 64 * t:FIXED["stab"] + 64 * (t + 1)]
                sw = wide[:, 0:640].rearrange("p (h d) -> p h d", d=HD)
                for j in range(4):
                    o = (1, 0, 3, 2)[j]
                    link(V.tensor_tensor(sw[:, :, 16 * j:16 * j + 16], both[:, :, 16 * o:16 * o + 16],
                                         S[:, None, 16 * j:16 * j + 16].to_broadcast((P, 10, 16)), ALU.mult))
                link(V.tensor_tensor(both, both, C[:, None, :].to_broadcast((P, 10, HD)), ALU.mult))
                link(V.tensor_tensor(xn[:, t, 0:512].rearrange("p (j s d) -> p s j d", s=2, d=HD),
                                     act[:, t, 0:512].rearrange("p (s j d) -> p s j d", s=2, d=HD),
                                     wide[:, 0:512].rearrange("p (s j d) -> p s j d", s=2, d=HD), ALU.add))
                link(V.tensor_tensor(xn[:, t, 512:640].rearrange("p (h d) -> p h d", d=HD), ka, sw[:, 8:10, :], ALU.add))
            dv.sem_inc(sem("a_ready"), 1)
            for t in range(NT):
                qk = act[:, t, 768:1792].rearrange("p (h d) -> p h d", d=HD)
                link(V.tensor_tensor(qk, qk, rs[:, 26 * t + 10:26 * t + 26, None].to_broadcast((P, 16, HD)), ALU.mult))
            dv.sem_inc(sem("b_ready"), 1)
            dv.wait_ge(sem("lam_e"), 1)
            link(V.tensor_tensor(lam[:, 4:5], lam[:, 3:4], lam[:, 2:3], ALU.subtract))
            link(V.tensor_scalar(lam[:, 4:5], lam[:, 4:5], LAMBDA0, None, ALU.subtract))
            for s in range(NH + 2):
                if s < NH:
                    h = s
                    b = h % 2
                    dv.wait_ge(sem("head_S"), NH + h + 1)
                    if h >= 1:
                        dv.wait_ge(sem("head_nm"), NH + h)
                    V.tensor_reduce(small[:, 68:70], bank[b][:, :].rearrange("p (q n) -> p q n", q=2), AX.X, ALU.max)\
                     .then_inc(sem("a_mx"), 1)
                    dv.wait_ge(sem("a_mx"), h + 1)
                    V.tensor_scalar(small[:, 64 + 2 * b:66 + 2 * b], small[:, 68:70], -(HD ** -0.5), None, ALU.mult)\
                     .then_inc(sem("head_nm"), 1)
                if 1 <= s <= NH:
                    h = s - 1
                    b = h % 2
                    dv.wait_ge(sem("head_e"), 2 * NH + 2 * h + 2)
                    if h >= 1:
                        dv.wait_ge(sem("head_p"), NH + h)
                    V.reciprocal(small[:, 76:78], small[:, 72 + 2 * b:74 + 2 * b]).then_inc(sem("head_sc"), 1)
                    dv.wait_ge(sem("head_sc"), NH + h + 1)
                    link(V.tensor_scalar(ebuf[:, b, 0:256], ebuf[:, b, 0:256], small[:, 76:77], None, ALU.mult))
                    V.tensor_scalar(ebuf[:, b, 256:512], ebuf[:, b, 256:512], small[:, 77:78], None, ALU.mult).then_inc(sem("head_p"), 1)
                if s >= 2 and s % 2 == 1:
                    j = (s - 2) // 2
                    dv.wait_ge(sem("head_oh"), NH + j + 1)
                    V.tensor_tensor(xtl[:, j, :], bank[4 + j % 2][:, 0:256], f32(xth[:, j, :]), ALU.subtract).then_inc(sem("head_ol"), 1)
            dv.wait_ge(sem("bias_in"), 16 * 8)
            for s in range(NB2 + 1):
                if s < NB2:
                    h = s
                    for c in range(2):
                        dv.wait_ge(sem("b_S"), 2 * h + c + 1)
                        m = 4 * (h % 2) + 2 * c
                        e = act[:, h % 2, 2304 + c * 512:2304 + (c + 1) * 512]
                        V.scalar_tensor_tensor(out=e, in0=bank[2 * (h % 2) + c][:, :], scalar=HD ** -0.5,
                                               in1=bias2[:, h, :, :].rearrange("p q n -> p (q n)"), op0=ALU.mult, op1=ALU.add)\
                         .then_inc(sem("b_sc"), 1)
                        dv.wait_ge(sem("b_sc"), 2 * h + c + 1)
                        if h + c >= 1:
                            dv.wait_ge(sem("b_nm"), 2 * h + c)
                        link(V.tensor_reduce(small[:, 68:70], e.rearrange("p (q n) -> p q n", q=2), AX.X, ALU.max))
                        V.tensor_scalar(small[:, 80 + m:82 + m], small[:, 68:70], -1.0, None, ALU.mult).then_inc(sem("b_nm"), 1)
                if s >= 1:
                    h = s - 1
                    m = 4 * (h % 2)
                    dv.wait_ge(sem("b_e"), 4 * h + 4)
                    if h >= 1:
                        dv.wait_ge(sem("b_p"), h)
                    link(V.reciprocal(small[:, 112:116], small[:, 96 + m:100 + m]))
                    link(V.tensor_scalar(small[:, 114:116], small[:, 114:116], lam[:, 4:5], None, ALU.mult))
                    if h >= 1:
                        dv.wait_ge(sem("b_PT"), h)
                    for qb in range(2):
                        a = act[:, h % 2, 2304 + qb * 256:2304 + (qb + 1) * 256]
                        b = act[:, h % 2, 2816 + qb * 256:2816 + (qb + 1) * 256]
                        link(V.tensor_scalar(a, a, small[:, 112 + qb:113 + qb], None, ALU.mult))
                        r = V.scalar_tensor_tensor(out=hbuf[:, 0, qb * 256:(qb + 1) * 256], in0=b,
                                                   scalar=small[:, 114 + qb:115 + qb], in1=a, op0=ALU.mult, op1=ALU.add)
                        if qb == 0:
                            link(r)
                        else:
                            r.then_inc(sem("b_p"), 1)
                    dv.wait_ge(sem("ob_rs"), h + 1)
                    for t in range(NT):
                        V.tensor_scalar(xn[:, t, h * P:(h + 1) * P], bank[6 + h % 2][:, t * P:(t + 1) * P],
                                        rs[:, 2 * h + t:2 * h + t + 1], None, ALU.mult).then_inc(sem("ob_c"), 1)
            for h in range(NB2):
                dv.wait_ge(sem("ob_h"), bank_end(h, NB2))
                V.scalar_tensor_tensor(out=xtl[:, 4 + h, :], in0=bank[4 + h // 2][:, (h % 2) * 256:(h % 2 + 1) * 256],
                                       scalar=lam[:, 5:6], in1=f32(xth[:, 4 + h, :]), op0=ALU.mult, op1=ALU.subtract)\
                 .then_inc(sem("ob_l"), 1)
            residual(U_OUT2, "out2_r")

            norm("mlp2")
            ffn("ff", U_FF2, FF2 // FM, 3, 2, FM, 4, 0, done=DONE_MOE)
            add_sums("x_final")


def weight_stream(w):
    units = np.zeros((U_END + 2, P, UNIT), np.float32)

    def pairs(u, m):
        k, n = m.shape
        v = m.reshape(k // 256, 2, P, n // WIDE, WIDE).transpose(3, 0, 2, 1, 4)
        units[u:u + k // 256 * (n // WIDE)] = v.reshape(-1, P, UNIT)

    def narrow(u, m):
        k, n = m.shape
        units[u:u + k // 512, :, 0:4 * n] = m.reshape(k // 512, 4, P, n).transpose(0, 2, 1, 3).reshape(k // 512, P, 4 * n)

    def gate_up_down(u, wg, wu, wd):
        nf = wg.shape[1] // FG
        g = np.stack([wg.reshape(4, 2, P, nf, FG), wu.reshape(4, 2, P, nf, FG)], 4)
        g = g.transpose(3, 0, 2, 1, 4, 5).reshape(nf, 4, P, UNIT)
        d = wd.reshape(nf, 2, P, D)
        interleave(u, g, d)

    def interleave(u, g, d):
        nf, ug, ud = g.shape[0], g.shape[1], d.shape[1]
        units[u:u + ug] = g[0]
        u += ug
        for f in range(1, nf):
            units[u:u + ug] = g[f]
            units[u + ug:u + ug + ud] = d[f - 1]
            u += ug + ud
        units[u:u + ud] = d[nf - 1]

    pairs(U_IN, w["conv_w_in"][0])
    pairs(U_OUT, w["conv_w_out"][0])
    gate_up_down(U_FF1, w["ffn_w_gate"][0], w["ffn_w_up"][0], w["ffn_w_down"][0])
    pairs(U_DOWN, w["mla_w_down"][0][:, :WIDE])
    narrow(U_DOWN + 4, w["mla_w_down"][0][:, WIDE:])
    for n in range(3):
        m = w["mla_w_uq"][0][:, n * WIDE:(n + 1) * WIDE]
        pairs(U_UQ + 2 * n, m[0:256])
        units[U_UQ + 2 * n + 1, :, 0:WIDE] = m[256:384]
    pairs(U_UKV, w["mla_w_ukv"][0])
    pairs(U_WO, w["mla_w_o"][0])
    for e in range(NE):
        gate_up_down(U_MOE + 48 * e, w["moe_w_gate"][0, e], w["moe_w_up"][0, e], w["moe_w_down"][0, e])
    pairs(U_IN2, w["w_in_2"][0][:, :2048])
    narrow(U_IN2 + 16, w["w_in_2"][0][:, 2048:])
    pairs(U_OUT2, w["w_out_2"][0])
    up = w["w_up_2"][0].reshape(4, 2, P, 8, FM).transpose(3, 0, 2, 1, 4).reshape(8, 4, P, UNIT)
    interleave(U_FF2, up, w["w_down_2"][0].reshape(8, 4, P, D))
    return units.reshape(-1, 2, P, UNIT).transpose(0, 2, 1, 3).reshape(-1, P, 2 * UNIT)


def shape_tables():
    f = np.zeros((P, NFIXED), np.float32)
    f[:, 0:P] = np.eye(P)
    causal = np.where(np.arange(P)[None, :] <= np.arange(P)[:, None], 0.0, -3.0e38)
    f[:, FIXED["mask"]:FIXED["mask"] + P] = causal
    f[:, FIXED["mask"] + 2 * P:FIXED["mask"] + 3 * P] = causal
    inv = 1.0 / (np.float32(10000.0) ** (np.arange(0, 32, 2, dtype=np.float32) / np.float32(32)))
    tok = np.arange(TOK)
    ar = (tok // 64).astype(np.float32)[:, None] * inv[None, :].astype(np.float32)
    ac = (tok % 64).astype(np.float32)[:, None] * inv[None, :].astype(np.float32)
    ct = np.concatenate([np.cos(ar), np.cos(ar), np.cos(ac), np.cos(ac)], 1)
    st = np.concatenate([-np.sin(ar), np.sin(ar), -np.sin(ac), np.sin(ac)], 1)
    f[:, FIXED["ctab"]:FIXED["ctab"] + 128] = ct.reshape(2, P, 64).transpose(1, 0, 2).reshape(P, 128)
    f[:, FIXED["stab"]:FIXED["stab"] + 128] = st.reshape(2, P, 64).transpose(1, 0, 2).reshape(P, 128)
    f[:, FIXED["freq"]:FIXED["freq"] + 32] = np.float32(10000.0) ** (-np.arange(0, 64, 2, dtype=np.float32) / np.float32(64))
    f[:, FIXED["iota"]:FIXED["iota"] + 8] = np.arange(8)
    f[:, FIXED["before"]:FIXED["before"] + P] = np.arange(P)[:, None] < np.arange(P)[None, :]
    f[:, FIXED["slots"]:FIXED["slots"] + P] = np.where(np.arange(P) < CAP, np.arange(P), -1000)
    f[:, FIXED["every"]:FIXED["every"] + P] = np.arange(P)
    r = np.arange(-255, 257)
    n = np.abs(r)
    far = 8 + (np.log(np.maximum(n, 1).astype(np.float32) / np.float32(8)) / np.float32(np.log(16.0)) * np.float32(8)).astype(np.int32)
    bucket = (r > 0) * 16 + np.where(n < 8, n, np.minimum(far, 15))
    onehot = (np.arange(BUCKETS)[:, None] == bucket[None, :]).astype(np.float32)
    return f, onehot


def kernel(**inputs):
    import concourse.bacc as _bacc
    from concourse.bass_utils import run_bass_kernel_spmd as _run

    w = {k: np.asarray(v) for k, v in inputs.items()}

    def column(v):
        return v.reshape(-1, P).T

    two = lambda v: np.concatenate([v, v]).reshape(P, 1)
    cols = np.concatenate([
        column(w["norm_mix"][0]), column(w["norm_ffn"][0]), column(w["norm_mix"][1]), column(w["norm_ffn"][1]),
        column(w["attn_norm_g_2"][0]), column(w["mlp_norm_g_2"][0]), column(w["mla_q_a_norm"][0]),
        column(w["mla_kv_a_norm"][0]), column(w["mla_q_norm"][0][:NOPE]), column(w["mla_k_norm"][0][:NOPE]),
        column(w["conv_w"][0]), two(w["b_q_norm_g_2"][0]), two(w["b_k_norm_g_2"][0]), column(w["b_subln_g_2"][0]),
        w["moe_router"][0].reshape(KD, P, NE).transpose(1, 0, 2).reshape(P, KD * NE)], 1)
    rows = np.concatenate([
        w["mla_q_norm"][0][NOPE:], w["mla_k_norm"][0][NOPE:], w["a_q_norm_g_2"][0], w["a_k_norm_g_2"][0],
        w["lambda_q1_2"][0], w["lambda_k1_2"][0], w["lambda_q2_2"][0], w["lambda_k2_2"][0]]).reshape(1, NROWS)
    fixed, onehot = shape_tables()
    arrays = {
        "x_dram": w["x"][0], "pos_dram": w["positions"].reshape(NT, P).T, "weights_dram": weight_stream(w),
        "cols_dram": cols, "rows_dram": rows, "fixed_dram": fixed, "onehot_dram": onehot, "relb_dram": w["rel_bias_2"],
    }
    arrays = {k: np.ascontiguousarray(v) for k, v in arrays.items()}
    nc = _bacc.Bacc("TRN2", target_bir_lowering=False, num_devices=1)
    args = [nc.dram_tensor(k, v.shape, mybir.dt.from_np(v.dtype), kind="ExternalInput").ap() for k, v in arrays.items()]
    out = nc.dram_tensor("out_dram", (TOK, D), F32, kind="ExternalOutput").ap()
    build(nc, *args, out)
    r = _run(nc, [arrays], core_ids=[0])
    return r.results[0]["out_dram"].reshape(1, TOK, D)
```

```python
from contextlib import ExitStack

import numpy as np
import concourse.bass as bass
from concourse import mybir

F32 = mybir.dt.float32
F32R = mybir.dt.float32r
I32 = mybir.dt.int32
U32 = mybir.dt.uint32
ALU = mybir.AluOpType
ACT = mybir.ActivationFunctionType
AX = mybir.AxisListType

P = 128
D = 1024
TOK = 256
NT = TOK // P
KD = D // P
EPS = 1e-6
UNIT = 1024
WIDE = 512
RAW = 6
SPLIT = 6
ROUND = 2 * RAW

NH = 8
NOPE, ROPE, VD = 128, 64, 128
QH = NOPE + ROPE
QR, KVR = 384, 256
HD = 64
AQ, AKV, BQK, BV = 512, 128, 512, 512
IN2 = AQ + 2 * AKV + 2 * BQK + BV
NB2 = 4
BUCKETS = 32
LAMBDA0 = 0.8 - 0.6 * 1.0
FF1, FFE, FF2, NE = 2816, 2048, 4096, 8
FG = 256
CAP = P
FM = 512

U_IN = 0
U_OUT = U_IN + 24
U_FF1 = U_OUT + 8
U_DOWN = U_FF1 + 6 * (FF1 // FG)
U_UQ = U_DOWN + 6
U_UKV = U_UQ + 6
U_WO = U_UKV + 4
U_MOE = U_WO + 8
U_IN2 = U_MOE + NE * 6 * (FFE // FG)
U_OUT2 = U_IN2 + 18
U_FF2 = U_OUT2 + 8
U_END = U_FF2 + 8 * (FF2 // FM)
TOTAL = U_END + 2

DONE_FF1 = NT * (FF1 // FG)
DONE_MOE = DONE_FF1 + NE * (FFE // FG)

CONV_CHUNKS = (2, 4, 0, 3, 5, 1)

COLS = {}
_at = 0
for _name, _n in (("mix0", 8), ("ffn0", 8), ("mix1", 8), ("ffn1", 8), ("attn2", 8), ("mlp2", 8), ("qa", 3), ("kva", 2),
                  ("qn", 1), ("kn", 1), ("conv", 24), ("bq", 1), ("bk", 1), ("sub", 1), ("router", 64)):
    COLS[_name] = _at
    _at += _n
NCOLS = _at
ROWS = {}
_at = 0
for _name, _n in (("qr", 64), ("kr", 64), ("aq", 64), ("ak", 64), ("lq1", 64), ("lk1", 64), ("lq2", 64), ("lk2", 64)):
    ROWS[_name] = _at
    _at += _n
NROWS = _at
FIXED = {}
_at = 0
for _name, _n in (("ident", 128), ("mask", 384), ("ctab", 128), ("stab", 128), ("freq", 32), ("iota", 8),
                  ("before", 128), ("slots", 128), ("every", 128)):
    FIXED[_name] = _at
    _at += _n
NFIXED = _at

TWO_PI = 2.0 * np.pi
PI_A = 6.28125
PI_B = float(np.float32(np.round((TWO_PI - PI_A) * 2.0 ** 21) / 2.0 ** 21))
PI_C = float(TWO_PI - PI_A - PI_B)
ROUNDER = 1.5 * 2.0 ** 23
PI_IN = 3.1415925


def build(nc, x_in, pos_in, weights, cols_in, rows_in, fixed_in, onehot_in, relb_in, out):
    ctx = ExitStack()
    with ctx:
        def sb(name, shape, dt=F32):
            return ctx.enter_context(nc.sbuf_tensor(name, shape, dt))

        sems = {}

        def sem(name):
            if name not in sems:
                sems[name] = ctx.enter_context(nc.semaphore(name))
            return sems[name]

        raw = sb("raw", [P, RAW, 2 * UNIT])
        wh = sb("wh", [P, SPLIT, UNIT], F32R)
        wl = sb("wl", [P, SPLIT, UNIT], F32R)
        x = sb("x", [P, NT, D])
        xn = sb("xn", [P, NT, D])
        xth = sb("xth", [P, KD, TOK], F32R)
        xtl = sb("xtl", [P, KD, TOK], F32R)
        act = sb("act", [P, NT, 3584])
        wide = sb("wide", [P, 6144])
        hth = sb("hth", [P, 4, TOK], F32R)
        htl = sb("htl", [P, 4, TOK], F32R)
        ebuf = sb("ebuf", [P, NT, WIDE])
        hbuf = sb("hbuf", [P, NT, WIDE])
        cols = sb("cols", [P, NCOLS])
        rows = sb("rows", [P, NROWS])
        fixed = sb("fixed", [P, NFIXED])
        posi = sb("posi", [P, NT], I32)
        posf = sb("posf", [P, NT])
        relb = sb("relb", [BUCKETS, NB2])
        ss = sb("ss", [P, 64])
        rs = sb("rs", [P, 64])
        sst = sb("sst", [P, 64])
        trig = sb("trig", [P, 2, NT, 32])
        gates = sb("gates", [P, NT, NE + 1])
        chosen = sb("chosen", [P, NT, NE + 1])
        place = sb("place", [P, NT, NE + 1])
        queue = sb("queue", [P, 2 * NE + 8])
        order = sb("order", [P, 16], U32)
        sel = act[:, 1, 0:TOK].rearrange("p (t n) -> p t n", t=NT)
        ones = act[:, 1, TOK:TOK + P]
        selt = sb("selt", [P, TOK], F32R)
        rth = sb("rth", [P, KD * NE], F32R)
        rtl = sb("rtl", [P, KD * NE], F32R)
        small = sb("small", [P, 128])
        topi = sb("topi", [P, NT, 8], U32)
        lam = sb("lam", [P, 8])
        half = sb("half", [P, 64])
        bank = [ctx.enter_context(nc.psum_tensor(f"bank{i}", [P, WIDE], F32)) for i in range(8)]
        scratch = nc.dram_tensor("bias_scratch", (NB2 * P + 1, WIDE), F32).ap()

        ident = fixed[:, FIXED["ident"]:FIXED["ident"] + P]
        maskt = fixed[:, FIXED["mask"]:FIXED["mask"] + 384]
        onehot = ebuf[0:BUCKETS, 0, :]
        relw = ebuf[0:BUCKETS, 1, :].rearrange("p (h n) -> p h n", h=NB2)

        NORMS = ("mix0", "ffn0", "mix1", "ffn1", "attn2", "mlp2")

        QK_ORDER = (4, 5, 6, 7, 0, 1, 2, 3, 8, 9, 10, 11)

        def nth(tag):
            return NORMS.index(tag)

        raw_full = [sem(f"raw_full{i}") for i in range(RAW)]
        hi_done, lo_done, unit_used = sem("hi_done"), sem("lo_done"), sem("unit_used")

        def col(name, k=0):
            return cols[:, COLS[name] + k:COLS[name] + k + 1]

        def f32(ap):
            return ap.bitcast(F32)

        def bank_end(k, n):
            return min(k // 2 * 2 + 2, n)

        qv = act[:, :, 0:NH * QH].rearrange("p t (h d) -> p t h d", h=NH)
        kvv = act[:, :, NH * QH:NH * QH + NH * 256].rearrange("p t (h d) -> p t h d", h=NH)
        down = wide[:, 0:NT * 704].rearrange("p (t n) -> p t n", t=NT)
        sq = wide[:, 1408:1408 + NT * 1536].rearrange("p (t n) -> p t n", t=NT)
        ksq = wide[:, 4608:5632].rearrange("p (b t h d) -> p b t h d", b=2, t=NT, h=2)
        kr1 = small[:, 0:128].rearrange("p (t n) -> p t n", t=NT)
        qrb = xn[:, :, 0:512].rearrange("p t (h d) -> p t h d", h=NH)
        krb = xn[:, :, 512:1024].rearrange("p t (h d) -> p t h d", h=NH)
        qnT = wide[:, 0:2048].rearrange("p (h n) -> p h n", h=NH)
        knT = wide[:, 2048:4096].rearrange("p (h n) -> p h n", h=NH)
        qrT = wide[:, 4096:5120].rearrange("p (h n) -> p h n", h=4)
        krT = wide[:, 5120:6144].rearrange("p (h n) -> p h n", h=4)
        hT2 = wide[:, 0:13 * TOK].rearrange("p (g n) -> p g n", g=13)
        bsq = wide[:, 1280:3328].rearrange("p (t n) -> p t n", t=NT)
        bias2 = wide[:, 3328:3328 + NB2 * 2 * TOK].rearrange("p (h q n) -> p h q n", h=NB2, q=2)
        opanel = wide[:, :].rearrange("p (s n) -> p s n", s=3)
        oact = act[:, 0, :]
        osel = oact[:, 0:256].rearrange("p (t n) -> p t n", t=NT)
        oselt = oact[:, 256:512]
        oxt = oact[:, 512:1536].rearrange("p (k n) -> p k n", k=KD)
        oht = oact[:, 1536:1792].rearrange("p (j n) -> p j n", j=2)
        oy = oact[:, 1792:2816]
        vp = wide[:, 0:KD * 258].rearrange("p (k n) -> p k n", k=KD)
        cv = wide[:, 2064:2064 + KD * 256].rearrange("p (k n) -> p k n", k=KD)

        block = ctx.enter_context(nc.Block())

        @block.sync
        def _(sp):
            sp.dma_start(relb[:, :], relb_in).then_inc(sem("rel_in"), 16)
            sp.dma_start(onehot, onehot_in).then_inc(sem("rel_in"), 16)
            sp.dma_start(x[:, :, :], x_in.rearrange("(t p) d -> p t d", p=P)).then_inc(sem("x_in"), 16)
            sp.dma_start(fixed[:, :], fixed_in).then_inc(sem("fixed_in"), 16)
            sp.dma_start(cols[:, :], cols_in).then_inc(sem("cols_in"), 16)
            for p in range(RAW):
                sp.dma_start(raw[:, p, :], weights[p]).then_inc(raw_full[p], 16)
            panels = TOTAL // 2
            rounds = (panels - RAW) // RAW

            def load(p, i):
                sp.wait_ge(lo_done, 2 * (p - RAW) + 2 + i * ROUND)
                src = weights[p] if isinstance(i, int) else weights[bass.ds(i * RAW + p, 1)].rearrange("a p n -> (a p) n")
                sp.dma_start(raw[:, p % RAW, :], src).then_inc(raw_full[p % RAW], 16)

            with sp.Fori(0, rounds) as i:
                for p in range(RAW, 2 * RAW):
                    load(p, i)
            for p in range(RAW + rounds * RAW, panels):
                load(p, 0)
            sp.wait_ge(sem("order"), 1)
            sp.wait_ge(sem("moe_go"), 4 * NE + 4)
            passes = sp.value_load(order[0:1, 8:9], min_val=0, max_val=3)
            with sp.If(passes > 0):
                with sp.Fori(0, passes) as v:
                    e = sp.value_load(order[0:1, bass.ds(v, 1)], min_val=0, max_val=NE - 1)
                    sp.wait_ge(sem("o_sel"), v + 1)
                    first = U_MOE // 2 + e * 24
                    for f in range(8):
                        if f > 0:
                            sp.wait_ge(sem("o_gu"), v * 8 + f)
                        for q in range(2):
                            at = first + (3 * f - 1 if f else 0) + q
                            sp.dma_start(opanel[:, q, :], weights[bass.ds(at, 1)].rearrange("a p n -> (a p) n"))\
                              .then_inc(sem("o_up"), 16)
                        if f > 0:
                            sp.wait_ge(sem("o_d"), v * 8 + f)
                        at = first + (3 * f + 4 if f < 7 else 23)
                        sp.dma_start(opanel[:, 2, :], weights[bass.ds(at, 1)].rearrange("a p n -> (a p) n"))\
                          .then_inc(sem("o_down"), 16)
            sp.wait_ge(sem("x_final"), 4)
            sp.dma_start(out.rearrange("(t p) d -> p t d", p=P), x[:, :, :]).then_inc(sem("stored"), 16)
            sp.wait_ge(sem("stored"), 16)

        @block.gpsimd
        def _(pool):
            g = nc.gpsimd
            pool.dma_start(rows[:, :], rows_in.to_broadcast((P, NROWS))).then_inc(sem("rows_in"), 16)
            pool.dma_start(posi[:, :], pos_in).then_inc(sem("pos_in"), 16)

            g.memset(half[:, :], -0.5).then_inc(sem("half"), 1)
            pool.wait_ge(sem("half"), 1)

            def rsqrt(tag, a, b, n):
                g.tensor_scalar(sst[:, a:b], ss[:, a:b], 1.0 / n, EPS, ALU.mult, ALU.add).then_inc(sem(tag + "_ms"), 1)

            def power(tag, a, b, lot):
                pool.wait_ge(sem(tag + "_ms"), lot)
                g.tensor_tensor(rs[:, a:b], sst[:, a:b], half[:, 0:b - a], ALU.pow).then_inc(sem(tag + "_rs"), 1)

            def norm_rs(tag):
                for t in range(NT):
                    pool.wait_ge(sem("norm_ss"), NT * nth(tag) + t + 1)
                    g.tensor_scalar(sst[:, t:t + 1], ss[:, t:t + 1], 1.0 / D, EPS, ALU.mult, ALU.add).then_inc(sem("norm_ms"), 1)
                    pool.wait_ge(sem("norm_ms"), NT * nth(tag) + t + 1)
                    g.tensor_tensor(rs[:, t:t + 1], sst[:, t:t + 1], half[:, 0:1], ALU.pow).then_inc(sem("norm_rs"), 1)

            norm_rs("mix0")
            norm_rs("ffn0")
            norm_rs("mix1")
            pool.wait_ge(sem("lora_ss"), 2 * NT)
            g.tensor_scalar(sst[:, 0:NT], ss[:, 0:NT], 1.0 / QR, EPS, ALU.mult, ALU.add).then_inc(sem("lora_m1"), 1)
            g.tensor_scalar(sst[:, NT:2 * NT], ss[:, NT:2 * NT], 1.0 / KVR, EPS, ALU.mult, ALU.add).then_inc(sem("lora_m2"), 1)
            pool.wait_ge(sem("lora_m1"), 1)
            pool.wait_ge(sem("lora_m2"), 1)
            g.tensor_tensor(rs[:, 0:2 * NT], sst[:, 0:2 * NT], half[:, 0:2 * NT], ALU.pow).then_inc(sem("lora_rs"), 1)
            pool.wait_ge(sem("qk_ss"), 1)
            rsqrt("qk", 0, 16, QH)
            power("qk", 0, 16, 1)
            for j in range(4):
                pool.wait_ge(sem("qk_ss"), j + 2)
                rsqrt("qk", 16 + 4 * j, 20 + 4 * j, QH)
                power("qk", 16 + 4 * j, 20 + 4 * j, j + 2)
            norm_rs("ffn1")
            norm_rs("attn2")
            pool.wait_ge(sem("h2_ss"), 1)
            rsqrt("h2", 0, 20, HD)
            power("h2", 0, 20, 1)
            pool.wait_ge(sem("h2_ss"), 2)
            rsqrt("h2", 20, 52, HD)
            power("h2", 20, 52, 2)
            for h in range(NB2):
                pool.wait_ge(sem("ob_ss"), 2 * h + 2)
                g.tensor_scalar(sst[:, 2 * h:2 * h + 2], ss[:, 2 * h:2 * h + 2], 1.0 / VD, EPS, ALU.mult, ALU.add)\
                 .then_inc(sem("ob_ms"), 1)
                pool.wait_ge(sem("ob_ms"), h + 1)
                g.tensor_tensor(rs[:, 2 * h:2 * h + 2], sst[:, 2 * h:2 * h + 2], half[:, 0:2], ALU.pow)\
                 .then_inc(sem("ob_rs"), 1)
            norm_rs("mlp2")

        @block.tensor
        def _(pe):
            mm = nc.tensor.matmul

            def mm3(o, lh, ll, wi, sl, start, stop):
                mm(o, lh, wh[:, wi, sl], start=start, stop=False)
                mm(o, lh, wl[:, wi, sl], start=False, stop=False)
                return mm(o, ll, wh[:, wi, sl], start=False, stop=stop)

            def xt(k, t):
                return xth[:, k, t * P:(t + 1) * P], xtl[:, k, t * P:(t + 1) * P]

            def product(c, i, ks, width, banks, k_first, k_last, k0=0, nt=NT):
                pe.wait_ge(lo_done, c + 1 + ROUND * i)
                for n, k in enumerate(ks):
                    for t in range(nt):
                        last = mm3(banks[t][:, 0:width], *xt(k0 + k, t), c % SPLIT, slice(n * width, (n + 1) * width),
                                   k == k_first, k == k_last)
                last.then_inc(unit_used, 1)

            def normed(tag):
                return lambda u: pe.wait_ge(sem("norm_l"), KD * nth(tag) + 2 * u + 2)

            def chunk512(c, i, banks, rows_ready=None):
                for u in range(4):
                    if rows_ready:
                        rows_ready(u)
                    product(c + u, i, (2 * u, 2 * u + 1), WIDE, banks, 0, KD - 1)

            def turn_norm(tag):
                for t in range(NT):
                    if t == 0:
                        pe.wait_ge(sem("norm_x0"), nth(tag) + 1)
                    else:
                        pe.wait_ge(sem("norm_xn"), 2 * nth(tag) + 2)
                    for k in range(KD):
                        last = nc.tensor.transpose(bank[4 + k // 2][:, (k % 2) * 256 + t * P:(k % 2) * 256 + (t + 1) * P],
                                                   xn[:, t, k * P:(k + 1) * P], ident)
                        if t == NT - 1:
                            last.then_inc(sem("norm_T"), 1)

            def ffn(tag, c0, nf, U, loops, width, nd, i0, f0=0, nt=NT, early=None, late=None, done=0, rows_ready=None):
                nj = width // P
                ug = 4

                def up(c, i, rows_ready=None):
                    for u in range(ug):
                        if rows_ready:
                            rows_ready(u)
                        product(c + u, i, (2 * u, 2 * u + 1), WIDE, bank[0:2], 0, KD - 1, nt=nt)

                def turn(fc, fv):
                    for t in range(nt):
                        pe.wait_ge(sem(tag + "_h"), done + nt * fc + t + 1 + fv * nt)
                        for j in range(nj):
                            last = nc.tensor.transpose(bank[2 + t][:, j * P:(j + 1) * P], hbuf[:, t, j * P:(j + 1) * P], ident)
                        last.then_inc(sem(tag + "_hT"), 1)

                def down_(c, i, fc, fv, first, final):
                    pe.wait_ge(sem(tag + "_hTl"), done + nt * fc + nt + fv * nt)
                    for j in range(nd):
                        pe.wait_ge(lo_done, c + j + 1 + ROUND * i)
                        for t in range(nt):
                            for n in range(2):
                                last = mm3(bank[4 + 2 * t + n][:, :], hth[:, j, t * P:(t + 1) * P],
                                           htl[:, j, t * P:(t + 1) * P], (c + j) % SPLIT, slice(n * WIDE, (n + 1) * WIDE),
                                           first and j == 0, final and j == nd - 1)
                        last.then_inc(unit_used, 1)

                fb = nf * f0
                up(c0, i0, rows_ready)
                if early:
                    early()
                turn(0, fb)
                up(c0 + ug, i0)
                if late:
                    pe.wait_ge(sem("moe_selc"), f0 + 1)
                down_(c0 + 2 * ug, i0, 0, fb, True, False)
                turn(1, fb)
                c = c0 + 2 * ug + nd
                with pe.Fori(0, loops) as it:
                    ii = i0 + it * (U * (ug + nd) // ROUND)
                    for s in range(U):
                        up(c + s * (ug + nd), ii)
                        down_(c + s * (ug + nd) + ug, ii, 1 + s, fb + it * U, False, False)
                        turn(2 + s, fb + it * U)
                c += loops * U * (ug + nd)
                for f in range(2 + loops * U, nf):
                    up(c, i0)
                    down_(c + ug, i0, f - 1, fb, False, False)
                    turn(f, fb)
                    c += ug + nd
                if late:
                    late()
                down_(c, i0, nf - 1, fb, False, True)

            pe.wait_ge(sem("rel_w"), 1)
            pe.wait_ge(sem("rel_in"), 32)
            for h in range(NB2):
                mm(bank[h][:, :], relw[:, h, :], onehot, start=True, stop=True).then_inc(sem("rel_T"), 1)

            pe.wait_ge(sem("fixed_in"), 16)
            turn_norm("mix0")
            pe.wait_ge(sem("rel_c"), NB2)

            def turn_conv(src, banks, half):
                for k in range(4):
                    for t in range(NT):
                        at = (4 * half + k) * P
                        last = nc.tensor.transpose(banks[k // 2][:, (k % 2) * 256 + t * P:(k % 2) * 256 + (t + 1) * P],
                                                   src[:, t, at:at + P], ident)
                    last.then_inc(sem("cv_T"), 1)

            for j in range(6):
                if j >= 3:
                    pe.wait_ge(sem("in_c"), 2 * (j - 2))
                chunk512(U_IN + 4 * j, 0, bank[2 * (j % 3):2 * (j % 3) + 2], normed("mix0") if j == 0 else None)
                if j == 3:
                    pe.wait_ge(sem("cv_v"), 1)
                    turn_conv(xn, bank[6:8], 0)
                if j == 4:
                    pe.wait_ge(sem("in_c"), 6)
                    pe.wait_ge(sem("cv_p"), 4)
                    turn_conv(act, bank[6:8], 0)
            pe.wait_ge(sem("cv_v"), 2)
            pe.wait_ge(sem("cv_y"), 4)
            turn_conv(xn, bank[6:8], 1)
            pe.wait_ge(sem("in_c"), 12)
            turn_conv(act, bank[2:4], 1)
            for n in range(2):
                chunk512(U_OUT + 4 * n, 0, bank[2 * n:2 * n + 2],
                         (lambda u: pe.wait_ge(sem("cv_l"), 2 * u + 2)) if n == 0 else None)

            turn_norm("ffn0")
            pe.wait_ge(sem("out_r"), 4)
            ffn("ff", U_FF1, FF1 // FG, 2, 4, FG, 2, 0, rows_ready=normed("ffn0"))

            turn_norm("mix1")
            pe.wait_ge(sem("f1_r"), 4)
            chunk512(U_DOWN, 0, bank[0:2], normed("mix1"))
            for u in range(2):
                product(U_DOWN + 4 + u, 0, range(4 * u, 4 * u + 4), 192, bank[2:4], 0, KD - 1)
            pe.wait_ge(sem("lora_xn"), 2 * NT)
            for k in range(5):
                for t in range(NT):
                    last = nc.tensor.transpose(bank[4 + k // 2][:, (k % 2) * 256 + t * P:(k % 2) * 256 + (t + 1) * P],
                                               xn[:, t, k * P:(k + 1) * P], ident)
                last.then_inc(sem("lora_T"), 1)
            pe.wait_ge(sem("lora_l"), 5)
            pe.wait_ge(sem("down_c"), 4)
            for n in range(7):
                if n >= 2:
                    pe.wait_ge(sem("quv_c"), 2 * (n - 1))
                b = bank[2 * (n % 2):2 * (n % 2) + 2]
                if n < 3:
                    product(U_UQ + 2 * n, 0, (0, 1), WIDE, b, 0, 2)
                    product(U_UQ + 2 * n + 1, 0, (2,), WIDE, b, 0, 2)
                else:
                    product(U_UKV + n - 3, 0, (0, 1), WIDE, b, 0, 1, k0=3)
            for p, n in enumerate(QK_ORDER):
                if p < 4:
                    pe.wait_ge(sem("k_ready"), p + 1)
                elif p < 8:
                    pe.wait_ge(sem("quv_c"), 14)
                    pe.wait_ge(sem("q_ready"), 4 * (p - 3))
                else:
                    pe.wait_ge(sem("qkT_d" if p % 2 else "qkT_a"), (p - 4) // 2 + 1)
                    pe.wait_ge(sem("qr_ready"), 1)
                for m in range(2):
                    for t in range(NT):
                        if n < 4:
                            src = qv[:, t, 2 * n + m, 0:NOPE]
                        elif n < 8:
                            src = kvv[:, t, 2 * (n - 4) + m, 0:NOPE]
                        elif n < 10:
                            src = xn[:, t, (2 * (n - 8) + m) * P:(2 * (n - 8) + m + 1) * P]
                        else:
                            src = xn[:, t, 512 + (2 * (n - 10) + m) * P:512 + (2 * (n - 10) + m + 1) * P]
                        last = nc.tensor.transpose(bank[n % 8][:, m * 256 + t * P:m * 256 + (t + 1) * P], src, ident)
                last.then_inc(sem("qk_T"), 1)
            pe.wait_ge(sem("qkT_a"), 6)
            pe.wait_ge(sem("qkT_d"), 6)
            for s in range(-1, NH + 2):
                if s + 1 < NH:
                    h = s + 1
                    if h >= 2:
                        pe.wait_ge(sem("head_sc"), h - 1)
                    r0 = (h % 2) * 64
                    for qb, (a, n) in enumerate(((0, P), (P, 2 * P))):
                        o = bank[h % 2][:, a:a + n]
                        mm(o, qnT[:, h, qb * P:(qb + 1) * P], knT[:, h, 0:n], start=True, stop=False)
                        last = mm(o, qrT[r0:r0 + 64, h // 2, qb * P:(qb + 1) * P], krT[r0:r0 + 64, h // 2, 0:n],
                                  start=False, stop=True)
                    last.then_inc(sem("head_S"), 1)
                if 1 <= s <= NH:
                    h = s - 1
                    pe.wait_ge(sem("head_p"), h + 1)
                    if h >= 2:
                        pe.wait_ge(sem("head_pT"), h - 1)
                    for j in range(3):
                        last = nc.tensor.transpose(bank[2 + h % 2][:, j * P:(j + 1) * P], ebuf[:, h % 2, j * P:(j + 1) * P], ident)
                    last.then_inc(sem("head_PT"), 1)
                if s >= 2:
                    h = s - 2
                    pe.wait_ge(sem("head_pT"), h + 1)
                    if h >= 2:
                        pe.wait_ge(sem("head_ol"), h - 1)
                    mm(bank[4 + h % 2][:, 0:P], kvv[:, 0, h, NOPE:256], hbuf[:, h % 2, 0:P], start=True, stop=True)
                    mm(bank[4 + h % 2][:, P:256], kvv[:, 0, h, NOPE:256], hbuf[:, h % 2, P:256], start=True, stop=False)
                    mm(bank[4 + h % 2][:, P:256], kvv[:, 1, h, NOPE:256], hbuf[:, h % 2, 256:384], start=False, stop=True)\
                        .then_inc(sem("head_O"), 1)
            pe.wait_ge(sem("head_ol"), NH)
            for n in range(2):
                chunk512(U_WO + 4 * n, 0, bank[2 * n:2 * n + 2])

            turn_norm("ffn1")
            pe.wait_ge(sem("norm_l"), KD * (nth("ffn1") + 1))
            pe.wait_ge(sem("wo_r"), 4)
            pe.wait_ge(sem("rt_l"), 1)
            for t in range(NT):
                for k in range(KD):
                    h, l = xt(k, t)
                    o = bank[t][:, 0:NE]
                    mm(o, h, rth[:, k * NE:(k + 1) * NE], start=(k == 0), stop=False)
                    mm(o, h, rtl[:, k * NE:(k + 1) * NE], start=False, stop=False)
                    last = mm(o, l, rth[:, k * NE:(k + 1) * NE], start=False, stop=(k == KD - 1))
                last.then_inc(sem("rt_S"), 1)
            before = fixed[:, FIXED["before"]:FIXED["before"] + P]
            pe.wait_ge(sem("chosen"), NT)
            mm(bank[0][:, 0:NE], before, chosen[:, 0, 0:NE], start=True, stop=True)
            mm(bank[0][:, 16:16 + NE], before, chosen[:, 1, 0:NE], start=True, stop=False)
            mm(bank[0][:, 16:16 + NE], ones, chosen[:, 0, 0:NE], start=False, stop=True)
            mm(bank[0][:, 32:32 + NE], ones, chosen[:, 0, 0:NE], start=True, stop=False)
            mm(bank[0][:, 32:32 + NE], ones, chosen[:, 1, 0:NE], start=False, stop=True).then_inc(sem("places"), 1)

            def gather(tag, source, lot):
                pe.wait_ge(sem(tag + "_sel"), lot)
                for k in range(KD):
                    for t in range(NT):
                        last = mm(bank[6 + k // 4][:, (k % 4) * P:(k % 4 + 1) * P], xn[:, t, k * P:(k + 1) * P],
                                  source[:, t, :], start=(t == 0), stop=(t == NT - 1))
                    if k % 4 == 3:
                        last.then_inc(sem(tag + "_g"), 1)

            def turn_sel(e):
                pe.wait_ge(sem("moe_sel"), e + 1)
                for t in range(NT):
                    last = nc.tensor.transpose(bank[5][:, t * P:(t + 1) * P], sel[:, t, :], ident)
                last.then_inc(sem("moe_selT"), 1)

            def scatter(e):
                pe.wait_ge(sem("moe_yl"), e * 2 + 2)
                for t in range(NT):
                    for n in range(2):
                        o = bank[(1, 3, 6, 7)[2 * t + n]][:, :]
                        yh, yl = (v[:, 4 * n:4 * n + 4, P:TOK] for v in (xth, xtl))
                        mm(o, selt[:, t * P:(t + 1) * P], yh, start=True, stop=False)
                        mm(o, selt[:, t * P:(t + 1) * P], yl, start=False, stop=True).then_inc(sem("moe_S"), 1)

            def scatter_and_turn(e):
                scatter(e)
                turn_sel(e)

            def gather_next(e):
                pe.wait_ge(sem("moe_go"), e * 4 + 4)
                gather("moe", sel, e + 2)

            gather("moe", sel, 1)
            with pe.Fori(0, NE) as e:
                pe.wait_ge(sem("moe_gl"), e * KD + KD)
                ffn("ff", U_MOE, FFE // FG, 2, 3, FG, 2, e * 4, e, nt=1, done=DONE_FF1,
                    early=lambda: scatter_and_turn(e), late=lambda: gather_next(e))
            pe.wait_ge(sem("moe_gl"), NE * KD + KD)
            scatter(NE)

            pe.wait_ge(sem("order"), 1)
            pe.wait_ge(sem("moe_go"), 4 * NE + 4)
            passes = pe.value_load(order[0:1, 8:9], min_val=0, max_val=3)
            with pe.If(passes > 0):
                with pe.Fori(0, passes) as v:
                    gather("o", osel, v + 1)
                    for t in range(NT):
                        last = nc.tensor.transpose(bank[3][:, t * P:(t + 1) * P], osel[:, t, :], ident)
                    last.then_inc(sem("o_selT"), 1)
                    pe.wait_ge(sem("o_xt"), v * 2 + 2)
                    for f in range(8):
                        pe.wait_ge(sem("o_up"), v * 256 + 32 * (f + 1))
                        for k in range(KD):
                            last = mm(bank[0][:, :], oxt[:, k, :], opanel[:, k // 4, (k % 4) * WIDE:(k % 4 + 1) * WIDE],
                                      start=(k == 0), stop=(k == KD - 1))
                        last.then_inc(sem("o_gu"), 1)
                        pe.wait_ge(sem("o_h"), v * 8 + f + 1)
                        for j in range(2):
                            last = nc.tensor.transpose(bank[2][:, j * P:(j + 1) * P], hbuf[:, 0, j * P:(j + 1) * P], ident)
                        last.then_inc(sem("o_hT"), 1)
                        pe.wait_ge(sem("o_hc"), v * 8 + f + 1)
                        pe.wait_ge(sem("o_down"), v * 128 + 16 * (f + 1))
                        for j in range(2):
                            for n in range(2):
                                last = mm(bank[4 + n][:, :], oht[:, j, :],
                                          opanel[:, 2, j * D + n * WIDE:j * D + (n + 1) * WIDE],
                                          start=(f == 0 and j == 0), stop=(f == 7 and j == 1))
                        last.then_inc(sem("o_d"), 1)
                    pe.wait_ge(sem("o_y"), v * 2 + 2)
                    for t in range(NT):
                        for n in range(2):
                            mm(bank[(2, 3, 1, 4)[2 * t + n]][:, :], oselt[:, t * P:(t + 1) * P],
                               oy[:, n * WIDE:(n + 1) * WIDE], start=True, stop=True).then_inc(sem("o_S"), 1)
                    pe.wait_ge(sem("o_x"), v * 4 + 4)

            turn_norm("attn2")
            pe.wait_ge(sem("moe_go"), 4 * NE + 4)
            for n in range(5):
                if n >= 2:
                    pe.wait_ge(sem("in2_c"), 2 * (n - 1))
                b = bank[2 * (n % 2):2 * (n % 2) + 2]
                if n < 4:
                    chunk512(U_IN2 + 4 * n, 0, b, normed("attn2") if n == 0 else None)
                else:
                    for u in range(2):
                        product(U_IN2 + 16 + u, 0, range(4 * u, 4 * u + 4), 256, b, 0, KD - 1)
            pe.wait_ge(sem("in2_c"), 10)
            pe.wait_ge(sem("a_ready"), 1)
            for g in range(5):
                for t in range(NT):
                    last = nc.tensor.transpose(bank[g // 2][:, (g % 2) * 256 + t * P:(g % 2) * 256 + (t + 1) * P],
                                               xn[:, t, g * P:(g + 1) * P], ident)
                last.then_inc(sem("h2_T"), 1)
            pe.wait_ge(sem("h2T_c"), 5)
            for s in range(-1, NH + 2):
                if s + 1 < NH:
                    h = s + 1
                    if h >= 2:
                        pe.wait_ge(sem("head_sc"), NH + h - 1)
                    r0 = (h // 4) * 64
                    for qb in range(2):
                        last = mm(bank[h % 2][:, qb * 256:(qb + 1) * 256], hT2[r0:r0 + 64, h % 4, qb * P:(qb + 1) * P],
                                  hT2[r0:r0 + 64, 4, :], start=True, stop=True)
                    last.then_inc(sem("head_S"), 1)
                if 1 <= s <= NH:
                    h = s - 1
                    pe.wait_ge(sem("head_p"), NH + h + 1)
                    if h >= 2:
                        pe.wait_ge(sem("head_pT"), NH + h - 1)
                    for kb in range(2):
                        for qb in range(2):
                            last = nc.tensor.transpose(bank[2 + h % 2][:, kb * 256 + qb * P:kb * 256 + (qb + 1) * P],
                                                       ebuf[:, h % 2, qb * 256 + kb * P:qb * 256 + (kb + 1) * P], ident)
                    last.then_inc(sem("head_PT"), 1)
                if s >= 2:
                    h = s - 2
                    pe.wait_ge(sem("head_pT"), NH + h + 1)
                    if h >= 4 and h % 2 == 0:
                        pe.wait_ge(sem("head_ol"), NH + h // 2 - 1)
                    r0 = (h % 2) * 64
                    v0 = 640 + (h // 4) * 64
                    for kb in range(2):
                        last = mm(bank[4 + (h // 2) % 2][r0:r0 + 64, 0:256], act[:, kb, v0:v0 + 64],
                                  hbuf[:, h % 2, kb * 256:(kb + 1) * 256], start=(kb == 0), stop=(kb == 1))
                    last.then_inc(sem("head_O"), 1)
            pe.wait_ge(sem("b_ready"), 1)
            for g in range(8):
                for t in range(NT):
                    last = nc.tensor.transpose(bank[g // 2][:, (g % 2) * 256 + t * P:(g % 2) * 256 + (t + 1) * P],
                                               act[:, t, 768 + g * P:768 + (g + 1) * P], ident)
                last.then_inc(sem("h2_T"), 1)
            pe.wait_ge(sem("h2T_c"), 13)
            pe.wait_ge(sem("head_ol"), NH + 4)
            for s in range(-1, NB2 + 1):
                if s + 1 < NB2:
                    h = s + 1
                    for c in range(2):
                        if h >= 2:
                            pe.wait_ge(sem("b_sc"), 2 * (h - 2) + c + 1)
                        for qb in range(2):
                            last = mm(bank[2 * (h % 2) + c][:, qb * 256:(qb + 1) * 256],
                                      hT2[c * 64:c * 64 + 64, 5 + h, qb * P:(qb + 1) * P],
                                      hT2[c * 64:c * 64 + 64, 9 + h, :], start=True, stop=True)
                        last.then_inc(sem("b_S"), 1)
                if s >= 1:
                    h = s - 1
                    pe.wait_ge(sem("b_p"), h + 1)
                    if h >= 2:
                        pe.wait_ge(sem("b_pT"), h - 1)
                    for kb in range(2):
                        for qb in range(2):
                            last = nc.tensor.transpose(bank[4 + h % 2][:, kb * 256 + qb * P:kb * 256 + (qb + 1) * P],
                                                       hbuf[:, 0, qb * 256 + kb * P:qb * 256 + (kb + 1) * P], ident)
                    last.then_inc(sem("b_PT"), 1)
                    pe.wait_ge(sem("b_pT"), h + 1)
                    if h >= 2:
                        pe.wait_ge(sem("ob_c"), 2 * (h - 1))
                    for qb in range(2):
                        for kb in range(2):
                            last = mm(bank[6 + h % 2][:, qb * P:(qb + 1) * P],
                                      hbuf[:, 1, kb * 256 + qb * P:kb * 256 + (qb + 1) * P],
                                      act[:, kb, 1792 + h * P:1792 + (h + 1) * P], start=(kb == 0), stop=(kb == 1))
                    last.then_inc(sem("b_O"), 1)
            pe.wait_ge(sem("ob_c"), 2 * NB2)
            for h in range(NB2):
                for t in range(NT):
                    last = nc.tensor.transpose(bank[4 + h // 2][:, (h % 2) * 256 + t * P:(h % 2) * 256 + (t + 1) * P],
                                               xn[:, t, h * P:(h + 1) * P], ident)
                last.then_inc(sem("ob_T"), 1)
            pe.wait_ge(sem("ob_l"), NB2)
            for n in range(2):
                chunk512(U_OUT2 + 4 * n, 0, bank[2 * n:2 * n + 2])

            turn_norm("mlp2")
            pe.wait_ge(sem("out2_r"), 4)
            ffn("ff", U_FF2, FF2 // FM, 3, 2, FM, 4, 0, done=DONE_MOE, rows_ready=normed("mlp2"))

        @block.scalar
        def _(sc):
            A = nc.scalar.activation

            def split_hi(c, i):
                sc.wait_ge(raw_full[(c // 2) % RAW], 16 * (c // ROUND + 1) + 16 * i)
                if c >= SPLIT:
                    sc.wait_ge(unit_used, c - SPLIT + 1 + ROUND * i)
                A(wh[:, c % SPLIT, :], raw[:, (c // 2) % RAW, (c % 2) * UNIT:(c % 2 + 1) * UNIT], ACT.Copy).then_inc(hi_done, 1)

            def follow(c, n, i):
                for u in range(c, c + n):
                    if u + SPLIT < TOTAL:
                        split_hi(u + SPLIT, i)
                    else:
                        sc.wait_ge(unit_used, u + 1 + ROUND * i)

            def followed(c, n, i, step):
                follow(c, n - 1, i)
                sc.wait_ge(unit_used, c + n + ROUND * i)
                step()
                follow(c + n - 1, 1, i)

            def norm(tag, ready, n, after=0):
                for t in range(NT):
                    sc.wait_ge(sem(ready), n - (NT - 1 - t) * after)
                    A(xn[:, t, :], x[:, t, :], ACT.Square, accum_out=ss[:, t:t + 1]).then_inc(sem("norm_ss"), 1)
                sc.wait_ge(sem("norm_rs"), NT * nth(tag) + 2)
                A(xn[:, 1, 0:WIDE], x[:, 1, 0:WIDE], ACT.Copy, scale=rs[:, 1:2]).then_inc(sem("norm_xn"), 1)
                for k in range(KD):
                    sc.wait_ge(sem("norm_T"), KD * nth(tag) + bank_end(k, KD))
                    A(xth[:, k, :], bank[4 + k // 2][:, (k % 2) * 256:(k % 2 + 1) * 256], ACT.Copy, scale=col(tag, k))\
                        .then_inc(sem("norm_hi"), 1)

            def ffn(tag, c0, nf, U, loops, width, nd, i0, f0=0, nt=NT, early=None, late=None, done=0):
                nj = width // P
                ug = 4

                def evac(fc, fv):
                    for t in range(nt):
                        if nd == 2:
                            A(ebuf[:, t, 0:FG], bank[t][:, 0:FG], ACT.Tanh, scale=0.5).then_inc(sem(tag + "_e"), 1)
                        else:
                            A(ebuf[:, t, :], bank[t][:, :], ACT.Relu).then_inc(sem(tag + "_e"), 1)

                def turned(fc, fv):
                    for t in range(nt):
                        sc.wait_ge(sem(tag + "_hT"), done + nt * fc + t + 1 + fv * nt)
                        A(hth[:, 0:nj, t * P:(t + 1) * P], bank[2 + t][:, 0:width].rearrange("p (j n) -> p j n", j=nj),
                          ACT.Copy).then_inc(sem(tag + "_hTh"), 1)

                fb = nf * f0
                followed(c0, ug, i0, lambda: evac(0, fb))
                if early:
                    early()
                turned(0, fb)
                followed(c0 + ug, ug, i0, lambda: evac(1, fb))
                follow(c0 + 2 * ug, nd, i0)
                turned(1, fb)
                c = c0 + 2 * ug + nd
                with sc.Fori(0, loops) as it:
                    ii = i0 + it * (U * (ug + nd) // ROUND)
                    for s in range(U):
                        followed(c + s * (ug + nd), ug, ii, lambda: evac(2 + s, fb + it * U))
                        follow(c + s * (ug + nd) + ug, nd, ii)
                        turned(2 + s, fb + it * U)
                c += loops * U * (ug + nd)
                for f in range(2 + loops * U, nf):
                    followed(c, ug, i0, lambda: evac(f, fb))
                    follow(c + ug, nd, i0)
                    turned(f, fb)
                    c += ug + nd
                if late:
                    late[0]()
                    followed(c, nd, i0, late[1])
                else:
                    follow(c, nd, i0)

            sc.wait_ge(sem("cols_in"), 16)
            norm("mix0", "x_in", 16)
            for c in range(SPLIT):
                split_hi(c, 0)
            sc.wait_ge(sem("rel_c"), NB2)
            sc.dma_start(scratch[0:NB2 * P, :].rearrange("(h p) n -> p h n", p=P), act[:, 0, 0:NB2 * WIDE].rearrange("p (h n) -> p h n", h=NB2))\
              .then_inc(sem("rel_st"), 16)
            sc.wait_ge(sem("ang"), 1)
            A(trig[:, :, :, :], trig[:, :, :, :], ACT.Sin).then_inc(sem("trig"), 1)
            sc.wait_ge(sem("rel_st"), 16)

            def first_tap(half):
                ks = range(4 * half, 4 * half + 4)
                for k in ks:
                    sc.wait_ge(sem("cv_T"), 8 * half + bank_end(k % 4, 4))
                    A(vp[:, k, 2:258], bank[6 + k % 4 // 2][:, (k % 2) * 256:(k % 2 + 1) * 256], ACT.Copy).then_inc(sem("cv_p"), 1)
                sc.wait_ge(sem("cv_z"), 1)
                for k in ks:
                    sc.wait_ge(sem("cv_p"), k + 1)
                    A(cv[:, k, :], vp[:, k, 0:256], ACT.Copy, scale=col("conv", k)).then_inc(sem("cv_0"), 1)

            def conv_hi(half):
                for k in range(4 * half, 4 * half + 4):
                    sc.wait_ge(sem("cv_y"), k + 1)
                    A(xth[:, k, :], cv[:, k, :], ACT.Copy).then_inc(sem("cv_hi"), 1)

            for j, chunk in enumerate(CONV_CHUNKS):
                follow(U_IN + 4 * j, 4, 0)
                for t in range(NT):
                    A(act[:, t, chunk * WIDE:(chunk + 1) * WIDE], bank[2 * (j % 3) + t][:, :], ACT.Copy).then_inc(sem("in_c"), 1)
                if j == 3:
                    first_tap(0)
            conv_hi(0)
            first_tap(1)
            conv_hi(1)
            follow(U_OUT, 8, 0)

            norm("ffn0", "out_r", 4, 1)
            ffn("ff", U_FF1, FF1 // FG, 2, 4, FG, 2, 0)

            norm("mix1", "f1_r", 4, 2)
            follow(U_DOWN, 4, 0)
            for t in range(NT):
                A(down[:, t, 0:WIDE], bank[t][:, :], ACT.Copy).then_inc(sem("down_c"), 1)
            sc.wait_ge(sem("down_c"), 2)
            for t in range(NT):
                A(xn[:, t, 0:QR], down[:, t, 0:QR], ACT.Square, accum_out=ss[:, t:t + 1]).then_inc(sem("lora_ss"), 1)
            follow(U_DOWN + 4, 2, 0)
            for t in range(NT):
                A(down[:, t, WIDE:704], bank[2 + t][:, 0:192], ACT.Copy).then_inc(sem("down_c"), 1)
            sc.wait_ge(sem("down_c"), 4)
            for t in range(NT):
                A(xn[:, t, QR:QR + KVR], down[:, t, QR:QR + KVR], ACT.Square, accum_out=ss[:, NT + t:NT + t + 1])\
                    .then_inc(sem("lora_ss"), 1)
            for k in range(5):
                sc.wait_ge(sem("lora_T"), bank_end(k, 5))
                A(xth[:, k, :], bank[4 + k // 2][:, (k % 2) * 256:(k % 2 + 1) * 256], ACT.Copy,
                  scale=col("qa", k) if k < 3 else col("kva", k - 3)).then_inc(sem("lora_hi"), 1)
            def scale_q(heads):
                for h in heads:
                    for t in range(NT):
                        A(qv[:, t, h, 0:NOPE], qv[:, t, h, 0:NOPE], ACT.Copy, scale=rs[:, 8 * t + h:8 * t + h + 1])\
                            .then_inc(sem("q_ready"), 1)

            for n in range(7):
                if n < 3:
                    follow(U_UQ + 2 * n, 2, 0)
                else:
                    follow(U_UKV + n - 3, 1, 0)
                for t in range(NT):
                    A(act[:, t, n * WIDE:(n + 1) * WIDE], bank[2 * (n % 2) + t][:, :], ACT.Copy).then_inc(sem("quv_c"), 1)
                if n == 2:
                    sc.wait_ge(sem("quv_c"), 6)
                    sc.wait_ge(sem("kr1"), 1)
                    for t in range(NT):
                        A(sq[:, t, :], act[:, t, 0:NH * QH], ACT.Square).then_inc(sem("q_sq"), 1)
                if n > 2:
                    j = n - 3
                    sc.wait_ge(sem("quv_c"), 2 * n + 2)
                    if j > 1:
                        sc.wait_ge(sem("k_sr"), j - 1)
                    A(ksq[:, j % 2, :, :, :], kvv[:, :, 2 * j:2 * j + 2, 0:NOPE], ACT.Square).then_inc(sem("k_sq"), 1)
                if n == 5:
                    sc.wait_ge(sem("qk_rs"), 1)
                    scale_q(range(0, 4))
            scale_q(range(4, NH))
            for p in range(0, 12, 2):
                n = QK_ORDER[p]
                sc.wait_ge(sem("qk_T"), p + 1)
                g = {"scale": col("qn")} if n < 4 else {"scale": col("kn")} if n < 8 else {}
                A(wide[:, n * WIDE:(n + 1) * WIDE], bank[n % 8][:, :], ACT.Copy, **g).then_inc(sem("qkT_a"), 1)
            for s in range(NH + 3):
                if s < NH:
                    h = s
                    sc.wait_ge(sem("head_nm"), h + 1)
                    for qb, (a, n) in enumerate(((0, P), (P, 2 * P))):
                        A(ebuf[:, h % 2, a:a + n], ebuf[:, h % 2, a:a + n], ACT.Exp,
                          bias=small[:, 64 + 2 * (h % 2) + qb:65 + 2 * (h % 2) + qb],
                          accum_out=small[:, 72 + 2 * (h % 2) + qb:73 + 2 * (h % 2) + qb]).then_inc(sem("head_e"), 1)
                if 1 <= s <= NH:
                    h = s - 1
                    sc.wait_ge(sem("head_PT"), h + 1)
                    if h >= 2:
                        sc.wait_ge(sem("head_O"), h - 1)
                    A(hbuf[:, h % 2, 0:384], bank[2 + h % 2][:, 0:384], ACT.Copy).then_inc(sem("head_pT"), 1)
                if s >= 3:
                    h = s - 3
                    sc.wait_ge(sem("head_O"), h + 1)
                    A(xth[:, h, :], bank[4 + h % 2][:, 0:256], ACT.Copy).then_inc(sem("head_oh"), 1)
            follow(U_WO, 8, 0)

            A(rth[:, :], cols[:, COLS["router"]:COLS["router"] + 64], ACT.Copy).then_inc(sem("rt_h"), 1)
            norm("ffn1", "wo_r", 4, 1)
            for t in range(NT):
                sc.wait_ge(sem("rt_m"), t + 1)
                A(small[:, 32 * t:32 * t + NE], small[:, 32 * t:32 * t + NE], ACT.Exp,
                  bias=small[:, 32 * t + 8:32 * t + 9], accum_out=small[:, 32 * t + 9:32 * t + 10]).then_inc(sem("rt_e"), 1)

            def gathered(lot):
                for k in range(KD):
                    if k % 4 == 0:
                        sc.wait_ge(sem("moe_g"), lot * 2 + k // 4 + 1)
                    A(xth[:, k, 0:P], bank[6 + k // 4][:, (k % 4) * P:(k % 4 + 1) * P], ACT.Copy, scale=col("ffn1", k))\
                        .then_inc(sem("moe_gh"), 1)

            def turned_sel(e):
                sc.wait_ge(sem("moe_selT"), e + 1)
                A(selt[:, :], bank[5][:, 0:TOK], ACT.Copy).then_inc(sem("moe_selc"), 1)

            def outputs():
                for n in range(2):
                    A(xth[:, 4 * n:4 * n + 4, P:TOK], bank[4 + n][:, :].rearrange("p (k n) -> p k n", k=4), ACT.Copy)\
                        .then_inc(sem("moe_yh"), 1)

            gathered(0)
            with sc.Fori(0, NE) as e:
                ffn("ff", U_MOE, FFE // FG, 2, 3, FG, 2, e * 4, e, nt=1, done=DONE_FF1, early=lambda: turned_sel(e),
                    late=(lambda: gathered(e + 1), outputs))

            sc.wait_ge(sem("order"), 1)
            sc.wait_ge(sem("moe_go"), 4 * NE + 4)
            passes = sc.value_load(order[0:1, 8:9], min_val=0, max_val=3)
            with sc.If(passes > 0):
                with sc.Fori(0, passes) as v:
                    for b in range(2):
                        sc.wait_ge(sem("o_g"), v * 2 + b + 1)
                        for k in range(4 * b, 4 * b + 4):
                            last = A(oxt[:, k, :], bank[6 + b][:, (k % 4) * P:(k % 4 + 1) * P], ACT.Copy, scale=col("ffn1", k))
                        last.then_inc(sem("o_xt"), 1)
                    sc.wait_ge(sem("o_selT"), v + 1)
                    A(oselt, bank[3][:, 0:TOK], ACT.Copy)
                    for f in range(8):
                        sc.wait_ge(sem("o_gu"), v * 8 + f + 1)
                        A(ebuf[:, 0, 0:FG], bank[0][:, 0:FG], ACT.Tanh, scale=0.5).then_inc(sem("o_e"), 1)
                        sc.wait_ge(sem("o_hT"), v * 8 + f + 1)
                        A(oht[:, :, :], bank[2][:, 0:FG].rearrange("p (j n) -> p j n", j=2), ACT.Copy).then_inc(sem("o_hc"), 1)
                    sc.wait_ge(sem("o_d"), v * 8 + 8)
                    for n in range(2):
                        A(oy[:, n * WIDE:(n + 1) * WIDE], bank[4 + n][:, :], ACT.Copy).then_inc(sem("o_y"), 1)

            norm("attn2", "moe_all", 1)
            for h in range(NB2):
                for qb in range(2):
                    at = h * P * WIDE + TOK - 1 - P * qb
                    src = scratch.rearrange("r n -> (r n)")[at:at + P * (WIDE - 1)]
                    sc.dma_start(bias2[:, h, qb, :], src.rearrange("(p n) -> p n", p=P)[:, 0:256]).then_inc(sem("bias_in"), 16)
            for n in range(5):
                w = WIDE if n < 4 else 256
                follow(U_IN2 + 4 * n, 4 if n < 4 else 2, 0)
                for t in range(NT):
                    A(act[:, t, n * WIDE:n * WIDE + w], bank[2 * (n % 2) + t][:, 0:w], ACT.Copy).then_inc(sem("in2_c"), 1)
                if n == 3:
                    sc.wait_ge(sem("in2_c"), 8)
                    for t in range(NT):
                        A(bsq[:, t, :], act[:, t, 768:1792], ACT.Square).then_inc(sem("b_sq"), 1)
            sc.wait_ge(sem("lam_s"), 2)
            A(lam[:, 2:4], lam[:, 0:2], ACT.Exp).then_inc(sem("lam_e"), 1)
            for g in range(5):
                sc.wait_ge(sem("h2_T"), bank_end(g, 5))
                A(hT2[:, g, :], bank[g // 2][:, (g % 2) * 256:(g % 2 + 1) * 256], ACT.Copy).then_inc(sem("h2T_c"), 1)
            for s in range(NH + 3):
                if s < NH:
                    h = s
                    sc.wait_ge(sem("head_nm"), NH + h + 1)
                    if h >= 2:
                        sc.wait_ge(sem("head_PT"), NH + h - 1)
                    for qb in range(2):
                        A(ebuf[:, h % 2, qb * 256:(qb + 1) * 256], bank[h % 2][:, qb * 256:(qb + 1) * 256], ACT.Exp,
                          scale=HD ** -0.5, bias=small[:, 64 + 2 * (h % 2) + qb:65 + 2 * (h % 2) + qb],
                          accum_out=small[:, 72 + 2 * (h % 2) + qb:73 + 2 * (h % 2) + qb]).then_inc(sem("head_e"), 1)
                if 1 <= s <= NH:
                    h = s - 1
                    sc.wait_ge(sem("head_PT"), NH + h + 1)
                    if h >= 2:
                        sc.wait_ge(sem("head_O"), NH + h - 1)
                    A(hbuf[:, h % 2, :], bank[2 + h % 2][:, :], ACT.Copy).then_inc(sem("head_pT"), 1)
                if s >= 4 and s % 2 == 0:
                    j = (s - 4) // 2
                    sc.wait_ge(sem("head_O"), NH + 2 * j + 2)
                    A(xth[:, j, :], bank[4 + j % 2][:, 0:256], ACT.Copy).then_inc(sem("head_oh"), 1)
            for g in range(8):
                sc.wait_ge(sem("h2_T"), 5 + bank_end(g, 8))
                A(hT2[:, 5 + g, :], bank[g // 2][:, (g % 2) * 256:(g % 2 + 1) * 256], ACT.Copy,
                  scale=col("bq" if g < 4 else "bk")).then_inc(sem("h2T_c"), 1)
            for s in range(NB2 + 1):
                if s < NB2:
                    h = s
                    for c in range(2):
                        sc.wait_ge(sem("b_nm"), 2 * h + c + 1)
                        for qb in range(2):
                            m = 4 * (h % 2) + 2 * c + qb
                            A(act[:, h % 2, 2304 + c * 512 + qb * 256:2304 + c * 512 + (qb + 1) * 256],
                              act[:, h % 2, 2304 + c * 512 + qb * 256:2304 + c * 512 + (qb + 1) * 256],
                              ACT.Exp, bias=small[:, 80 + m:81 + m], accum_out=small[:, 96 + m:97 + m]).then_inc(sem("b_e"), 1)
                if s >= 1:
                    h = s - 1
                    sc.wait_ge(sem("b_PT"), h + 1)
                    if h >= 1:
                        sc.wait_ge(sem("b_O"), h)
                    A(hbuf[:, 1, :], bank[4 + h % 2][:, :], ACT.Copy).then_inc(sem("b_pT"), 1)
                    sc.wait_ge(sem("b_O"), h + 1)
                    for t in range(NT):
                        A(xn[:, t, h * P:(h + 1) * P], bank[6 + h % 2][:, t * P:(t + 1) * P], ACT.Square,
                          accum_out=ss[:, 2 * h + t:2 * h + t + 1]).then_inc(sem("ob_ss"), 1)
            for h in range(NB2):
                sc.wait_ge(sem("ob_T"), bank_end(h, NB2))
                sc.wait_ge(sem("sub_g"), 1)
                A(xth[:, 4 + h, :], bank[4 + h // 2][:, (h % 2) * 256:(h % 2 + 1) * 256], ACT.Copy, scale=lam[:, 5:6])\
                    .then_inc(sem("ob_h"), 1)
            follow(U_OUT2, 8, 0)

            norm("mlp2", "out2_r", 4, 1)
            ffn("ff", U_FF2, FF2 // FM, 3, 2, FM, 4, 0, done=DONE_MOE)

        @block.vector
        def _(dv):
            V = nc.vector
            chain = [0]
            dve_chain = sem("dve_chain")

            def link(ins):
                chain[0] += 1
                ins.then_inc(dve_chain, 1)
                dv.wait_ge(dve_chain, chain[0])

            def mark(ins):
                chain[0] += 1
                ins.then_inc(dve_chain, 1)

            def split_lo(c, i):
                dv.wait_ge(hi_done, c + 1 + ROUND * i)
                V.tensor_tensor(wl[:, c % SPLIT, :], raw[:, (c // 2) % RAW, (c % 2) * UNIT:(c % 2 + 1) * UNIT],
                                f32(wh[:, c % SPLIT, :]), ALU.subtract).then_inc(lo_done, 1)

            def follow(c, n, i):
                for u in range(c, c + n):
                    if u + SPLIT < TOTAL:
                        split_lo(u + SPLIT, i)
                    else:
                        dv.wait_ge(unit_used, u + 1 + ROUND * i)

            def followed(c, n, i, step):
                follow(c, n - 1, i)
                step()
                follow(c + n - 1, 1, i)

            def norm(tag):
                dv.wait_ge(sem("norm_rs"), NT * nth(tag) + 1)
                V.tensor_scalar(xn[:, 0, :], x[:, 0, :], rs[:, 0:1], None, ALU.mult).then_inc(sem("norm_x0"), 1)
                dv.wait_ge(sem("norm_rs"), NT * nth(tag) + 2)
                V.tensor_scalar(xn[:, 1, WIDE:D], x[:, 1, WIDE:D], rs[:, 1:2], None, ALU.mult).then_inc(sem("norm_xn"), 1)
                for k in range(KD):
                    dv.wait_ge(sem("norm_hi"), KD * nth(tag) + bank_end(k, KD))
                    V.scalar_tensor_tensor(out=xtl[:, k, :], in0=bank[4 + k // 2][:, (k % 2) * 256:(k % 2 + 1) * 256],
                                           scalar=col(tag, k), in1=f32(xth[:, k, :]), op0=ALU.mult, op1=ALU.subtract)\
                     .then_inc(sem("norm_l"), 1)

            def residual(c0, tag):
                for n in range(2):
                    follow(c0 + 4 * n, 3, 0)
                    dv.wait_ge(unit_used, c0 + 4 * n + 4)
                    for t in range(NT):
                        V.tensor_tensor(x[:, t, n * WIDE:(n + 1) * WIDE], x[:, t, n * WIDE:(n + 1) * WIDE],
                                        bank[2 * n + t][:, :], ALU.add).then_inc(sem(tag), 1)
                    follow(c0 + 4 * n + 3, 1, 0)

            def ffn(tag, c0, nf, U, loops, width, nd, i0, f0=0, nt=NT, early=None, late=None, done=0, finish=None):
                nj = width // P
                ug = 4

                def evac(fc, fv):
                    for t in range(nt):
                        dv.wait_ge(sem(tag + "_e"), done + nt * fc + t + 1 + fv * nt)
                        if nd == 2:
                            step = sem(tag + "_s")
                            e, g, u, h = ebuf[:, t, 0:FG], bank[t][:, 0:FG], bank[t][:, FG:2 * FG], hbuf[:, t, 0:FG]
                            V.scalar_tensor_tensor(out=e, in0=e, scalar=1.0, in1=g, op0=ALU.add, op1=ALU.mult).then_inc(step, 1)
                            dv.wait_ge(step, done + nt * fc + t + 1 + fv * nt)
                            V.scalar_tensor_tensor(out=h, in0=e, scalar=0.5, in1=u, op0=ALU.mult, op1=ALU.mult)\
                             .then_inc(sem(tag + "_h"), 1)
                        else:
                            V.tensor_tensor(hbuf[:, t, :], ebuf[:, t, :], ebuf[:, t, :], ALU.mult).then_inc(sem(tag + "_h"), 1)

                def turned(fc, fv):
                    for t in range(nt):
                        dv.wait_ge(sem(tag + "_hTh"), done + nt * fc + t + 1 + fv * nt)
                        V.tensor_tensor(htl[:, 0:nj, t * P:(t + 1) * P], bank[2 + t][:, 0:width].rearrange("p (j n) -> p j n", j=nj),
                                        f32(hth[:, 0:nj, t * P:(t + 1) * P]), ALU.subtract).then_inc(sem(tag + "_hTl"), 1)

                fb = nf * f0
                followed(c0, ug, i0, lambda: evac(0, fb))
                if early:
                    early()
                turned(0, fb)
                followed(c0 + ug, ug, i0, lambda: evac(1, fb))
                follow(c0 + 2 * ug, nd, i0)
                turned(1, fb)
                c = c0 + 2 * ug + nd
                with dv.Fori(0, loops) as it:
                    ii = i0 + it * (U * (ug + nd) // ROUND)
                    for s in range(U):
                        followed(c + s * (ug + nd), ug, ii, lambda: evac(2 + s, fb + it * U))
                        follow(c + s * (ug + nd) + ug, nd, ii)
                        turned(2 + s, fb + it * U)
                c += loops * U * (ug + nd)
                for f in range(2 + loops * U, nf):
                    followed(c, ug, i0, lambda: evac(f, fb))
                    follow(c + ug, nd, i0)
                    turned(f, fb)
                    c += ug + nd
                if late:
                    late[0]()
                    followed(c, nd, i0, late[1])
                else:
                    follow(c, nd - 1, i0)
                    dv.wait_ge(unit_used, c + nd + ROUND * i0)
                    finish()
                    follow(c + nd - 1, 1, i0)

            def rotate(dst, src, cs, sn, heads, t):
                def b3(ap):
                    return ap[:, None, :].to_broadcast((P, heads, 32))
                a, b = src[:, :, 0:32], src[:, :, 32:64]
                t1, t2, t3, t4 = (b[:, r, 0:heads * 32].rearrange("p (h d) -> p h d", h=heads) for b in (ebuf, hbuf) for r in range(2))
                mark(V.tensor_tensor(t1, a, b3(cs), ALU.mult))
                mark(V.tensor_tensor(t2, b, b3(sn), ALU.mult))
                mark(V.tensor_tensor(t3, b, b3(cs), ALU.mult))
                link(V.tensor_tensor(t4, a, b3(sn), ALU.mult))
                mark(V.tensor_tensor(dst[:, :, 0:32], t1, t2, ALU.subtract))
                link(V.tensor_tensor(dst[:, :, 32:64], t3, t4, ALU.add))

            dv.wait_ge(sem("rel_in"), 32)
            V.tensor_copy(relw[:, :, :], relb[:, :, None].to_broadcast((BUCKETS, NB2, P))).then_inc(sem("rel_w"), 1)
            for h in range(NB2):
                dv.wait_ge(sem("rel_T"), h + 1)
                V.tensor_copy(act[:, 0, h * WIDE:(h + 1) * WIDE], bank[h][:, :]).then_inc(sem("rel_c"), 1)
            dv.wait_ge(sem("cols_in"), 16)
            norm("mix0")
            for c in range(SPLIT):
                split_lo(c, 0)
            dv.wait_ge(sem("pos_in"), 16)
            dv.wait_ge(sem("fixed_in"), 16)
            dv.wait_ge(sem("rows_in"), 16)
            link(V.tensor_copy(posf[:, :], posi[:, :]))
            ang = sq[:, 0, 0:64].rearrange("p (t n) -> p t n", t=NT)
            for t in range(NT):
                link(V.tensor_scalar(ang[:, t, :], fixed[:, FIXED["freq"]:FIXED["freq"] + 32], posf[:, t:t + 1], None, ALU.mult))
            for w, quarter in ((0, 0.25), (1, 0.0)):
                turns = sq[:, 0, 64 + 64 * w:128 + 64 * w].rearrange("p (t n) -> p t n", t=NT)
                link(V.tensor_scalar(turns, ang, 1.0 / TWO_PI, quarter, ALU.mult, ALU.add))
                link(V.tensor_scalar(turns, turns, ROUNDER, None, ALU.add))
                link(V.tensor_scalar(turns, turns, ROUNDER, None, ALU.subtract))
                r = trig[:, w, :, :]
                link(V.scalar_tensor_tensor(out=r, in0=turns, scalar=-PI_A, in1=ang, op0=ALU.mult, op1=ALU.add))
                link(V.scalar_tensor_tensor(out=r, in0=turns, scalar=-PI_B, in1=r, op0=ALU.mult, op1=ALU.add))
                link(V.scalar_tensor_tensor(out=r, in0=turns, scalar=-PI_C, in1=r, op0=ALU.mult, op1=ALU.add))
                link(V.tensor_scalar(r, r, quarter * TWO_PI, PI_IN, ALU.add, ALU.min))
                if w == 0:
                    link(V.tensor_scalar(r, r, -PI_IN, None, ALU.max))
                else:
                    V.tensor_scalar(r, r, -PI_IN, None, ALU.max).then_inc(sem("ang"), 1)
            V.memset(vp[:, :, 0:2], 0.0).then_inc(sem("cv_z"), 1)

            def v_half(half):
                a, b = half * WIDE, (half + 1) * WIDE
                V.tensor_tensor(xn[:, :, a:b], act[:, :, D + a:D + b], act[:, :, 2 * D + a:2 * D + b], ALU.mult)\
                 .then_inc(sem("cv_v"), 1)

            def taps(k):
                v = cv[:, k, :]
                dv.wait_ge(sem("cv_0"), k + 1)
                link(V.scalar_tensor_tensor(out=v, in0=vp[:, k, 1:257], scalar=col("conv", 8 + k), in1=v, op0=ALU.mult, op1=ALU.add))
                link(V.scalar_tensor_tensor(out=v, in0=vp[:, k, 2:258], scalar=col("conv", 16 + k), in1=v, op0=ALU.mult, op1=ALU.add))
                dv.wait_ge(sem("cv_T"), 8 * (k // 4) + 4 + bank_end(k % 4, 4))
                V.tensor_tensor(v, v, bank[(2 if k >= 4 else 6) + k % 4 // 2][:, (k % 2) * 256:(k % 2 + 1) * 256], ALU.mult)\
                 .then_inc(sem("cv_y"), 1)

            def conv_lo(k):
                dv.wait_ge(sem("cv_hi"), k + 1)
                V.tensor_tensor(xtl[:, k, :], cv[:, k, :], f32(xth[:, k, :]), ALU.subtract).then_inc(sem("cv_l"), 1)

            for j in range(6):
                follow(U_IN + 4 * j, 4, 0)
                if j == 2:
                    dv.wait_ge(sem("in_c"), 4)
                    v_half(0)
                if j == 4:
                    for k in range(4):
                        taps(k)
                    dv.wait_ge(sem("in_c"), 10)
                    v_half(1)
            for k in range(4):
                conv_lo(k)
            taps(4)
            for k in range(5, KD):
                taps(k)
                conv_lo(k - 1)
            conv_lo(KD - 1)
            residual(U_OUT, "out_r")

            def add_sums(tag):
                for t in range(NT):
                    V.tensor_tensor(x[:, t, :].rearrange("p (n c) -> p n c", n=2)[:, 0, :], x[:, t, 0:WIDE], bank[4 + 2 * t][:, :],
                                    ALU.add).then_inc(sem(tag), 1)
                    V.tensor_tensor(x[:, t, WIDE:D], x[:, t, WIDE:D], bank[5 + 2 * t][:, :], ALU.add).then_inc(sem(tag), 1)

            norm("ffn0")
            ffn("ff", U_FF1, FF1 // FG, 2, 4, FG, 2, 0, finish=lambda: add_sums("f1_r"))

            norm("mix1")
            follow(U_DOWN, 6, 0)
            dv.wait_ge(sem("lora_rs"), 1)
            for t in range(NT):
                V.tensor_scalar(xn[:, t, 0:QR], down[:, t, 0:QR], rs[:, t:t + 1], None, ALU.mult).then_inc(sem("lora_xn"), 1)
                V.tensor_scalar(xn[:, t, QR:QR + KVR], down[:, t, QR:QR + KVR], rs[:, NT + t:NT + t + 1], None, ALU.mult)\
                 .then_inc(sem("lora_xn"), 1)
            for k in range(5):
                dv.wait_ge(sem("lora_hi"), bank_end(k, 5))
                V.scalar_tensor_tensor(out=xtl[:, k, :], in0=bank[4 + k // 2][:, (k % 2) * 256:(k % 2 + 1) * 256],
                                       scalar=col("qa", k) if k < 3 else col("kva", k - 3), in1=f32(xth[:, k, :]),
                                       op0=ALU.mult, op1=ALU.subtract).then_inc(sem("lora_l"), 1)
            dv.wait_ge(sem("trig"), 1)
            krs = down[:, :, 640:704]
            link(V.tensor_tensor(sq[:, 0, 0:128].rearrange("p (t d) -> p t d", t=NT), krs, krs, ALU.mult))
            link(V.tensor_reduce(ss[:, 32:34], sq[:, 0, 0:128].rearrange("p (t d) -> p t d", t=NT), AX.X, ALU.add))
            link(V.tensor_tensor(krs, krs, rows[:, None, ROWS["kr"]:ROWS["kr"] + 64].to_broadcast((P, NT, 64)), ALU.mult))
            for t in range(NT):
                rotate(kr1[:, t:t + 1, :], down[:, t:t + 1, 640:704], trig[:, 0, t, :], trig[:, 1, t, :], 1, t)
            dv.sem_inc(sem("kr1"), 1)
            def k_sums(j):
                c = 16 + 4 * j
                dv.wait_ge(sem("k_sq"), j + 1)
                V.tensor_reduce(ss[:, c:c + 4].rearrange("p (t h) -> p t h", t=NT), ksq[:, j % 2, :, :, :], AX.X, ALU.add)\
                 .then_inc(sem("k_sr"), 1)
                dv.wait_ge(sem("k_sr"), j + 1)
                V.tensor_tensor(ss[:, c:c + 4].rearrange("p (t h) -> p t h", t=NT),
                                ss[:, c:c + 4].rearrange("p (t h) -> p t h", t=NT),
                                ss[:, 32:34, None].to_broadcast((P, NT, 2)), ALU.add).then_inc(sem("qk_ss"), 1)

            def k_scaled(j):
                rk = rs[:, 16 + 4 * j:20 + 4 * j].rearrange("p (t h) -> p t h", t=NT)[:, :, :, None]
                dv.wait_ge(sem("qk_rs"), j + 2)
                kn = kvv[:, :, 2 * j:2 * j + 2, 0:NOPE]
                link(V.tensor_tensor(kn, kn, rk.to_broadcast((P, NT, 2, NOPE)), ALU.mult))
                V.tensor_tensor(krb[:, :, 2 * j:2 * j + 2, :], kr1[:, :, None, :].to_broadcast((P, NT, 2, 64)),
                                rk.to_broadcast((P, NT, 2, 64)), ALU.mult).then_inc(sem("k_ready"), 1)

            def q_rotated(t):
                link(V.tensor_tensor(qv[:, t, :, NOPE:QH], qv[:, t, :, NOPE:QH],
                                     rows[:, None, ROWS["qr"]:ROWS["qr"] + 64].to_broadcast((P, NH, 64)), ALU.mult))
                rotate(qrb[:, t, :, :], qv[:, t, :, NOPE:QH], trig[:, 0, t, :], trig[:, 1, t, :], NH, t)

            follow(U_UQ, 6, 0)
            for t in range(NT):
                dv.wait_ge(sem("q_sq"), t + 1)
                r = V.tensor_reduce(ss[:, 8 * t:8 * t + 8], sq[:, t, :].rearrange("p (h d) -> p h d", h=NH), AX.X, ALU.add)
                if t == 0:
                    link(r)
                else:
                    r.then_inc(sem("qk_ss"), 1)
            follow(U_UKV, 1, 0)
            k_sums(0)
            q_rotated(0)
            k_sums(1)
            k_scaled(0)
            q_rotated(1)
            k_sums(2)
            k_scaled(1)
            for t in range(NT):
                link(V.tensor_tensor(qrb[:, t, :, :], qrb[:, t, :, :], rs[:, 8 * t:8 * t + 8, None].to_broadcast((P, NH, 64)),
                                     ALU.mult))
            dv.sem_inc(sem("qr_ready"), 1)
            k_sums(3)
            k_scaled(2)
            k_scaled(3)
            for p in range(1, 12, 2):
                n = QK_ORDER[p]
                dv.wait_ge(sem("qk_T"), p + 1)
                if n < 8:
                    V.tensor_scalar(wide[:, n * WIDE:(n + 1) * WIDE], bank[n % 8][:, :], col("qn" if n < 4 else "kn"), None,
                                    ALU.mult).then_inc(sem("qkT_d"), 1)
                else:
                    V.tensor_copy(wide[:, n * WIDE:(n + 1) * WIDE], bank[n % 8][:, :]).then_inc(sem("qkT_d"), 1)
            for s in range(NH + 3):
                if s < NH:
                    h = s
                    dv.wait_ge(sem("head_S"), h + 1)
                    if h >= 2:
                        dv.wait_ge(sem("head_PT"), h - 1)
                    b = h % 2
                    V.scalar_tensor_tensor(out=ebuf[:, b, 0:384], in0=bank[b][:, 0:384], scalar=QH ** -0.5, in1=maskt,
                                           op0=ALU.mult, op1=ALU.add).then_inc(sem("head_sc"), 1)
                    dv.wait_ge(sem("head_sc"), h + 1)
                    link(V.tensor_reduce(small[:, 68 + 0:68 + 1], ebuf[:, b, 0:P], AX.X, ALU.max))
                    link(V.tensor_reduce(small[:, 68 + 1:68 + 2], ebuf[:, b, P:384], AX.X, ALU.max))
                    V.tensor_scalar(small[:, 64 + 2 * b:66 + 2 * b], small[:, 68:70], -1.0, None, ALU.mult).then_inc(sem("head_nm"), 1)
                if 1 <= s <= NH:
                    h = s - 1
                    b = h % 2
                    dv.wait_ge(sem("head_e"), 2 * h + 2)
                    link(V.reciprocal(small[:, 76:78], small[:, 72 + 2 * b:74 + 2 * b]))
                    link(V.tensor_scalar(ebuf[:, b, 0:P], ebuf[:, b, 0:P], small[:, 76:77], None, ALU.mult))
                    V.tensor_scalar(ebuf[:, b, P:384], ebuf[:, b, P:384], small[:, 77:78], None, ALU.mult).then_inc(sem("head_p"), 1)
                if s >= 3:
                    h = s - 3
                    dv.wait_ge(sem("head_oh"), h + 1)
                    V.tensor_tensor(xtl[:, h, :], bank[4 + h % 2][:, 0:256], f32(xth[:, h, :]), ALU.subtract).then_inc(sem("head_ol"), 1)
            follow(U_UKV + 1, 3, 0)
            residual(U_WO, "wo_r")

            dv.wait_ge(sem("rt_h"), 1)
            V.tensor_tensor(rtl[:, :], cols[:, COLS["router"]:COLS["router"] + 64], f32(rth[:, :]), ALU.subtract).then_inc(sem("rt_l"), 1)
            norm("ffn1")
            link(V.memset(ones, 1.0))
            link(V.memset(gates[:, :, :], 0.0))
            link(V.memset(f32(selt[:, :]), 0.0))
            for t in range(NT):
                lg = small[:, 32 * t:32 * t + NE]
                mx = small[:, 32 * t + 16:32 * t + 24]
                fi = small[:, 32 * t + 24:32 * t + 32]
                dv.wait_ge(sem("rt_S"), t + 1)
                V.tensor_copy(lg, bank[t][:, 0:NE]).then_inc(sem("rt_c"), 1)
                dv.wait_ge(sem("rt_c"), t + 1)
                link(V.tensor_reduce(small[:, 32 * t + 10:32 * t + 11], lg, AX.X, ALU.max))
                V.tensor_scalar(small[:, 32 * t + 8:32 * t + 9], small[:, 32 * t + 10:32 * t + 11], -1.0, None, ALU.mult)\
                 .then_inc(sem("rt_m"), 1)
                dv.wait_ge(sem("rt_e"), t + 1)
                link(V.reciprocal(small[:, 32 * t + 11:32 * t + 12], small[:, 32 * t + 9:32 * t + 10]))
                link(V.tensor_scalar(lg, lg, small[:, 32 * t + 11:32 * t + 12], None, ALU.mult))
                link(V.max(mx, lg))
                link(V.max_index(topi[:, t, :], mx, lg))
                link(V.tensor_copy(fi, topi[:, t, :]))
                link(V.tensor_tensor(small[:, 32 * t + 12:32 * t + 13], mx[:, 0:1], mx[:, 1:2], ALU.add))
                link(V.reciprocal(small[:, 32 * t + 13:32 * t + 14], small[:, 32 * t + 12:32 * t + 13]))
                link(V.tensor_scalar(mx[:, 0:2], mx[:, 0:2], small[:, 32 * t + 13:32 * t + 14], None, ALU.mult))
                io = fixed[:, FIXED["iota"]:FIXED["iota"] + 8]
                link(V.tensor_scalar(lg, io, fi[:, 0:1], mx[:, 0:1], ALU.is_equal, ALU.mult))
                link(V.tensor_scalar(gates[:, t, 1:NE + 1], io, fi[:, 1:2], mx[:, 1:2], ALU.is_equal, ALU.mult))
                link(V.tensor_tensor(gates[:, t, 1:NE + 1], gates[:, t, 1:NE + 1], lg, ALU.add))
                link(V.tensor_scalar(lg, io, fi[:, 0:1], None, ALU.is_equal))
                link(V.memset(chosen[:, t, :], 0.0))
                V.scalar_tensor_tensor(out=chosen[:, t, 0:NE], in0=io, scalar=fi[:, 1:2], in1=lg, op0=ALU.is_equal,
                                       op1=ALU.add).then_inc(sem("chosen"), 1)
            link(V.memset(place[:, :, :], 0.0))
            dv.wait_ge(sem("places"), 1)
            link(V.tensor_copy(place[:, :, 0:NE], bank[0][:, 0:32].rearrange("p (t n) -> p t n", t=NT)[:, :, 0:NE]))
            link(V.tensor_copy(queue[:, 0:NE], bank[0][:, 32:32 + NE]))

            slots = fixed[:, FIXED["slots"]:FIXED["slots"] + P]
            every = fixed[:, FIXED["every"]:FIXED["every"] + P]

            def gathered(lot):
                for k in range(KD):
                    dv.wait_ge(sem("moe_gh"), lot * KD + k // 4 * 4 + 4)
                    V.scalar_tensor_tensor(out=xtl[:, k, 0:P], in0=bank[6 + k // 4][:, (k % 4) * P:(k % 4 + 1) * P],
                                           scalar=col("ffn1", k), in1=f32(xth[:, k, 0:P]), op0=ALU.mult, op1=ALU.subtract)\
                     .then_inc(sem("moe_gl"), 1)

            for t in range(NT):
                ins = V.tensor_scalar(sel[:, t, :], slots, place[:, t, 0:1], chosen[:, t, 0:1], ALU.is_equal, ALU.mult)
            ins.then_inc(sem("moe_sel"), 1)
            link(V.max(queue[:, NE:2 * NE], queue[:, 0:NE]))
            link(V.max_index(order[:, 0:8], queue[:, NE:2 * NE], queue[:, 0:NE]))
            link(V.tensor_scalar(queue[:, 0:NE], queue[:, 0:NE], float(CAP), None, ALU.is_gt))
            link(V.tensor_reduce(queue[:, 2 * NE:2 * NE + 1], queue[:, 0:NE], AX.X, ALU.add))
            V.tensor_copy(order[:, 8:9], queue[:, 2 * NE:2 * NE + 1]).then_inc(sem("order"), 1)
            gathered(0)
            for j in range(2):
                dv.sem_inc(sem("moe_yl"), 1)

            def next_sel(e):
                dv.wait_ge(sem("moe_selT"), e + 1)
                for t in range(NT):
                    ins = V.tensor_scalar(sel[:, t, :], slots, place[:, t, bass.ds(e + 1, 1)], chosen[:, t, bass.ds(e + 1, 1)],
                                          ALU.is_equal, ALU.mult)
                ins.then_inc(sem("moe_sel"), 1)

            def add_scattered(e):
                for t in range(NT):
                    gate = gates[:, t, bass.ds(e, 1)] if not isinstance(e, int) else gates[:, t, e:e + 1]
                    for n in range(2):
                        dv.wait_ge(sem("moe_S"), e * 4 + 2 * t + n + 1)
                        V.scalar_tensor_tensor(out=x[:, t, n * WIDE:(n + 1) * WIDE], in0=bank[(1, 3, 6, 7)[2 * t + n]][:, :],
                                               scalar=gate, in1=x[:, t, n * WIDE:(n + 1) * WIDE], op0=ALU.mult, op1=ALU.add)\
                         .then_inc(sem("moe_go"), 1)

            def outputs(e):
                for n in range(2):
                    dv.wait_ge(sem("moe_yh"), e * 2 + n + 1)
                    V.tensor_tensor(xtl[:, 4 * n:4 * n + 4, P:TOK], bank[4 + n][:, :].rearrange("p (k n) -> p k n", k=4),
                                    f32(xth[:, 4 * n:4 * n + 4, P:TOK]), ALU.subtract).then_inc(sem("moe_yl"), 1)

            def add_and_select(e):
                add_scattered(e)
                next_sel(e)

            with dv.Fori(0, NE) as e:
                ffn("ff", U_MOE, FFE // FG, 2, 3, FG, 2, e * 4, e, nt=1, done=DONE_FF1, early=lambda: add_and_select(e),
                    late=(lambda: gathered(e + 1), lambda: outputs(e)))
            add_scattered(NE)
            dv.wait_ge(sem("moe_go"), 4 * NE + 4)
            passes = dv.value_load(order[0:1, 8:9], min_val=0, max_val=3)
            with dv.If(passes > 0):
                with dv.Fori(0, passes) as v:
                    e = dv.value_load(order[0:1, bass.ds(v, 1)], min_val=0, max_val=NE - 1)
                    at = small[:, 80:80 + NT]
                    for t in range(NT):
                        V.tensor_scalar(at[:, t:t + 1], place[:, t, bass.ds(e, 1)], float(CAP), None, ALU.subtract)\
                         .then_inc(sem("o_at"), 1)
                    dv.wait_ge(sem("o_at"), v * 2 + 2)
                    for t in range(NT):
                        ins = V.tensor_scalar(osel[:, t, :], every, at[:, t:t + 1], chosen[:, t, bass.ds(e, 1)],
                                              ALU.is_equal, ALU.mult)
                    ins.then_inc(sem("o_sel"), 1)
                    for f in range(8):
                        g, u, h = bank[0][:, 0:FG], bank[0][:, FG:2 * FG], hbuf[:, 0, 0:FG]
                        dv.wait_ge(sem("o_e"), v * 8 + f + 1)
                        V.scalar_tensor_tensor(out=ebuf[:, 0, 0:FG], in0=ebuf[:, 0, 0:FG], scalar=1.0, in1=g, op0=ALU.add,
                                               op1=ALU.mult).then_inc(sem("o_s"), 1)
                        dv.wait_ge(sem("o_s"), v * 8 + f + 1)
                        V.scalar_tensor_tensor(out=h, in0=ebuf[:, 0, 0:FG], scalar=0.5, in1=u, op0=ALU.mult, op1=ALU.mult)\
                         .then_inc(sem("o_h"), 1)
                    for t in range(NT):
                        gate = gates[:, t, bass.ds(e + 1, 1)]
                        for n in range(2):
                            dv.wait_ge(sem("o_S"), v * 4 + 2 * t + n + 1)
                            V.scalar_tensor_tensor(out=x[:, t, n * WIDE:(n + 1) * WIDE],
                                                   in0=bank[(2, 3, 1, 4)[2 * t + n]][:, :], scalar=gate,
                                                   in1=x[:, t, n * WIDE:(n + 1) * WIDE], op0=ALU.mult, op1=ALU.add)\
                             .then_inc(sem("o_x"), 1)
                    dv.wait_ge(sem("o_x"), v * 4 + 4)
            dv.sem_inc(sem("moe_all"), 1)
            for n in range(2):
                a, b = ROWS[("lq1", "lq2")[n]], ROWS[("lk1", "lk2")[n]]
                link(V.tensor_tensor(small[:, 0:64], rows[:, a:a + 64], rows[:, b:b + 64], ALU.mult))
                V.tensor_reduce(lam[:, n:n + 1], small[:, 0:64], AX.X, ALU.add).then_inc(sem("lam_s"), 1)
                dv.wait_ge(sem("lam_s"), n + 1)
            V.tensor_scalar(lam[:, 5:6], col("sub"), 1.0 - LAMBDA0, None, ALU.mult).then_inc(sem("sub_g"), 1)
            norm("attn2")
            follow(U_IN2, 8, 0)
            dv.wait_ge(sem("in2_c"), 4)
            for t in range(NT):
                link(V.tensor_tensor(xn[:, t, 0:640], act[:, t, 0:640], act[:, t, 0:640], ALU.mult))
                r = V.tensor_reduce(ss[:, 10 * t:10 * t + 10], xn[:, t, 0:640].rearrange("p (h d) -> p h d", d=HD), AX.X, ALU.add)
                if t == 0:
                    link(r)
                else:
                    r.then_inc(sem("h2_ss"), 1)
            follow(U_IN2 + 8, 3, 0)
            dv.wait_ge(sem("h2_rs"), 1)
            for t in range(NT):
                qa = act[:, t, 0:512].rearrange("p (h d) -> p h d", d=HD)
                ka = act[:, t, 512:640].rearrange("p (h d) -> p h d", d=HD)
                both = act[:, t, 0:640].rearrange("p (h d) -> p h d", d=HD)
                link(V.tensor_tensor(both, both, rs[:, 10 * t:10 * t + 10, None].to_broadcast((P, 10, HD)), ALU.mult))
                link(V.tensor_tensor(qa, qa, rows[:, None, ROWS["aq"]:ROWS["aq"] + 64].to_broadcast((P, 8, HD)), ALU.mult))
                link(V.tensor_tensor(ka, ka, rows[:, None, ROWS["ak"]:ROWS["ak"] + 64].to_broadcast((P, 2, HD)), ALU.mult))
                C = fixed[:, FIXED["ctab"] + 64 * t:FIXED["ctab"] + 64 * (t + 1)]
                S = fixed[:, FIXED["stab"] + 64 * t:FIXED["stab"] + 64 * (t + 1)]
                sw = wide[:, 0:640].rearrange("p (h d) -> p h d", d=HD)
                for j in range(4):
                    o = (1, 0, 3, 2)[j]
                    link(V.tensor_tensor(sw[:, :, 16 * j:16 * j + 16], both[:, :, 16 * o:16 * o + 16],
                                         S[:, None, 16 * j:16 * j + 16].to_broadcast((P, 10, 16)), ALU.mult))
                link(V.tensor_tensor(both, both, C[:, None, :].to_broadcast((P, 10, HD)), ALU.mult))
                link(V.tensor_tensor(xn[:, t, 0:512].rearrange("p (j s d) -> p s j d", s=2, d=HD),
                                     act[:, t, 0:512].rearrange("p (s j d) -> p s j d", s=2, d=HD),
                                     wide[:, 0:512].rearrange("p (s j d) -> p s j d", s=2, d=HD), ALU.add))
                link(V.tensor_tensor(xn[:, t, 512:640].rearrange("p (h d) -> p h d", d=HD), ka, sw[:, 8:10, :], ALU.add))
                if t == 0:
                    follow(U_IN2 + 11, 3, 0)
            dv.sem_inc(sem("a_ready"), 1)
            follow(U_IN2 + 14, 2, 0)
            for t in range(NT):
                dv.wait_ge(sem("b_sq"), t + 1)
                r = V.tensor_reduce(ss[:, 20 + 16 * t:36 + 16 * t], bsq[:, t, :].rearrange("p (h d) -> p h d", d=HD), AX.X, ALU.add)
                if t == 0:
                    link(r)
                else:
                    r.then_inc(sem("h2_ss"), 1)
            follow(U_IN2 + 16, 2, 0)

            def b_scaled(t):
                qk = act[:, t, 768:1792].rearrange("p (h d) -> p h d", d=HD)
                link(V.tensor_tensor(qk, qk, rs[:, 20 + 16 * t:36 + 16 * t, None].to_broadcast((P, 16, HD)), ALU.mult))

            dv.wait_ge(sem("lam_e"), 1)
            link(V.tensor_tensor(lam[:, 4:5], lam[:, 3:4], lam[:, 2:3], ALU.subtract))
            link(V.tensor_scalar(lam[:, 4:5], lam[:, 4:5], LAMBDA0, None, ALU.subtract))
            for s in range(NH + 3):
                if s < NH:
                    h = s
                    b = h % 2
                    dv.wait_ge(sem("head_S"), NH + h + 1)
                    if h >= 1:
                        dv.wait_ge(sem("head_nm"), NH + h)
                    V.tensor_reduce(small[:, 68:70], bank[b][:, :].rearrange("p (q n) -> p q n", q=2), AX.X, ALU.max)\
                     .then_inc(sem("a_mx"), 1)
                    dv.wait_ge(sem("a_mx"), h + 1)
                    V.tensor_scalar(small[:, 64 + 2 * b:66 + 2 * b], small[:, 68:70], -(HD ** -0.5), None, ALU.mult)\
                     .then_inc(sem("head_nm"), 1)
                if 1 <= s <= NH:
                    h = s - 1
                    b = h % 2
                    dv.wait_ge(sem("head_e"), 2 * NH + 2 * h + 2)
                    if h >= 1:
                        dv.wait_ge(sem("head_p"), NH + h)
                    V.reciprocal(small[:, 76:78], small[:, 72 + 2 * b:74 + 2 * b]).then_inc(sem("head_sc"), 1)
                    dv.wait_ge(sem("head_sc"), NH + h + 1)
                    link(V.tensor_scalar(ebuf[:, b, 0:256], ebuf[:, b, 0:256], small[:, 76:77], None, ALU.mult))
                    V.tensor_scalar(ebuf[:, b, 256:512], ebuf[:, b, 256:512], small[:, 77:78], None, ALU.mult).then_inc(sem("head_p"), 1)
                    if h in (3, 5):
                        dv.wait_ge(sem("h2_rs"), 2)
                        b_scaled(h // 2 - 1)
                        if h == 5:
                            dv.sem_inc(sem("b_ready"), 1)
                if s >= 4 and s % 2 == 0:
                    j = (s - 4) // 2
                    dv.wait_ge(sem("head_oh"), NH + j + 1)
                    V.tensor_tensor(xtl[:, j, :], bank[4 + j % 2][:, 0:256], f32(xth[:, j, :]), ALU.subtract).then_inc(sem("head_ol"), 1)
            dv.wait_ge(sem("bias_in"), 16 * 8)
            for s in range(NB2 + 2):
                if s < NB2:
                    h = s
                    if h >= 2:
                        dv.wait_ge(sem("b_p"), h - 1)
                    for c in range(2):
                        dv.wait_ge(sem("b_S"), 2 * h + c + 1)
                        m = 4 * (h % 2) + 2 * c
                        e = act[:, h % 2, 2304 + c * 512:2304 + (c + 1) * 512]
                        V.scalar_tensor_tensor(out=e, in0=bank[2 * (h % 2) + c][:, :], scalar=HD ** -0.5,
                                               in1=bias2[:, h, :, :].rearrange("p q n -> p (q n)"), op0=ALU.mult, op1=ALU.add)\
                         .then_inc(sem("b_sc"), 1)
                        dv.wait_ge(sem("b_sc"), 2 * h + c + 1)
                        if h + c >= 1:
                            dv.wait_ge(sem("b_nm"), 2 * h + c)
                        link(V.tensor_reduce(small[:, 68:70], e.rearrange("p (q n) -> p q n", q=2), AX.X, ALU.max))
                        V.tensor_scalar(small[:, 80 + m:82 + m], small[:, 68:70], -1.0, None, ALU.mult).then_inc(sem("b_nm"), 1)
                if 1 <= s <= NB2:
                    h = s - 1
                    m = 4 * (h % 2)
                    dv.wait_ge(sem("b_e"), 4 * h + 4)
                    if h >= 1:
                        dv.wait_ge(sem("b_p"), h)
                    link(V.reciprocal(small[:, 112:116], small[:, 96 + m:100 + m]))
                    link(V.tensor_scalar(small[:, 114:116], small[:, 114:116], lam[:, 4:5], None, ALU.mult))
                    if h >= 1:
                        dv.wait_ge(sem("b_PT"), h)
                    for qb in range(2):
                        a = act[:, h % 2, 2304 + qb * 256:2304 + (qb + 1) * 256]
                        b = act[:, h % 2, 2816 + qb * 256:2816 + (qb + 1) * 256]
                        link(V.tensor_scalar(a, a, small[:, 112 + qb:113 + qb], None, ALU.mult))
                        r = V.scalar_tensor_tensor(out=hbuf[:, 0, qb * 256:(qb + 1) * 256], in0=b,
                                                   scalar=small[:, 114 + qb:115 + qb], in1=a, op0=ALU.mult, op1=ALU.add)
                        if qb == 0:
                            link(r)
                        else:
                            r.then_inc(sem("b_p"), 1)
                if s >= 2:
                    h = s - 2
                    dv.wait_ge(sem("ob_rs"), h + 1)
                    for t in range(NT):
                        V.tensor_scalar(xn[:, t, h * P:(h + 1) * P], bank[6 + h % 2][:, t * P:(t + 1) * P],
                                        rs[:, 2 * h + t:2 * h + t + 1], None, ALU.mult).then_inc(sem("ob_c"), 1)
            for h in range(NB2):
                dv.wait_ge(sem("ob_h"), bank_end(h, NB2))
                V.scalar_tensor_tensor(out=xtl[:, 4 + h, :], in0=bank[4 + h // 2][:, (h % 2) * 256:(h % 2 + 1) * 256],
                                       scalar=lam[:, 5:6], in1=f32(xth[:, 4 + h, :]), op0=ALU.mult, op1=ALU.subtract)\
                 .then_inc(sem("ob_l"), 1)
            residual(U_OUT2, "out2_r")

            norm("mlp2")
            ffn("ff", U_FF2, FF2 // FM, 3, 2, FM, 4, 0, done=DONE_MOE, finish=lambda: add_sums("x_final"))


def weight_stream(w):
    units = np.zeros((U_END + 2, P, UNIT), np.float32)

    def pairs(u, m):
        k, n = m.shape
        v = m.reshape(k // 256, 2, P, n // WIDE, WIDE).transpose(3, 0, 2, 1, 4)
        units[u:u + k // 256 * (n // WIDE)] = v.reshape(-1, P, UNIT)

    def narrow(u, m):
        k, n = m.shape
        units[u:u + k // 512, :, 0:4 * n] = m.reshape(k // 512, 4, P, n).transpose(0, 2, 1, 3).reshape(k // 512, P, 4 * n)

    def gate_up_down(u, wg, wu, wd):
        nf = wg.shape[1] // FG
        g = np.stack([wg.reshape(4, 2, P, nf, FG), wu.reshape(4, 2, P, nf, FG)], 4)
        g = g.transpose(3, 0, 2, 1, 4, 5).reshape(nf, 4, P, UNIT)
        d = wd.reshape(nf, 2, P, D)
        interleave(u, g, d)

    def interleave(u, g, d):
        nf, ug, ud = g.shape[0], g.shape[1], d.shape[1]
        units[u:u + ug] = g[0]
        u += ug
        for f in range(1, nf):
            units[u:u + ug] = g[f]
            units[u + ug:u + ug + ud] = d[f - 1]
            u += ug + ud
        units[u:u + ud] = d[nf - 1]

    pairs(U_IN, w["conv_w_in"][0].reshape(D, 6, WIDE)[:, CONV_CHUNKS, :].reshape(D, 6 * WIDE))
    pairs(U_OUT, w["conv_w_out"][0])
    gate_up_down(U_FF1, w["ffn_w_gate"][0], w["ffn_w_up"][0], w["ffn_w_down"][0])
    pairs(U_DOWN, w["mla_w_down"][0][:, :WIDE])
    narrow(U_DOWN + 4, w["mla_w_down"][0][:, WIDE:])
    for n in range(3):
        m = w["mla_w_uq"][0][:, n * WIDE:(n + 1) * WIDE]
        pairs(U_UQ + 2 * n, m[0:256])
        units[U_UQ + 2 * n + 1, :, 0:WIDE] = m[256:384]
    pairs(U_UKV, w["mla_w_ukv"][0])
    pairs(U_WO, w["mla_w_o"][0])
    for e in range(NE):
        gate_up_down(U_MOE + 48 * e, w["moe_w_gate"][0, e], w["moe_w_up"][0, e], w["moe_w_down"][0, e])
    pairs(U_IN2, w["w_in_2"][0][:, :2048])
    narrow(U_IN2 + 16, w["w_in_2"][0][:, 2048:])
    pairs(U_OUT2, w["w_out_2"][0])
    up = w["w_up_2"][0].reshape(4, 2, P, 8, FM).transpose(3, 0, 2, 1, 4).reshape(8, 4, P, UNIT)
    interleave(U_FF2, up, w["w_down_2"][0].reshape(8, 4, P, D))
    return units.reshape(-1, 2, P, UNIT).transpose(0, 2, 1, 3).reshape(-1, P, 2 * UNIT)


def shape_tables():
    f = np.zeros((P, NFIXED), np.float32)
    f[:, 0:P] = np.eye(P)
    causal = np.where(np.arange(P)[None, :] <= np.arange(P)[:, None], 0.0, -3.0e38)
    f[:, FIXED["mask"]:FIXED["mask"] + P] = causal
    f[:, FIXED["mask"] + 2 * P:FIXED["mask"] + 3 * P] = causal
    inv = 1.0 / (np.float32(10000.0) ** (np.arange(0, 32, 2, dtype=np.float32) / np.float32(32)))
    tok = np.arange(TOK)
    ar = (tok // 64).astype(np.float32)[:, None] * inv[None, :].astype(np.float32)
    ac = (tok % 64).astype(np.float32)[:, None] * inv[None, :].astype(np.float32)
    ct = np.concatenate([np.cos(ar), np.cos(ar), np.cos(ac), np.cos(ac)], 1)
    st = np.concatenate([-np.sin(ar), np.sin(ar), -np.sin(ac), np.sin(ac)], 1)
    f[:, FIXED["ctab"]:FIXED["ctab"] + 128] = ct.reshape(2, P, 64).transpose(1, 0, 2).reshape(P, 128)
    f[:, FIXED["stab"]:FIXED["stab"] + 128] = st.reshape(2, P, 64).transpose(1, 0, 2).reshape(P, 128)
    f[:, FIXED["freq"]:FIXED["freq"] + 32] = np.float32(10000.0) ** (-np.arange(0, 64, 2, dtype=np.float32) / np.float32(64))
    f[:, FIXED["iota"]:FIXED["iota"] + 8] = np.arange(8)
    f[:, FIXED["before"]:FIXED["before"] + P] = np.arange(P)[:, None] < np.arange(P)[None, :]
    f[:, FIXED["slots"]:FIXED["slots"] + P] = np.where(np.arange(P) < CAP, np.arange(P), -1000)
    f[:, FIXED["every"]:FIXED["every"] + P] = np.arange(P)
    r = np.arange(-255, 257)
    n = np.abs(r)
    far = 8 + (np.log(np.maximum(n, 1).astype(np.float32) / np.float32(8)) / np.float32(np.log(16.0)) * np.float32(8)).astype(np.int32)
    bucket = (r > 0) * 16 + np.where(n < 8, n, np.minimum(far, 15))
    onehot = (np.arange(BUCKETS)[:, None] == bucket[None, :]).astype(np.float32)
    return f, onehot


def kernel(**inputs):
    import concourse.bacc as _bacc
    from concourse.bass_utils import run_bass_kernel_spmd as _run

    w = {k: np.asarray(v) for k, v in inputs.items()}

    def column(v):
        return v.reshape(-1, P).T

    two = lambda v: np.concatenate([v, v]).reshape(P, 1)
    cols = np.concatenate([
        column(w["norm_mix"][0]), column(w["norm_ffn"][0]), column(w["norm_mix"][1]), column(w["norm_ffn"][1]),
        column(w["attn_norm_g_2"][0]), column(w["mlp_norm_g_2"][0]), column(w["mla_q_a_norm"][0]),
        column(w["mla_kv_a_norm"][0]), column(w["mla_q_norm"][0][:NOPE]), column(w["mla_k_norm"][0][:NOPE]),
        column(w["conv_w"][0]), two(w["b_q_norm_g_2"][0]), two(w["b_k_norm_g_2"][0]), column(w["b_subln_g_2"][0]),
        w["moe_router"][0].reshape(KD, P, NE).transpose(1, 0, 2).reshape(P, KD * NE)], 1)
    rows = np.concatenate([
        w["mla_q_norm"][0][NOPE:], w["mla_k_norm"][0][NOPE:], w["a_q_norm_g_2"][0], w["a_k_norm_g_2"][0],
        w["lambda_q1_2"][0], w["lambda_k1_2"][0], w["lambda_q2_2"][0], w["lambda_k2_2"][0]]).reshape(1, NROWS)
    fixed, onehot = shape_tables()
    arrays = {
        "x_dram": w["x"][0], "pos_dram": w["positions"].reshape(NT, P).T, "weights_dram": weight_stream(w),
        "cols_dram": cols, "rows_dram": rows, "fixed_dram": fixed, "onehot_dram": onehot, "relb_dram": w["rel_bias_2"],
    }
    arrays = {k: np.ascontiguousarray(v) for k, v in arrays.items()}
    nc = _bacc.Bacc("TRN2", target_bir_lowering=False, num_devices=1)
    args = [nc.dram_tensor(k, v.shape, mybir.dt.from_np(v.dtype), kind="ExternalInput").ap() for k, v in arrays.items()]
    out = nc.dram_tensor("out_dram", (TOK, D), F32, kind="ExternalOutput").ap()
    build(nc, *args, out)
    r = _run(nc, [arrays], core_ids=[0])
    return r.results[0]["out_dram"].reshape(1, TOK, D)
```
